# Optimizing a Trainium2 kernel written in Bass

```python
import math
import jax, jax.numpy as jnp
from jax import lax
import numpy as np

D_MODEL = 1024
BATCH = 1
SEQ = 512
DEPTH = 1

MEM_LEN = 256
A_HEADS = 4
A_QK_DIM = 64
A_V_DIM = 2 * A_QK_DIM
B_HEADS = 4
B_HEAD_DIM = 64
DILATED_PATTERNS = ((128, 1), (512, 4), (2048, 16))
DILATED_BLK = 128
C_HEADS = 4
C_HEAD_DIM = 64
IDX_HEADS = 8
IDX_DIM = 64
TOPK_MAX = 256
IN_SPLITS = (
    A_HEADS * 2 * A_QK_DIM,
    A_HEADS * 2 * A_QK_DIM,
    A_HEADS * A_V_DIM,
    B_HEADS * B_HEAD_DIM,
    B_HEADS * B_HEAD_DIM,
    B_HEADS * B_HEAD_DIM,
    C_HEADS * C_HEAD_DIM,
    C_HEADS * C_HEAD_DIM,
    C_HEADS * C_HEAD_DIM,
    IDX_HEADS * IDX_DIM,
    IDX_DIM,
    IDX_HEADS,
)
N_IN = 3656
MIX_WIDTH = A_HEADS * A_V_DIM + B_HEADS * B_HEAD_DIM + C_HEADS * C_HEAD_DIM
REL_BUCKETS = 32
REL_MAX_DIST = 2048
N_BIAS_HEADS = A_HEADS + B_HEADS + C_HEADS
MEM_HEADS = 4
MEM_HEAD_DIM = D_MODEL // MEM_HEADS
D_FF = 2816
CONV_WIDTH = 3

Q_BLK = 128
EPS = 1e-6
NEG = -1e30


def rmsnorm(x, g):
    x32 = x.astype(jnp.float32)
    y = x32 * lax.rsqrt(jnp.mean(x32 * x32, axis=-1, keepdims=True) + EPS)
    return (y * g.astype(jnp.float32)).astype(x.dtype)

def rel_bucket(dist):
    n = jnp.maximum(dist, 0)
    max_exact = REL_BUCKETS // 2
    nf = jnp.maximum(n, 1).astype(jnp.float32)
    large = max_exact + (jnp.log(nf / max_exact) / math.log(REL_MAX_DIST / max_exact)
                         * (REL_BUCKETS - max_exact)).astype(jnp.int32)
    large = jnp.minimum(large, REL_BUCKETS - 1)
    return jnp.where(n < max_exact, n, large)

def diff_attention(q, k, v, lam, lam_init, subln_g, table):
    Bn, S, H, _, d = q.shape
    nb = S // Q_BLK
    scale = d ** -0.5
    kpos = jnp.arange(S, dtype=jnp.int32)
    v32 = v.astype(jnp.float32)

    def block(args):
        qb, start = args
        qpos = start + jnp.arange(Q_BLK, dtype=jnp.int32)
        s = jnp.einsum('bqhmd,bkhmd->bhmqk', qb, k).astype(jnp.float32) * scale
        dist = qpos[:, None] - kpos[None, :]
        bias = jnp.transpose(table[rel_bucket(dist)].astype(jnp.float32), (2, 0, 1))
        s = jnp.where(dist >= 0, s + bias[None, :, None], NEG)
        p = jax.nn.softmax(s, axis=-1)
        attn = p[:, :, 0] - lam * p[:, :, 1]
        return jnp.einsum('bhqk,bkhd->bqhd', attn, v32)

    qb = jnp.moveaxis(q.reshape(Bn, nb, Q_BLK, H, 2, d), 1, 0)
    starts = jnp.arange(nb, dtype=jnp.int32) * Q_BLK
    o = lax.map(block, (qb, starts))
    o = jnp.moveaxis(o, 0, 1).reshape(Bn, S, H, v.shape[-1])
    return rmsnorm(o, subln_g) * (1.0 - lam_init)

def dilated_branch(q, k, v, window, r, table, scale):
    Bn, S, H, d = q.shape
    n_back = window // r
    unit = r * DILATED_BLK
    S_pad = -(-S // unit) * unit
    nb = S_pad // unit
    pad = ((0, 0), (0, S_pad - S), (0, 0), (0, 0))
    qb = jnp.pad(q, pad).reshape(Bn, nb, DILATED_BLK, r, H, d)
    kb = jnp.pad(k, pad).reshape(Bn, nb, DILATED_BLK, r, H, d)
    vb = jnp.pad(v, pad).reshape(Bn, nb, DILATED_BLK, r, H, d)

    def with_prev(t):
        prev = jnp.pad(t, ((0, 0), (1, 0), (0, 0), (0, 0), (0, 0), (0, 0)))[:, :nb]
        return jnp.concatenate([prev, t], axis=2)

    kk = with_prev(kb)
    vv = with_prev(vb).astype(jnp.float32)
    s = jnp.einsum('bnqchd,bnkchd->bnchqk', qb, kk).astype(jnp.float32) * scale
    qi = jnp.arange(DILATED_BLK, dtype=jnp.int32)[:, None]
    ki = jnp.arange(2 * DILATED_BLK, dtype=jnp.int32)[None, :]
    dist_m = qi + DILATED_BLK - ki
    m_q = jnp.arange(nb, dtype=jnp.int32)[:, None, None] * DILATED_BLK + qi[None]
    mask = (dist_m >= 0) & (dist_m <= n_back) & (m_q - dist_m >= 0)
    bias = jnp.transpose(table[rel_bucket(dist_m * r)].astype(jnp.float32), (2, 0, 1))
    s = jnp.where(mask[None, :, None, None], s + bias, NEG)
    lse = jax.nn.logsumexp(s, axis=-1)
    p = jnp.exp(s - lse[..., None])
    o = jnp.einsum('bnchqk,bnkchd->bnqchd', p, vv).reshape(Bn, S_pad, H, d)[:, :S]
    lse = jnp.transpose(lse, (0, 1, 4, 2, 3)).reshape(Bn, S_pad, H)[:, :S]
    return o, lse

def dilated_attention(q, k, v, table):
    scale = q.shape[-1] ** -0.5
    outs, lses = [], []
    for window, r in DILATED_PATTERNS:
        o, lse = dilated_branch(q, k, v, window, r, table, scale)
        outs.append(o)
        lses.append(lse)
    wts = jax.nn.softmax(jnp.stack(lses, 0), axis=0)
    return jnp.einsum('pbsh,pbshd->bshd', wts, jnp.stack(outs, 0))

def dsa_attention(q, k, v, iq, ik, iw, table):
    Bn, S, H, d = q.shape
    nb = S // Q_BLK
    topk = min(TOPK_MAX, S // 4)
    scale = d ** -0.5
    kpos = jnp.arange(S, dtype=jnp.int32)
    iw = iw.astype(jnp.float32) * (IDX_HEADS ** -0.5)

    def block(args):
        qb, iqb, iwb, start = args
        qpos = start + jnp.arange(Q_BLK, dtype=jnp.int32)
        logits = jnp.einsum('bqhd,bkd->bqhk', iqb, ik).astype(jnp.float32) * (IDX_DIM ** -0.5)
        score = jnp.einsum('bqhk,bqh->bqk', jax.nn.relu(logits), iwb)
        score = jnp.where(kpos[None, None, :] <= qpos[None, :, None], score, NEG)
        _, idx = lax.top_k(score, topk)
        valid = idx <= qpos[None, :, None]
        flat = idx.reshape(Bn, Q_BLK * topk)
        ks = jax.vmap(lambda kb, ib: kb[ib])(k, flat).reshape(Bn, Q_BLK, topk, H, d)
        vs = jax.vmap(lambda vb, ib: vb[ib])(v, flat).reshape(Bn, Q_BLK, topk, H, d)
        s = jnp.einsum('bqhd,bqkhd->bhqk', qb, ks).astype(jnp.float32) * scale
        bias = jnp.transpose(table[rel_bucket(qpos[None, :, None] - idx)].astype(jnp.float32), (0, 3, 1, 2))
        s = jnp.where(valid[:, None], s + bias, NEG)
        p = jax.nn.softmax(s, axis=-1)
        return jnp.einsum('bhqk,bqkhd->bqhd', p, vs.astype(jnp.float32))

    qb = jnp.moveaxis(q.reshape(Bn, nb, Q_BLK, H, d), 1, 0)
    iqb = jnp.moveaxis(iq.reshape(Bn, nb, Q_BLK, IDX_HEADS, IDX_DIM), 1, 0)
    iwb = jnp.moveaxis(iw.reshape(Bn, nb, Q_BLK, IDX_HEADS), 1, 0)
    starts = jnp.arange(nb, dtype=jnp.int32) * Q_BLK
    o = lax.map(block, (qb, iqb, iwb, starts))
    return jnp.moveaxis(o, 0, 1).reshape(Bn, S, H, d)

def hybrid_mixer(h, w_in, lam_q1, lam_k1, lam_q2, lam_k2, subln_g, w_out, rel_bias, layer_idx):
    Bn, S, _ = h.shape
    proj = h @ w_in
    (aq, ak, av, bq, bk, bv, cq, ck, cv, iq, ik, iw) = jnp.split(
        proj, np.cumsum(IN_SPLITS)[:-1].tolist(), axis=-1)
    lam_init = 0.8 - 0.6 * math.exp(-0.3 * layer_idx)
    lam = (jnp.exp(jnp.sum(lam_q1.astype(jnp.float32) * lam_k1.astype(jnp.float32)))
           - jnp.exp(jnp.sum(lam_q2.astype(jnp.float32) * lam_k2.astype(jnp.float32))) + lam_init)
    o_a = diff_attention(aq.reshape(Bn, S, A_HEADS, 2, A_QK_DIM), ak.reshape(Bn, S, A_HEADS, 2, A_QK_DIM),
                         av.reshape(Bn, S, A_HEADS, A_V_DIM), lam, lam_init, subln_g,
                         rel_bias[:, :A_HEADS])
    o_b = dilated_attention(bq.reshape(Bn, S, B_HEADS, B_HEAD_DIM), bk.reshape(Bn, S, B_HEADS, B_HEAD_DIM),
                            bv.reshape(Bn, S, B_HEADS, B_HEAD_DIM),
                            rel_bias[:, A_HEADS:A_HEADS + B_HEADS])
    o_c = dsa_attention(cq.reshape(Bn, S, C_HEADS, C_HEAD_DIM), ck.reshape(Bn, S, C_HEADS, C_HEAD_DIM),
                        cv.reshape(Bn, S, C_HEADS, C_HEAD_DIM), iq.reshape(Bn, S, IDX_HEADS, IDX_DIM),
                        ik, iw, rel_bias[:, A_HEADS + B_HEADS:])
    o = jnp.concatenate([o_a.reshape(Bn, S, -1), o_b.reshape(Bn, S, -1), o_c.reshape(Bn, S, -1)],
                        axis=-1).astype(h.dtype)
    return o @ w_out

def memory_attention(h, mem_n, w_mq, w_mkv, w_mo):
    Bn, S, D = h.shape
    q = (h @ w_mq).reshape(Bn, S, MEM_HEADS, MEM_HEAD_DIM)
    k, v = jnp.split(mem_n @ w_mkv, 2, axis=-1)
    k = k.reshape(Bn, -1, MEM_HEADS, MEM_HEAD_DIM)
    v = v.reshape(Bn, -1, MEM_HEADS, MEM_HEAD_DIM)
    s = jnp.einsum('bqhd,bkhd->bhqk', q, k).astype(jnp.float32) * (MEM_HEAD_DIM ** -0.5)
    p = jax.nn.softmax(s, axis=-1)
    o = jnp.einsum('bhqk,bkhd->bqhd', p, v.astype(jnp.float32)).astype(h.dtype).reshape(Bn, S, D)
    return o @ w_mo

def conv_ffn(h, w_up, conv_w, conv_b, w_down):
    S = h.shape[1]
    u = h @ w_up
    u_p = jnp.pad(u, ((0, 0), (CONV_WIDTH - 1, 0), (0, 0)))
    c = conv_b
    for j in range(CONV_WIDTH):
        c = c + conv_w[j] * u_p[:, j:j + S]
    gate, val = jnp.split(c, 2, axis=-1)
    return (jax.nn.silu(gate) * val) @ w_down

def first_inputs(seed: int = 0) -> dict:
    key = jax.random.key(seed)
    ks = jax.random.split(key, 24)

    def nrm(k, shape, scale):
        return jax.random.normal(k, shape, jnp.float32) * scale

    L, D, F = DEPTH, D_MODEL, D_FF
    return {
        "x": nrm(ks[0], (BATCH, SEQ, D), 1.0),
        "mem": nrm(ks[1], (BATCH, MEM_LEN, D), 1.0),
        "rel_bias": nrm(ks[2], (REL_BUCKETS, N_BIAS_HEADS), 0.2),
        "norm_mix": 1.0 + nrm(ks[3], (L, D), 0.1),
        "w_in": nrm(ks[4], (L, D, N_IN), D ** -0.5),
        "lam_q1": nrm(ks[5], (L, A_QK_DIM), 0.1),
        "lam_k1": nrm(ks[6], (L, A_QK_DIM), 0.1),
        "lam_q2": nrm(ks[7], (L, A_QK_DIM), 0.1),
        "lam_k2": nrm(ks[8], (L, A_QK_DIM), 0.1),
        "subln": 1.0 + nrm(ks[9], (L, A_V_DIM), 0.1),
        "w_out": nrm(ks[10], (L, MIX_WIDTH, D), MIX_WIDTH ** -0.5),
        "norm_mem": 1.0 + nrm(ks[11], (L, D), 0.1),
        "norm_memkv": 1.0 + nrm(ks[12], (L, D), 0.1),
        "w_mq": nrm(ks[13], (L, D, D), D ** -0.5),
        "w_mkv": nrm(ks[14], (L, D, 2 * D), D ** -0.5),
        "w_mo": nrm(ks[15], (L, D, D), D ** -0.5),
        "norm_ffn": 1.0 + nrm(ks[16], (L, D), 0.1),
        "w_up": nrm(ks[17], (L, D, 2 * F), D ** -0.5),
        "conv_w": nrm(ks[18], (L, CONV_WIDTH, 2 * F), CONV_WIDTH ** -0.5),
        "conv_b": nrm(ks[19], (L, 2 * F), 0.02),
        "w_down": nrm(ks[20], (L, F, D), F ** -0.5),
        "norm_final": 1.0 + nrm(ks[21], (D,), 0.1),
    }

def first_block(x, mem, rel_bias, norm_mix, w_in, lam_q1, lam_k1, lam_q2, lam_k2, subln, w_out,
              norm_mem, norm_memkv, w_mq, w_mkv, w_mo, norm_ffn, w_up, conv_w, conv_b, w_down,
              norm_final):
    for l in range(DEPTH):
        h = rmsnorm(x, norm_mix[l])
        x = x + hybrid_mixer(h, w_in[l], lam_q1[l], lam_k1[l], lam_q2[l], lam_k2[l], subln[l],
                             w_out[l], rel_bias, l)
        h = rmsnorm(x, norm_mem[l])
        x = x + memory_attention(h, rmsnorm(mem, norm_memkv[l]), w_mq[l], w_mkv[l], w_mo[l])
        h = rmsnorm(x, norm_ffn[l])
        x = x + conv_ffn(h, w_up[l], conv_w[l], conv_b[l], w_down[l])
    return rmsnorm(x, norm_final)


DEPTH_2 = 2

RMS_EPS = 1e-6
MACARON_WEIGHT = 0.5
N_EVEN = (DEPTH_2 + 1) // 2
N_ODD = DEPTH_2 // 2

POOL_WIDTH = D_MODEL // 2
POOL_GROUPS = 4
POOL_GROUP_DIM = POOL_WIDTH // POOL_GROUPS
POOL_WINDOWS = (2, 4, 8, 16)

HYENA_WIDTH = D_MODEL // 2
HYENA_ORDER = 2
HYENA_SHORT_CONV = 3
HYENA_POS_DIM = 33
HYENA_FILTER_HIDDEN = 64
HYENA_FAST_DECAY_PCT = 0.3
HYENA_SLOW_DECAY_PCT = 1.5
HYENA_DECAY_TARGET = 1e-2

EVEN_IN_WIDTH = POOL_WIDTH + (HYENA_ORDER + 1) * HYENA_WIDTH
EVEN_OUT_WIDTH = POOL_WIDTH + HYENA_WIDTH

MLA_HEADS = 16
MLA_Q_LORA = 256
MLA_KV_LORA = 128
MLA_NOPE = 64
MLA_ROPE = 32
MLA_V = 64
ROPE_THETA = 10000.0
Q_BLOCK = 128


def rmsnorm_2(x, g):
    x32 = x.astype(jnp.float32)
    y = x32 * lax.rsqrt(jnp.mean(x32 * x32, axis=-1, keepdims=True) + RMS_EPS)
    return (y * g.astype(jnp.float32)).astype(x.dtype)

def swiglu(h, w_gate, w_up, w_down):
    return (jax.nn.silu(h @ w_gate) * (h @ w_up)) @ w_down

def centred_pool_minus_self(a):
    L = a.shape[1]
    a32 = a.astype(jnp.float32)
    csum = jnp.pad(jnp.cumsum(a32, axis=1), ((0, 0), (1, 0), (0, 0)))
    t = jnp.arange(L)
    outs = []
    for g, w in enumerate(POOL_WINDOWS):
        cg = csum[..., g * POOL_GROUP_DIM:(g + 1) * POOL_GROUP_DIM]
        lo = jnp.clip(t - w // 2, 0, L)
        hi = jnp.clip(t - w // 2 + w, 0, L)
        cnt = (hi - lo).astype(jnp.float32)[None, :, None]
        outs.append((jnp.take(cg, hi, axis=1) - jnp.take(cg, lo, axis=1)) / cnt)
    return (jnp.concatenate(outs, axis=-1) - a32).astype(a.dtype)

def pool_mixer(a, pool_w, pool_scale):
    B, L, _ = a.shape
    p = centred_pool_minus_self(a).reshape(B, L, POOL_GROUPS, POOL_GROUP_DIM)
    y = jnp.einsum('blgc,gcd->blgd', p, pool_w).reshape(B, L, POOL_WIDTH)
    return y * pool_scale

def short_conv_centred(u, w, b):
    L = u.shape[1]
    pad = HYENA_SHORT_CONV // 2
    up = jnp.pad(u, ((0, 0), (pad, HYENA_SHORT_CONV - 1 - pad), (0, 0)))
    y = b
    for k in range(HYENA_SHORT_CONV):
        y = y + up[:, k:k + L] * w[k]
    return y

def hyena_position_features(L):
    f32 = jnp.float32
    t = jnp.linspace(0.0, 1.0, L, dtype=f32)
    bands = (HYENA_POS_DIM - 1) // 2
    w = 2.0 * math.pi * jnp.arange(L, dtype=f32) / L
    f = jnp.linspace(1e-4, bands - 1, bands, dtype=f32)
    phase = w[:, None] * f[None, :]
    z = jnp.concatenate([t[:, None], jnp.cos(phase), -jnp.sin(phase)], axis=-1)
    return t, z

def hyena_filter_spectra(t, z, w1, b1, w2, b2, w3, b3, sin_freq, w_out, decay):
    f32 = jnp.float32
    L = t.shape[0]
    h = jnp.sin(sin_freq[0].astype(f32) * (z @ w1.astype(f32) + b1.astype(f32)))
    h = jnp.sin(sin_freq[1].astype(f32) * (h @ w2.astype(f32) + b2.astype(f32)))
    h = jnp.sin(sin_freq[2].astype(f32) * (h @ w3.astype(f32) + b3.astype(f32)))
    h = (h @ w_out.astype(f32)).reshape(L, HYENA_ORDER, 2, HYENA_WIDTH)
    h = h * jnp.exp(-t[:, None, None, None] * jnp.abs(decay.astype(f32)))
    fwd, bwd = h[:, :, 0], h[:, :, 1]
    two = jnp.concatenate(
        [fwd, jnp.zeros((1, HYENA_ORDER, HYENA_WIDTH), f32), bwd[:0:-1]], axis=0)
    two = two * lax.rsqrt(jnp.sum(two * two, axis=0, keepdims=True))
    return jnp.fft.rfft(two, axis=0)

def fft_long_conv(u, spec, bias):
    L = u.shape[1]
    u32 = u.astype(jnp.float32)
    y = jnp.fft.irfft(jnp.fft.rfft(u32, n=2 * L, axis=1) * spec[None], n=2 * L, axis=1)[:, :L]
    return (y + u32 * bias.astype(jnp.float32)).astype(u.dtype)

def hyena_mixer(u, conv_w, conv_b, spec, bias):
    u = short_conv_centred(u, conv_w, conv_b)
    parts = jnp.split(u, HYENA_ORDER + 1, axis=-1)
    z = parts[-1]
    for o in range(HYENA_ORDER):
        z = parts[o] * fft_long_conv(z, spec[:, o], bias[o])
    return z

def apply_rope(x, cos, sin):
    half = x.shape[-1] // 2
    x1, x2 = x[..., :half], x[..., half:]
    return jnp.concatenate([x1 * cos - x2 * sin, x1 * sin + x2 * cos], axis=-1)

def mla_mixer(h, w_dq, q_norm_g, w_uq, w_dkv, kv_norm_g, w_ukv, w_o, cos, sin):
    B, L, _ = h.shape
    cq = rmsnorm_2(h @ w_dq, q_norm_g)
    q = (cq @ w_uq).reshape(B, L, MLA_HEADS, MLA_NOPE + MLA_ROPE)
    q_nope, q_rope = q[..., :MLA_NOPE], q[..., MLA_NOPE:]
    q_rope = apply_rope(q_rope, cos[None, :, None, :], sin[None, :, None, :])
    ckv_full = h @ w_dkv
    ckv = rmsnorm_2(ckv_full[..., :MLA_KV_LORA], kv_norm_g)
    k_rope = apply_rope(ckv_full[..., MLA_KV_LORA:], cos[None], sin[None])
    kv = (ckv @ w_ukv).reshape(B, L, MLA_HEADS, MLA_NOPE + MLA_V)
    k_nope, v = kv[..., :MLA_NOPE], kv[..., MLA_NOPE:]
    scale = (MLA_NOPE + MLA_ROPE) ** -0.5
    nb = L // Q_BLOCK

    def to_blocks(a):
        return jnp.moveaxis(a.reshape(B, nb, Q_BLOCK, *a.shape[2:]), 1, 0)

    def attend(qs):
        qn, qr = qs
        s = (jnp.einsum('bqhd,bkhd->bhqk', qn, k_nope)
             + jnp.einsum('bqhr,bkr->bhqk', qr, k_rope))
        p = jax.nn.softmax(s.astype(jnp.float32) * scale, axis=-1).astype(v.dtype)
        return jnp.einsum('bhqk,bkhd->bqhd', p, v)

    o = lax.map(attend, (to_blocks(q_nope), to_blocks(q_rope)))
    o = jnp.moveaxis(o, 0, 1).reshape(B, L, MLA_HEADS * MLA_V)
    return o @ w_o

def second_inputs(seed: int = 0) -> dict:
    key = jax.random.key(seed)
    ks = iter(jax.random.split(key, 32))

    def nrm(shape, scale):
        return jax.random.normal(next(ks), shape, jnp.float32) * scale

    D, F, W, FH = D_MODEL, D_FF, HYENA_WIDTH, HYENA_FILTER_HIDDEN
    decay_base = jnp.linspace(-math.log(HYENA_DECAY_TARGET) / HYENA_SLOW_DECAY_PCT,
                              -math.log(HYENA_DECAY_TARGET) / HYENA_FAST_DECAY_PCT, W,
                              dtype=jnp.float32)
    inp = {}
    inp["x"] = nrm((BATCH, SEQ, D), 1.0)
    inp["norm_g"] = 1.0 + nrm((DEPTH_2, 3, D), 0.05)
    inp["ffn_w_gate"] = nrm((DEPTH_2, 2, D, F), D ** -0.5)
    inp["ffn_w_up"] = nrm((DEPTH_2, 2, D, F), D ** -0.5)
    inp["ffn_w_down"] = nrm((DEPTH_2, 2, F, D), F ** -0.5)
    inp["mix_w_in"] = nrm((N_EVEN, D, EVEN_IN_WIDTH), D ** -0.5)
    inp["pool_w"] = nrm((N_EVEN, POOL_GROUPS, POOL_GROUP_DIM, POOL_GROUP_DIM), POOL_GROUP_DIM ** -0.5)
    inp["pool_scale"] = 1.0 + nrm((N_EVEN, POOL_WIDTH), 0.05)
    inp["hyena_conv_w"] = nrm((N_EVEN, HYENA_SHORT_CONV, (HYENA_ORDER + 1) * W), HYENA_SHORT_CONV ** -0.5)
    inp["hyena_conv_b"] = nrm((N_EVEN, (HYENA_ORDER + 1) * W), 0.02)
    inp["hyena_ffn_w1"] = nrm((N_EVEN, HYENA_POS_DIM, FH), HYENA_POS_DIM ** -0.5)
    inp["hyena_ffn_b1"] = nrm((N_EVEN, FH), 0.02)
    inp["hyena_ffn_w2"] = nrm((N_EVEN, FH, FH), FH ** -0.5)
    inp["hyena_ffn_b2"] = nrm((N_EVEN, FH), 0.02)
    inp["hyena_ffn_w3"] = nrm((N_EVEN, FH, FH), FH ** -0.5)
    inp["hyena_ffn_b3"] = nrm((N_EVEN, FH), 0.02)
    inp["hyena_sin_freq"] = 1.0 + nrm((N_EVEN, 3, FH), 0.1)
    inp["hyena_ffn_w_out"] = nrm((N_EVEN, FH, HYENA_ORDER * 2 * W), FH ** -0.5)
    inp["hyena_decay"] = decay_base * jnp.exp(nrm((N_EVEN, HYENA_ORDER, 2, W), 0.1))
    inp["hyena_bias"] = nrm((N_EVEN, HYENA_ORDER, W), 0.5)
    inp["mix_w_out"] = nrm((N_EVEN, EVEN_OUT_WIDTH, D), EVEN_OUT_WIDTH ** -0.5)
    inp["mla_w_dq"] = nrm((N_ODD, D, MLA_Q_LORA), D ** -0.5)
    inp["mla_q_norm_g"] = 1.0 + nrm((N_ODD, MLA_Q_LORA), 0.05)
    inp["mla_w_uq"] = nrm((N_ODD, MLA_Q_LORA, MLA_HEADS * (MLA_NOPE + MLA_ROPE)), MLA_Q_LORA ** -0.5)
    inp["mla_w_dkv"] = nrm((N_ODD, D, MLA_KV_LORA + MLA_ROPE), D ** -0.5)
    inp["mla_kv_norm_g"] = 1.0 + nrm((N_ODD, MLA_KV_LORA), 0.05)
    inp["mla_w_ukv"] = nrm((N_ODD, MLA_KV_LORA, MLA_HEADS * (MLA_NOPE + MLA_V)), MLA_KV_LORA ** -0.5)
    inp["mla_w_o"] = nrm((N_ODD, MLA_HEADS * MLA_V, D), (MLA_HEADS * MLA_V) ** -0.5)
    inp["final_norm_g"] = 1.0 + nrm((D,), 0.05)
    return inp

def second_block(x, norm_g, ffn_w_gate, ffn_w_up, ffn_w_down, mix_w_in, pool_w, pool_scale,
              hyena_conv_w, hyena_conv_b, hyena_ffn_w1, hyena_ffn_b1, hyena_ffn_w2, hyena_ffn_b2,
              hyena_ffn_w3, hyena_ffn_b3, hyena_sin_freq, hyena_ffn_w_out, hyena_decay, hyena_bias,
              mix_w_out, mla_w_dq, mla_q_norm_g, mla_w_uq, mla_w_dkv, mla_kv_norm_g, mla_w_ukv,
              mla_w_o, final_norm_g):
    L = x.shape[1]
    t_pos, z_pos = hyena_position_features(L)
    inv_freq = ROPE_THETA ** (-jnp.arange(0, MLA_ROPE, 2, dtype=jnp.float32) / MLA_ROPE)
    ang = jnp.arange(L, dtype=jnp.float32)[:, None] * inv_freq[None, :]
    cos = jnp.cos(ang).astype(x.dtype)
    sin = jnp.sin(ang).astype(x.dtype)

    for i in range(DEPTH_2):
        x = x + MACARON_WEIGHT * swiglu(rmsnorm_2(x, norm_g[i, 0]),
                                        ffn_w_gate[i, 0], ffn_w_up[i, 0], ffn_w_down[i, 0])
        h = rmsnorm_2(x, norm_g[i, 1])
        j = i // 2
        if i % 2 == 0:
            proj = h @ mix_w_in[j]
            y_pool = pool_mixer(proj[..., :POOL_WIDTH], pool_w[j], pool_scale[j])
            spec = hyena_filter_spectra(t_pos, z_pos, hyena_ffn_w1[j], hyena_ffn_b1[j],
                                        hyena_ffn_w2[j], hyena_ffn_b2[j], hyena_ffn_w3[j],
                                        hyena_ffn_b3[j], hyena_sin_freq[j], hyena_ffn_w_out[j],
                                        hyena_decay[j])
            y_hyena = hyena_mixer(proj[..., POOL_WIDTH:], hyena_conv_w[j], hyena_conv_b[j],
                                  spec, hyena_bias[j])
            x = x + jnp.concatenate([y_pool, y_hyena], axis=-1) @ mix_w_out[j]
        else:
            x = x + mla_mixer(h, mla_w_dq[j], mla_q_norm_g[j], mla_w_uq[j], mla_w_dkv[j],
                              mla_kv_norm_g[j], mla_w_ukv[j], mla_w_o[j], cos, sin)
        x = x + MACARON_WEIGHT * swiglu(rmsnorm_2(x, norm_g[i, 2]),
                                        ffn_w_gate[i, 1], ffn_w_up[i, 1], ffn_w_down[i, 1])
    return rmsnorm_2(x, final_norm_g)


def setup_inputs(seed=0):
    out = dict(first_inputs(seed))
    for name, value in second_inputs(seed + 1).items():
        if name != "x":
            out[name + "_2"] = value
    return out


def reference(
    x, mem, rel_bias, norm_mix, w_in, lam_q1, lam_k1, lam_q2, lam_k2, subln, w_out, norm_mem,
    norm_memkv, w_mq, w_mkv, w_mo, norm_ffn, w_up, conv_w, conv_b, w_down, norm_final, norm_g_2,
    ffn_w_gate_2, ffn_w_up_2, ffn_w_down_2, mix_w_in_2, pool_w_2, pool_scale_2, hyena_conv_w_2,
    hyena_conv_b_2, hyena_ffn_w1_2, hyena_ffn_b1_2, hyena_ffn_w2_2, hyena_ffn_b2_2,
    hyena_ffn_w3_2, hyena_ffn_b3_2, hyena_sin_freq_2, hyena_ffn_w_out_2, hyena_decay_2,
    hyena_bias_2, mix_w_out_2, mla_w_dq_2, mla_q_norm_g_2, mla_w_uq_2, mla_w_dkv_2,
    mla_kv_norm_g_2, mla_w_ukv_2, mla_w_o_2, final_norm_g_2,
):
    x = first_block(
        x, mem, rel_bias, norm_mix, w_in, lam_q1, lam_k1, lam_q2, lam_k2, subln, w_out,
        norm_mem, norm_memkv, w_mq, w_mkv, w_mo, norm_ffn, w_up, conv_w, conv_b, w_down,
        norm_final,
    )
    return second_block(
        x, norm_g_2, ffn_w_gate_2, ffn_w_up_2, ffn_w_down_2, mix_w_in_2, pool_w_2, pool_scale_2,
        hyena_conv_w_2, hyena_conv_b_2, hyena_ffn_w1_2, hyena_ffn_b1_2, hyena_ffn_w2_2,
        hyena_ffn_b2_2, hyena_ffn_w3_2, hyena_ffn_b3_2, hyena_sin_freq_2, hyena_ffn_w_out_2,
        hyena_decay_2, hyena_bias_2, mix_w_out_2, mla_w_dq_2, mla_q_norm_g_2, mla_w_uq_2,
        mla_w_dkv_2, mla_kv_norm_g_2, mla_w_ukv_2, mla_w_o_2, final_norm_g_2,
    )


_drawn_inputs = setup_inputs


def setup_inputs(seed=0):
    import zlib

    import numpy as np

    out = dict(_drawn_inputs(seed))
    spreads = {}
    factors = {'lam_q1': 8.0,
     'norm_mem': 3.576,
     'pool_scale_2': 3.64,
     'mla_q_norm_g_2': 8.0,
     'mla_kv_norm_g_2': 8.0}
    for name, (base, spread) in spreads.items():
        noise = np.random.default_rng([zlib.crc32(name.encode()), seed]).standard_normal(out[name].shape)
        drawn = base * np.exp(spread * noise) if base else spread * noise
        out[name] = __import__('jax').numpy.asarray(drawn.astype(out[name].dtype))
    for name, factor in factors.items():
        out[name] = (out[name] * factor).astype(out[name].dtype)
    return out
```

```python
import math
from contextlib import ExitStack

import numpy as np

import concourse.bass as bass
from concourse import mybir

F32 = mybir.dt.float32
F32R = mybir.dt.float32r
ALU = mybir.AluOpType
ACT = mybir.ActivationFunctionType
AX_X = mybir.AxisListType.X

P = 128
D = 1024
DC = D // P
T = 512
QT = T // P
M = 256
FF = 2816
FC = FF // P
EPS = 1e-6
NEG = -1e30
HEADS = 4
LAM_INIT = 0.8 - 0.6 * math.exp(-0.3 * 0)
TAKEN = -3e38
TWO_PI = 2 * math.pi
TWO_PI_PARTS = (6.28125, 0.0019350051879882812, 3.0199159819567636e-07)
ROUND = 1.5 * 2.0 ** 23
SIN_MAX = 3.1415925
WIDTH = 640
MLA_HEADS = 16

STREAM = [
    ("mixer", 32), ("mixer_out", 8), ("memory_kv", 16), ("memory_q", 8), ("memory_out", 8),
    ("conv_up", 2 * FC), ("conv_down", 3 * DC),
    ("ffn0_up", 2 * FC), ("ffn0_down", 3 * DC), ("pool_hyena", 16), ("pool_hyena_out", 8),
    ("ffn1_up", 2 * FC), ("ffn1_down", 3 * DC), ("ffn2_up", 2 * FC), ("ffn2_down", 3 * DC),
    ("mla_down", 4), ("mla_heads", 8), ("mla_out", 8), ("ffn3_up", 2 * FC), ("ffn3_down", 3 * DC),
]
PACKS, PACK_BASE = 0, {}
for _name, _n in STREAM:
    PACK_BASE[_name] = PACKS
    PACKS += _n
AHEAD = 3
OUTPUTS = [
    ("mixer", 32), ("mixer_out", 8), ("memory_kv", 16), ("memory_q", 8), ("memory_out", 8),
    ("conv_up", 2 * FC), ("conv_down", 8), ("ffn0_up", 2 * FC), ("ffn0_down", 8), ("pool_hyena", 16),
    ("pool_hyena_out", 8), ("ffn1_up", 2 * FC), ("ffn1_down", 8), ("ffn2_up", 2 * FC),
    ("ffn2_down", 8), ("mla_down", 4), ("mla_out", 8), ("ffn3_up", 2 * FC), ("ffn3_down", 8),
]
OUT_BASE, _o = {}, 0
for _name, _n in OUTPUTS:
    OUT_BASE[_name] = _o
    _o += _n

COLS = {}
_c = 0
for _name, _n in [
    ("norm_mix", 8), ("norm_mem", 8), ("norm_memkv", 8), ("norm_ffn", 8), ("norm_final", 8),
    ("norm_g", 48), ("final_norm_g", 8), ("subln", 1), ("q_norm", 2), ("kv_norm", 1), ("pool_scale", 4),
    ("conv_w", 3 * 2 * FC), ("conv_b", 2 * FC), ("hyena_w", 36), ("hyena_b", 12),
    ("filter_b", 3), ("filter_freq", 3), ("neg_time", 4), ("dft_weight", 1), ("nyquist", 4),
]:
    COLS[_name] = _c
    _c += _n
N_COLS = _c
COLS_OF_SET = [COLS["norm_mix"], COLS["norm_mem"], COLS["norm_ffn"], COLS["norm_ffn"]] + \
    [COLS["norm_g"] + 8 * _n for _n in range(6)] + [COLS["final_norm_g"]]

AQ, AK, BQ, BK, CQ, CK, IQ, IK, IW, AV, BV, CV = 0, 4, 8, 10, 12, 14, 16, 20, 21, 22, 26, 28
N_MIXER = 30


def value(i, step, const):
    return const if i is None else i * step + const


FILT_STEPS = 5
SPEC_DVE = 3 + FILT_STEPS * QT + 1
PARTS_DVE = SPEC_DVE + 18 + 1
CONV_DVE = PARTS_DVE
CONV_STEPS = 2 * QT + 1
HY_LOADS = 10


class Order:

    def __init__(self, engine, sem):
        self.engine, self.sem, self.n, self.i, self.per = engine, sem, 0, None, 0

    def __call__(self, ins):
        ins.then_inc(self.sem, 1)
        self.n += 1
        self.engine.wait_ge(self.sem, value(self.i, self.per, self.n))

    def loop(self, i, per):
        self.i, self.per, self.begin = i, per, self.n

    def end(self, times):
        assert self.n - self.begin == self.per, (self.n - self.begin, self.per)
        self.n, self.i = self.begin + times * self.per, None


def build_program(nc, A, out):
    ctx = ExitStack()
    def sem(name):
        return ctx.enter_context(nc.semaphore(name))

    def region(start):
        place = {"at": start}

        def put(name, shape, dt=F32):
            n = 4
            for s in shape[1:]:
                n *= s
            n = (n + 31) // 32 * 32
            t = nc.alloc_sbuf_tensor_at(name, shape, dt, offset=place["at"])
            place["at"] += n
            return t
        return put, place

    start = (nc.sbuf_base + 63) // 64 * 64
    put, fixed = region(start)
    x = put("x", [P, DC, T])
    raw = put("raw", [P, 2, 8 * P])
    whi = put("whi", [P, 4, 8 * P], F32R)
    wlo = put("wlo", [P, 4, 8 * P], F32R)
    ident = put("ident", [P, P])
    ones = put("ones", [P, P])
    rstd = put("rstd", [P, T])
    sumsq = put("sumsq", [P, T])
    scratch_at = fixed["at"]
    scratch = put("scratch", [P, 4, T])
    squares = scratch[:, 0:2, :]
    gained = scratch[:, 2:4, :]
    cols = put("cols", [P, N_COLS])
    small = put("small", [P, 96])
    lin_at = fixed["at"]
    lin_hi = put("lin_hi", [P, DC, T], F32R)
    lin_lo = put("lin_lo", [P, DC, T], F32R)
    big_at = fixed["at"]
    end = nc.sbuf_usable_end

    def col(name, n=0, rows=P):
        return cols[0:rows, COLS[name] + n:COLS[name] + n + 1]

    eps_c, lam_c, neglam_c = small[:, 0:1], small[:, 1:2], small[:, 2:3]
    lamsum = small[:, 4:6]
    lamexp = small[:, 6:8]
    rowmax = small[:, 8:12]
    negmax = small[:, 12:16]
    expsum = small[:, 16:20]
    invsum = small[:, 20:24]
    idx_w = small[:, 24:56]
    top8 = small[:, 56:64]

    put, m1 = region(big_at)
    proj = put("proj", [P, N_MIXER, T])
    o_hi = put("o_hi", [P, DC, T], F32R)
    o_lo = put("o_lo", [P, DC, T], F32R)
    table = put("table", [P, 2, T])
    topmask = put("topmask", [P, 9 * P])
    assert m1["at"] <= end, (m1["at"], end)
    put, m1l = region(lin_at)
    probs = put("probs", [P, 2, 2, T])
    probs_t = put("probs_t", [P, 2, QT, T])
    diff_out = put("diff_out", [P, HEADS, T])
    assert m1l["at"] <= big_at
    put, m1b = region(lin_at + 8192)
    relu = put("relu", [P, 2, T])
    score = put("score", [P, T])
    work = put("work", [P, T])
    put, m1c = region(lin_at + 8192)
    diff_root = put("diff_root", [P, HEADS, T])
    diff_sq = put("diff_sq", [P, HEADS, T])
    assert m1c["at"] <= lin_at + 24576
    put, m1d = region(big_at + 61440)
    onehot = put("onehot", [32, WIDTH])
    relb = put("relb", [32, 12])
    biasrow = put("biasrow", [12, WIDTH])
    maskrow = put("maskrow", [12, WIDTH])
    lamrows = put("lamrows", [P, 4, 64])
    lamprod = put("lamprod", [P, 2, 64])
    diagmask = put("diagmask", [P, P])

    put, m2 = region(big_at)
    mem = put("mem", [P, DC, M])
    mem_hi = put("mem_hi", [P, DC, M], F32R)
    mem_lo = put("mem_lo", [P, DC, M], F32R)
    mem_sq = nc.alloc_sbuf_tensor_at("mem_sq", [P, DC, M], F32, offset=m2["at"])
    memv_f = put("memv_f", [P, DC, M])
    mem_k = put("mem_k", [P, DC, M])
    mem_v = put("mem_v", [P, 2, D])
    mem_q = put("mem_q", [P, DC, T])
    rstd_mem = put("rstd_mem", [P, M])
    o2_hi = put("o2_hi", [P, DC, T], F32R)
    o2_lo = put("o2_lo", [P, DC, T], F32R)
    assert m2["at"] <= end, (m2["at"], end)
    put, m2l = region(lin_at)
    mprobs = put("mprobs", [P, 2, 1, M])
    mprobs_t = put("mprobs_t", [P, 2, 2, T])

    put, m3 = region(big_at)
    act_hi = put("act_hi", [P, FC, T], F32R)
    act_lo = put("act_lo", [P, FC, T], F32R)
    m3f = m3["at"]
    gate = put("gate", [P, 2, T])
    up = put("up", [P, 2, T])
    hidden = put("hidden", [P, 2, T])
    assert m3["at"] <= end, (m3["at"], end)
    put, m3c = region(m3f)
    padded = put("padded", [P, 2, 2 + T])
    conved = put("conved", [P, 4, T])
    assert m3c["at"] <= end, (m3c["at"], end)

    put, m4 = region(big_at)
    dcos = put("dcos", [P, QT, T])
    dsin = put("dsin", [P, QT, T])
    fsum_at = m4["at"]
    fsum = put("fsum", [P, QT, 2, T])
    fdiff = put("fdiff", [P, QT, 2, T])
    spec_at = m4["at"]
    spec_r = put("spec_r", [P, QT, 2, T])
    spec_s = put("spec_s", [P, QT, 2, T])
    spec_n = put("spec_n", [1, 2, T])
    inv_at = m4["at"]
    inv_norm = put("inv_norm", [P, 2, T])
    bias_b = put("bias_b", [P, 2, T])
    nyrow = put("nyrow", [1, T])
    yn_at = m4["at"]
    y_n = put("y_n", [1, T])
    poolw = put("poolw", [P, 4, P])
    hid = put("hid", [64, T])
    fw = put("fw", [64, 3, 64])
    window_at = m4["at"]
    window = put("window", [P, 2, T + 2])
    o4 = nc.alloc_sbuf_tensor_at("o4", [P, 2, T], F32, offset=window_at)
    pool_count = nc.alloc_sbuf_tensor_at("pool_count", [P, 4, T], F32, offset=inv_at)
    put, m4p = region(scratch_at)
    pool_in = put("pool_in", [P, 16 + T + 16])
    pool_a = put("pool_a", [P, 16 + T + 16])
    pool_b = put("pool_b", [P, 16 + T + 16])
    assert m4p["at"] <= scratch_at + 8192
    zpos = nc.alloc_sbuf_tensor_at("zpos", [33, T], F32, offset=yn_at)
    assert m4["at"] <= end, (m4["at"], end)
    put, m4s = region(spec_at)
    absdecay = put("absdecay", [P, 4 * T])
    decayed = put("decayed", [P, 4 * T])
    filt = put("filt", [P, 4 * T])
    filt_sq = put("filt_sq", [P, 4 * T])
    assert m4s["at"] <= spec_at + 32768
    hy_wout = nc.alloc_sbuf_tensor_at("hy_wout", [64, 4 * T], F32, offset=inv_at)
    put, m4f = region(fsum_at)
    gate0_f = put("gate0_f", [P, 4, T])
    gate1_f = put("gate1_f", [P, 4, T])
    z_f = put("z_f", [P, 4, T])
    pooled = put("pooled", [P, 4, T])
    parts = (gate0_f, gate1_f, z_f)
    put, m4l = region(lin_at)
    gate0_t = put("gate0_t", [P, QT, T])
    z_t = put("z_t", [P, QT, T])
    y_r = put("y_r", [P, QT, T])
    y_s = put("y_s", [P, QT, T])
    assert m4l["at"] <= big_at
    put, m4o = region(spec_at)
    o4_hi = put("o4_hi", [P, DC, T], F32R)
    o4_lo = put("o4_lo", [P, DC, T], F32R)

    put, m5 = region(big_at)
    cq = put("cq", [P, 3, T])
    cq_hi = put("cq_hi", [P, 3, T], F32R)
    cq_lo = put("cq_lo", [P, 3, T], F32R)
    cq_root = put("cq_root", [P, 2, T])
    rope = put("rope", [P, T])
    roped = put("roped", [P, T])
    head_q = put("head_q", [P, 4, T])
    head_k = put("head_k", [P, 4, T])
    pair_v = put("pair_v", [P, 2, QT, P])
    o5_hi = put("o5_hi", [P, DC, T], F32R)
    o5_lo = put("o5_lo", [P, DC, T], F32R)
    assert m5["at"] <= end, (m5["at"], end)
    put, m5l = region(lin_at)
    lprobs = put("lprobs", [P, 2, 1, T])
    lprobs_t = put("lprobs_t", [P, 2, QT, T])

    ps = ctx.enter_context(nc.psum_tensor("ps", [P, 8, T], F32))
    STAT = 7

    bias_scratch = nc.dram_tensor("bias_scratch", (12, P, WIDTH), F32, kind="Internal").ap()

    raw_arrived = [sem("raw_even_arrived"), sem("raw_odd_arrived")]
    high_split = sem("high_split")
    low_split = sem("low_split")
    packs_used = sem("packs_used")
    outs_done = sem("outs_done")
    x_arrived = [sem("x_low_arrived"), sem("x_high_arrived")]
    consts_arrived = sem("consts_arrived")
    gain_applied = sem("gain_applied")
    chunk_high = sem("chunk_high")
    chunk_ready = sem("chunk_ready")
    squares_ready = sem("squares_ready")
    squares_summed = sem("squares_summed")
    stats_ready = sem("stats_ready")
    root_ready = sem("root_ready")
    renormed = sem("renormed")
    out_high = sem("out_high")
    out_ready = sem("out_ready")
    dve_order = sem("dve_order")
    act_order = sem("act_order")
    stored = sem("stored")

    gate_ready = sem("gate_ready")
    hidden_ready = sem("hidden_ready")
    hidden_high = sem("hidden_high")
    hidden_low = sem("hidden_low")
    conv_begun = sem("conv_begun")
    conv_gate = sem("conv_gate")
    bias_ready = sem("bias_ready")
    biasrow_ready = sem("biasrow_ready")
    bias_stored = sem("bias_stored")
    table_arrived = [sem("table_even_arrived"), sem("table_odd_arrived")]
    v_turned = sem("v_turned")
    v_stored = sem("v_stored")
    iw_turned = sem("iw_turned")
    idx_logits = sem("idx_logits")
    idx_relu = sem("idx_relu")
    idx_added = sem("idx_added")
    idx_selected = sem("idx_selected")
    lam_dot = sem("lam_dot")
    lam_exp = sem("lam_exp")
    mixer_consts = sem("mixer_consts")
    diff_squares = sem("diff_squares")
    diff_sums = sem("diff_sums")
    diff_rooted = sem("diff_rooted")
    diff_scaled = sem("diff_scaled")
    diff_high = sem("diff_high")
    diff_done = sem("diff_done")
    mem_arrived = sem("mem_arrived")
    mem_squares = sem("mem_squares")
    mem_sums = sem("mem_sums")
    mem_rooted = sem("mem_rooted")
    mem_gained = sem("mem_gained")
    mem_high = sem("mem_high")
    mem_ready = sem("mem_ready")
    memv_turned = sem("memv_turned")
    memv_stored = sem("memv_stored")
    hy_arrived = sem("hy_arrived")
    hy_pe = sem("hy_pe")
    hy_dve = sem("hy_dve")
    hy_act = sem("hy_act")
    conv_mid = sem("conv_mid")
    mixed_ready = sem("mixed_ready")
    lat_arrived = sem("lat_arrived")
    lat_squares = sem("lat_squares")
    lat_sums = sem("lat_sums")
    lat_rooted = sem("lat_rooted")
    lat_normed = sem("lat_normed")
    lat_high = sem("lat_high")
    lat_ready = sem("lat_ready")
    rope_ready = sem("rope_ready")
    up_ready = sem("up_ready")
    up_stored = sem("up_stored")
    up_roped = sem("up_roped")

    class Attend:

        def __init__(self, name, base_o):
            s = lambda what: sem(f"{name}_{what}")
            self.scores_ready = s("scores_ready")
            self.scores_read = s("scores_read")
            self.max_ready = s("max_ready")
            self.exp_ready = s("exp_ready")
            self.probs_ready = s("probs_ready")
            self.turned = s("turned")
            self.turned_stored = s("turned_stored")
            self.head_done = s("head_done")
            self.head_stored = s("head_stored")
            self.base_o = base_o

    att1 = Attend("mixer", 0)
    att2 = Attend("memory", 0)
    att3 = Attend("latent", 0)

    block = ctx.enter_context(nc.Block())

    LIN = (lin_hi, lin_lo)

    @block.sync
    def _(sp):
        for half in range(2):
            sp.dma_start(x[:, 4 * half:4 * half + 4, :], A["x_t"][:, 4 * half:4 * half + 4, :]).then_inc(x_arrived[half], 16)

        def load(n, i):
            m = value(i, 4, n)
            if i is not None or n >= 2:
                sp.wait_ge(low_split, value(i, 4, n - 1))
            sp.dma_start(raw[:, n % 2, :], A["packs"][bass.ds(m, 1), :, :].rearrange("a p f -> p (a f)")
                         if i is not None else A["packs"][n]).then_inc(raw_arrived[n % 2], 16)

        for n in range(4):
            load(n, None)
        with sp.Fori(0, PACKS // 4 - 1) as i:
            for n in range(4, 8):
                load(n, i)
        for n in range(PACKS, PACKS + AHEAD):
            load(n, None)
        sp.wait_ge(stored, 16 * DC)

    @block.gpsimd
    def _(pool):
        def split_low(n, i):
            pool.wait_ge(high_split, value(i, 4, n + 1))
            pool.tensor_tensor(wlo[:, n % 4, :], raw[:, n % 2, :], whi[:, n % 4, :].bitcast(F32),
                               ALU.subtract).then_inc(low_split, 1)

        with pool.Fori(0, PACKS // 4) as i:
            for n in range(4):
                split_low(n, i)
        for n in range(PACKS, PACKS + AHEAD):
            split_low(n, None)

    @block.tensor
    def _(pe):
        def wait_bank(phase, i, step, j):
            n = OUT_BASE[phase] + j - 3
            if i is not None or n > 0:
                pe.wait_ge(outs_done, value(i, step, n))

        def pack(phase, i, per_body, j, target, rhs, chunk0=0, chunks=8, total=8, ready=None):
            hi, lo = rhs
            m = PACK_BASE[phase] + j
            pe.wait_ge(low_split, value(i, per_body, m + 1))
            for b in range(chunks):
                k = chunk0 + b
                if ready is not None:
                    pe.wait_ge(ready[0], ready[1] + k + 1)
                wh = whi[:, j % 4, b * P:(b + 1) * P]
                wl = wlo[:, j % 4, b * P:(b + 1) * P]
                pe.matmul(target, wh, hi[:, k, :], start=(k == 0), stop=False)
                pe.matmul(target, wh, lo[:, k, :], start=False, stop=False)
                mm = pe.matmul(target, wl, hi[:, k, :], start=False, stop=(k == total - 1))
            mm.then_inc(packs_used, 1)

        def stats(s):
            pe.wait_ge(squares_summed, 8 * (s + 1))
            if s:
                pe.wait_ge(root_ready, s)
            pe.matmul(ps[:, STAT, :], ones[:, :], sumsq[:, :], start=True, stop=True).then_inc(stats_ready, 1)

        def project(phase, outputs, rhs, ready, s=None, n=T):
            for j in range(4):
                wait_bank(phase, None, 4, j)
                pack(phase, None, 4, j, ps[:, j, 0:n], rhs, ready=ready if j == 0 else None)
                if j == 0 and s is not None:
                    stats(s)
            if outputs > 4:
                with pe.Fori(1, outputs // 4) as i:
                    for j in range(4):
                        wait_bank(phase, i, 4, j)
                        pack(phase, i, 4, j, ps[:, j, 0:n], rhs)

        def project_out(phase, rhs, ready, packs_each=1, total=8):
            with pe.Fori(0, 2) as i:
                for j in range(4):
                    wait_bank(phase, i, 4, j)
                    for c in range(packs_each):
                        pack(phase, i, 4 * packs_each, packs_each * j + c, ps[:, j, :], rhs, chunk0=8 * c,
                             chunks=min(8, total - 8 * c), total=total, ready=ready if j == 0 else None)

        def attend(A_, units, scores, turn_blocks, product, extra=None):
            for s in range(units + 3):
                if s < units:
                    scores(s)
                if 0 <= s - 2 < units:
                    u = s - 2
                    pe.wait_ge(A_.probs_ready, u + 1)
                    if u >= 2:
                        pe.wait_ge(A_.turned_stored, u - 1)
                    source, blocks = turn_blocks(u)
                    for b in range(blocks):
                        mm = pe.transpose(ps[:, 4 + u % 2, b * P:(b + 1) * P], source[:, b * P:(b + 1) * P], ident[:, :])
                    mm.then_inc(A_.turned, 1)
                if extra:
                    extra(s)
                if s >= 3 and (s - 3) % 4 == 3:
                    product((s - 3) // 4)

        pe.wait_ge(consts_arrived, 32)
        pe.wait_ge(mixer_consts, 16 * 5)
        pe.wait_ge(dve_order, 1)
        project("mixer", 28, LIN, (chunk_ready, 0), s=0)
        for j in range(28, 30):
            wait_bank("mixer", None, 4, j)
            pack("mixer", None, 4, j, ps[:, j % 4, :], LIN)
        for j in range(30, 32):
            pe.wait_ge(low_split, j + 1)
            pe.wait_ge(packs_used, j)
            pe.sem_inc(packs_used, 1)
        pe.wait_ge(outs_done, 32)
        pe.matmul(ps[0:12, 2, :], relb[:, :], onehot[:, 0:512], start=True, stop=True)
        pe.matmul(ps[0:12, 3, 0:WIDTH - 512], relb[:, :], onehot[:, 512:WIDTH], start=True, stop=True).then_inc(bias_ready, 1)
        for v in range(8):
            if v >= 2:
                pe.wait_ge(v_stored, v - 1)
            for t in range(QT):
                mm = pe.transpose(ps[:, v % 2, t * P:(t + 1) * P], proj[:, AV + v, t * P:(t + 1) * P], ident[:, :])
            mm.then_inc(v_turned, 1)
        for t in range(QT):
            mm = pe.transpose(ps[:, 6, t * 8:(t + 1) * 8], proj[0:8, IW, t * P:(t + 1) * P], ident[0:8, 0:8])
        mm.then_inc(iw_turned, 1)
        n = 0
        for qt in range(1, QT):
            for h in range(8):
                r = 64 * (h % 2)
                if n >= 2:
                    pe.wait_ge(idx_relu, n - 1)
                pe.matmul(ps[:, 4 + n % 2, 0:(qt + 1) * P], proj[r:r + 64, IQ + h // 2, qt * P:(qt + 1) * P],
                          proj[r:r + 64, IK, 0:(qt + 1) * P], start=True, stop=True).then_inc(idx_logits, 1)
                n += 1

        def mixer_scores(u):
            hd, qt = u // 4, u % 4
            nk = (qt + 1) * P
            if u == 0:
                pe.wait_ge(v_stored, 8)
                pe.wait_ge(biasrow_ready, 1)
                pe.wait_ge(idx_added, 24)
            if u >= 2:
                pe.wait_ge(att1.scores_read, u - 1)
            if hd < 4:
                maps = [(AQ + hd, AK + hd, 0), (AQ + hd, AK + hd, 64)]
            else:
                h = hd % 4
                q0, k0 = (BQ, BK) if hd < 8 else (CQ, CK)
                maps = [(q0 + h // 2, k0 + h // 2, 64 * (h % 2))]
            for m, (q, k, r) in enumerate(maps):
                mm = pe.matmul(ps[:, 2 * (u % 2) + m, 0:nk], proj[r:r + 64, q, qt * P:(qt + 1) * P],
                               proj[r:r + 64, k, 0:nk], start=True, stop=True)
            mm.then_inc(att1.scores_ready, 1)

        def mixer_product(hd):
            pe.wait_ge(att1.turned_stored, 4 * (hd + 1))
            if hd:
                pe.wait_ge(att1.head_stored, hd)
            for j in range(QT):
                if hd < 4:
                    v, target = proj[:, AV + hd, j * P:(j + 1) * P], ps[:, 6, j * P:T]
                else:
                    h = hd % 4
                    tile = (BV if hd < 8 else CV) + h // 2
                    r = 64 * (h % 2)
                    v, target = proj[:, tile, j * P + r:j * P + r + 64], ps[r:r + 64, 6, j * P:T]
                mm = pe.matmul(target, v, probs_t[:, hd % 2, j, j * P:T], start=(j == 0), stop=(j == QT - 1))
            mm.then_inc(att1.head_done, 1)

        attend(att1, 48, mixer_scores, lambda u: (probs[:, u % 2, 0, :], u % 4 + 1), mixer_product)
        for h in range(HEADS):
            pe.wait_ge(diff_squares, h + 1)
            pe.wait_ge(att1.scores_read, 48)
            pe.matmul(ps[:, h, :], ones[:, :], diff_sq[:, h, :], start=True, stop=True).then_inc(diff_sums, 1)
        pe.wait_ge(att1.head_stored, 12)
        pe.wait_ge(diff_done, HEADS)
        project_out("mixer_out", (o_hi, o_lo), None)

        pe.wait_ge(mem_squares, 1)
        pe.wait_ge(root_ready, 1)
        for k in range(DC):
            mm = pe.matmul(ps[:, STAT, 0:M], ones[:, :], mem_sq[:, k, :], start=(k == 0), stop=(k == DC - 1))
        mm.then_inc(mem_sums, 1)
        pe.wait_ge(mem_ready, 1)
        project("memory_kv", 16, (mem_hi, mem_lo), None, n=M)
        pe.wait_ge(mem_rooted, 1)
        project("memory_q", 8, LIN, (chunk_ready, 8), s=1)
        for g in range(4):
            if g >= 2:
                pe.wait_ge(memv_stored, g - 1)
            for c in range(2):
                for t in range(2):
                    mm = pe.transpose(ps[:, 4 + g % 2, t * M + c * P:t * M + (c + 1) * P],
                                      memv_f[:, 2 * g + c, t * P:(t + 1) * P], ident[:, :])
            mm.then_inc(memv_turned, 1)
        pe.wait_ge(outs_done, OUT_BASE["memory_out"])
        pe.wait_ge(memv_stored, 4)

        def memory_scores(u):
            h, qt = u // 4, u % 4
            if u >= 2:
                pe.wait_ge(att2.exp_ready, u - 1)
            for c in range(2):
                mm = pe.matmul(ps[:, u % 2, 0:M], mem_q[:, 2 * h + c, qt * P:(qt + 1) * P], mem_k[:, 2 * h + c, :],
                               start=(c == 0), stop=(c == 1))
            mm.then_inc(att2.scores_ready, 1)

        def memory_product(h):
            pe.wait_ge(att2.turned_stored, 4 * (h + 1))
            for c in range(2):
                if h:
                    pe.wait_ge(out_ready, 2 * h - 1 + c)
                for j in range(2):
                    mm = pe.matmul(ps[:, 2 + c, :], mem_v[:, j, (2 * h + c) * P:(2 * h + c + 1) * P],
                                   mprobs_t[:, h % 2, j, :], start=(j == 0), stop=(j == 1))
                mm.then_inc(att2.head_done, 1)

        attend(att2, 16, memory_scores, lambda u: (mprobs[:, u % 2, 0, :], 2), memory_product)
        project_out("memory_out", (o2_hi, o2_lo), (out_ready, 0))

        def feed_forward(name, s, hidden_base):
            project(name + "_up", 2 * FC, LIN, (chunk_ready, 8 * s), s=s)
            project_out(name + "_down", (act_hi, act_lo), (hidden_low, hidden_base), packs_each=3, total=FC)

        feed_forward("conv", 2, 0)
        stats(3)
        feed_forward("ffn0", 4, FC)

        pe.wait_ge(hy_arrived, 16 * HY_LOADS)
        for l in range(3):
            if l:
                pe.wait_ge(hy_act, l)
            w = fw[0:33, 0, :] if l == 0 else fw[:, l, :]
            rhs = zpos[:, :] if l == 0 else hid[:, :]
            pe.matmul(ps[0:64, 4 + l % 2, :], w, rhs, start=True, stop=True).then_inc(hy_pe, 1)
        pe.wait_ge(hy_act, 3)
        for t in range(QT):
            for c in range(4):
                if t:
                    pe.wait_ge(hy_dve, 3 + FILT_STEPS * (t - 1) + c + 1)
                pe.matmul(ps[:, c, :], hid[:, t * P:(t + 1) * P], hy_wout[:, c * T:(c + 1) * T],
                          start=True, stop=True).then_inc(hy_pe, 1)
            pe.wait_ge(hy_act, 4 + 2 * (t + 1))
            for c in range(4):
                mm = pe.matmul(ps[:, 4 + c // 2, :], ones[:, :], filt_sq[:, c * T:(c + 1) * T],
                               start=(t == 0 and c % 2 == 0), stop=(t == QT - 1 and c % 2 == 1),
                               skip_group_check=True)
            mm.then_inc(hy_pe, 1)
        n = 0
        pe.wait_ge(hy_dve, 3 + FILT_STEPS * QT)
        for ft in range(QT):
            for part, (tab, src) in enumerate([(dcos, fsum), (dsin, fdiff)]):
                for o in range(2):
                    if n >= 4:
                        pe.wait_ge(hy_dve, SPEC_DVE + n - 3)
                    for t in range(QT):
                        mm = pe.matmul(ps[:, n % 4, :], tab[:, t, ft * P:(ft + 1) * P], src[:, t, o, :],
                                       start=(t == 0), stop=(t == QT - 1))
                    mm.then_inc(hy_pe, 1)
                    n += 1
        for o in range(2):
            pe.wait_ge(hy_dve, SPEC_DVE + n - 3)
            for t in range(QT):
                mm = pe.matmul(ps[0:1, n % 4, :], col("nyquist", t), fsum[:, t, o, :], start=(t == 0), stop=(t == QT - 1))
            mm.then_inc(hy_pe, 1)
            n += 1
        pe.wait_ge(hy_dve, SPEC_DVE + n)
        project("pool_hyena", 16, LIN, (chunk_ready, 40), s=5)
        n = 0
        for src in (gate0_f, z_f):
            for c in range(4):
                if n == 0:
                    pe.wait_ge(hy_dve, PARTS_DVE)
                if n >= 2:
                    pe.wait_ge(hy_act, 13 + n - 1)
                for t in range(QT):
                    mm = pe.transpose(ps[:, 4 + n % 2, t * P:(t + 1) * P], src[:, c, t * P:(t + 1) * P], ident[:, :])
                mm.then_inc(hy_pe, 1)
                n += 1
        for o in range(2):
            base = CONV_DVE + o * CONV_STEPS
            pe.wait_ge(hy_act, 13 + 8)
            pe.wait_ge(hy_dve, base)
            for ft in range(QT):
                if ft >= 2:
                    pe.wait_ge(hy_dve, base + ft - 1)
                for part, tab in enumerate((dcos, dsin)):
                    for t in range(QT):
                        mm = pe.matmul(ps[:, 2 * (ft % 2) + part, :], tab[:, t, ft * P:(ft + 1) * P], z_t[:, t, :],
                                       start=(t == 0), stop=(t == QT - 1))
                mm.then_inc(hy_pe, 1)
            for t in range(QT):
                mm = pe.matmul(ps[0:1, 6, :], col("nyquist", t), z_t[:, t, :], start=(t == 0), stop=(t == QT - 1))
            mm.then_inc(hy_pe, 1)
            pe.wait_ge(hy_dve, base + QT + 1)
            for t in range(QT):
                if t >= 2:
                    pe.wait_ge(hy_dve, base + QT + 1 + t - 1)
                cut = slice(t * P, (t + 1) * P)
                for ft in range(QT):
                    for part, (tab, y) in enumerate(((dcos, y_r), (dsin, y_s))):
                        if o == 0:
                            pe.matmul(ps[:, 4 + t % 2, :], tab[:, ft, cut], y[:, ft, :], start=(ft == 0 and part == 0), stop=False)
                        else:
                            pe.matmul(ps[:, 4 + t % 2, :], y[:, ft, cut], tab[:, ft, :], start=(ft == 0 and part == 0), stop=False)
                if o == 0:
                    mm = pe.matmul(ps[:, 4 + t % 2, :], nyrow[0:1, cut], y_n[0:1, :], start=False, stop=True)
                else:
                    mm = pe.matmul(ps[:, 4 + t % 2, :], y_n[0:1, cut], nyrow[0:1, :], start=False, stop=True)
                mm.then_inc(hy_pe, 1)
        for g in range(4):
            pe.matmul(ps[:, g, :], poolw[:, g, :], pooled[:, g, :], start=True, stop=True).then_inc(hy_pe, 1)
        pe.wait_ge(out_ready, 16)
        project_out("pool_hyena_out", (o4_hi, o4_lo), None)
        feed_forward("ffn1", 6, 2 * FC)
        feed_forward("ffn2", 7, 3 * FC)

        project("mla_down", 4, LIN, (chunk_ready, 64), s=8)
        pe.wait_ge(lat_squares, 1)
        for k in range(2):
            mm = pe.matmul(ps[:, 4, :], ones[:, :], scratch[:, k, :], start=(k == 0), stop=(k == 1))
        mm.then_inc(lat_sums, 1)
        pe.matmul(ps[:, 5, :], ones[:, :], scratch[:, 2, :], start=True, stop=True).then_inc(lat_sums, 1)
        pe.wait_ge(lat_ready, 3)
        pe.wait_ge(rope_ready, 1)
        pe.wait_ge(outs_done, OUT_BASE["mla_out"])

        def up_project(pr):
            slot = pr % 4
            pe.wait_ge(low_split, PACK_BASE["mla_heads"] + pr + 1)
            for job, blocks, chunks in [(0, [0, 1], [0, 1]), (1, [2, 3], [0, 1]), (2, [4], [2]), (3, [5], [2])]:
                n = 5 * pr + job
                if n >= 2:
                    pe.wait_ge(up_stored, n - 1)
                if job >= 2:
                    pe.wait_ge(up_roped, 2 * pr + job - 1)
                for b, k in zip(blocks, chunks):
                    wh, wl = whi[:, slot, b * P:(b + 1) * P], wlo[:, slot, b * P:(b + 1) * P]
                    first, last = b == blocks[0], b == blocks[-1]
                    pe.matmul(ps[:, 2 + n % 2, :], wh, cq_hi[:, k, :], start=first, stop=False)
                    pe.matmul(ps[:, 2 + n % 2, :], wh, cq_lo[:, k, :], start=False, stop=False)
                    mm = pe.matmul(ps[:, 2 + n % 2, :], wl, cq_hi[:, k, :], start=False, stop=last)
                mm.then_inc(up_ready, 1)
            n = 5 * pr + 4
            pe.wait_ge(up_stored, n - 1)
            wh, wl = whi[:, slot, 6 * P:7 * P], wlo[:, slot, 6 * P:7 * P]
            for t in range(QT):
                cut = slice(t * P, (t + 1) * P)
                target = ps[:, 2 + n % 2, cut]
                pe.matmul(target, cq_hi[:, 2, cut], wh, start=True, stop=False)
                pe.matmul(target, cq_lo[:, 2, cut], wh, start=False, stop=False)
                mm = pe.matmul(target, cq_hi[:, 2, cut], wl, start=False, stop=True)
            mm.then_inc(up_ready, 1)
            pe.wait_ge(up_ready, n + 1)
            pe.sem_inc(packs_used, 1)

        def latent_scores(u):
            hd, qt = u // 4, u % 4
            if u == 0:
                up_project(0)
            if u % 8 == 0:
                pe.wait_ge(up_stored, 5 * (u // 8) + 5)
                pe.wait_ge(up_roped, 2 * (u // 8) + 2)
            if u >= 2:
                pe.wait_ge(att3.exp_ready, u - 1)
            pe.matmul(ps[:, u % 2, :], head_q[0:96, hd % 4, qt * P:(qt + 1) * P], head_k[0:96, hd % 4, :],
                      start=True, stop=True).then_inc(att3.scores_ready, 1)

        def latent_extra(s):
            if s % 8 == 4 and s // 8 < 7:
                up_project(s // 8 + 1)

        def latent_product(hd):
            pe.wait_ge(att3.turned_stored, 4 * (hd + 1))
            if hd:
                pe.wait_ge(att3.head_stored, hd)
            r = 64 * (hd % 2)
            for j in range(QT):
                mm = pe.matmul(ps[r:r + 64, 6, :], pair_v[:, (hd // 2) % 2, j, r:r + 64],
                               lprobs_t[:, hd % 2, j, :], start=(j == 0), stop=(j == QT - 1))
            mm.then_inc(att3.head_done, 1)

        attend(att3, 64, latent_scores, lambda u: (lprobs[:, u % 2, 0, :], 4), latent_product,
               extra=latent_extra)
        pe.wait_ge(att3.head_stored, MLA_HEADS)
        project_out("mla_out", (o5_hi, o5_lo), None)
        feed_forward("ffn3", 9, 4 * FC)
        stats(10)

    @block.scalar
    def _(act):
        order = Order(act, act_order)

        def split_high(n, i=None, per=4):
            act.wait_ge(raw_arrived[n % 2], value(i, 8 * per, 16 * (n // 2 + 1)))
            if i is not None or n >= 4:
                act.wait_ge(packs_used, value(i, per, n - 3))
            act.activation(whi[:, n % 4, :], raw[:, n % 2, :], ACT.Copy).then_inc(high_split, 1)

        def split_only(phase, packs):
            base = PACK_BASE[phase] + AHEAD
            with act.Fori(0, packs // 4) as i:
                for j in range(4):
                    split_high(base + j, i)

        def chunk(s, d, i, ready):
            c = 8 * s + d
            row = bass.ds(value(i, 4, d), 1)
            act.wait_ge(ready[0], value(i, 4, ready[1] + d + 1))
            if i is not None or c >= 2:
                act.wait_ge(squares_summed, value(i, 4, c - 1))
            act.activation(squares[:, d % 2, :], x[:, row, :].rearrange("p a t -> p (a t)"), ACT.Square).then_inc(squares_ready, 1)
            act.wait_ge(gain_applied, value(i, 4, c + 1))
            act.activation(lin_hi[:, row, :].rearrange("p a t -> p (a t)"), gained[:, d % 2, :], ACT.Copy).then_inc(chunk_high, 1)

        def root(s):
            act.wait_ge(stats_ready, s + 1)
            act.activation(rstd[:, :], ps[:, STAT, :], ACT.Sqrt, scale=1.0 / D, bias=eps_c).then_inc(root_ready, 1)

        def project(phase, packs, s):
            base = PACK_BASE[phase] + AHEAD
            split_high(base)
            root(s)
            for j in range(1, 4):
                split_high(base + j)
            if packs > 4:
                with act.Fori(1, packs // 4) as i:
                    for j in range(4):
                        split_high(base + j, i)

        def residual(phase, s, packs_each=1):
            base = PACK_BASE[phase] + AHEAD
            with act.Fori(0, 2) as i:
                for j in range(4):
                    for c in range(packs_each):
                        split_high(base + packs_each * j + c, i, 4 * packs_each)
                    chunk(s, j, i, (outs_done, OUT_BASE[phase]))

        def feed_forward(n, name, s, conv=False):
            base, outs = PACK_BASE[name + "_up"] + AHEAD, OUT_BASE[name + "_up"]

            def up_step(i, g, first=False):
                split_high(base + 2 * g, i)
                if first:
                    root(s)
                split_high(base + 2 * g + 1, i)
                f = value(i, 2, g)
                if conv:
                    for side in range(2):
                        act.wait_ge(outs_done, value(i, 4, outs + 2 * g + 1 + side))
                        if i is not None or g >= 2:
                            act.wait_ge(hidden_low, value(i, 2, n * FC + g - 1))
                        tile = value(i, 2, g + side * FC)
                        act.activation(conved[:, 2 * g + side, :], padded[:, side, 2:2 + T], ACT.Identity,
                                       scale=cols[:, bass.ds(tile + (COLS["conv_w"] + 2 * 2 * FC), 1)],
                                       bias=cols[:, bass.ds(tile + COLS["conv_b"], 1)]).then_inc(conv_begun, 1)
                    act.wait_ge(conv_gate, value(i, 2, g + 1))
                    g_buf, h_buf = conved[:, 2 * g, :], conved[:, 2 * g + 1, :]
                else:
                    act.wait_ge(outs_done, value(i, 4, outs + 2 * g + 1))
                    g_buf, h_buf = gate[:, g, :], hidden[:, g, :]
                act.activation(g_buf, g_buf, ACT.Silu).then_inc(gate_ready, 1)
                act.wait_ge(hidden_ready, value(i, 2, n * FC + g + 1))
                act.activation(act_hi[:, bass.ds(f, 1), :].rearrange("p a t -> p (a t)"), h_buf, ACT.Copy).then_inc(hidden_high, 1)

            up_step(None, 0, first=True)
            up_step(None, 1)
            with act.Fori(1, FC // 2) as i:
                up_step(i, 0)
                up_step(i, 1)
            residual(name + "_down", s + 1, packs_each=3)

        act.dma_start(cols[:, :], A["cols"]).then_inc(consts_arrived, 16)
        act.dma_start(ident[:, :], A["ident"]).then_inc(consts_arrived, 16)
        act.dma_start(onehot[:, :], A["onehot"]).then_inc(mixer_consts, 16)
        act.dma_start(relb[:, :], A["rel_bias"]).then_inc(mixer_consts, 16)
        act.dma_start(maskrow[:, :], A["maskrow"]).then_inc(mixer_consts, 16)
        act.dma_start(diagmask[:, :], A["diagmask"]).then_inc(mixer_consts, 16)
        act.dma_start(lamrows[:, :, :], A["lam"].rearrange("(o a) b -> o a b", o=1).broadcast_to([P, 4, 64])).then_inc(mixer_consts, 16)
        for n in range(AHEAD):
            split_high(n)
        for d in range(DC):
            chunk(0, d, None, (x_arrived[d // 4], 15 - d))
        project("mixer", 32, 0)

        act.wait_ge(lam_dot, 2)
        act.activation(lamexp, lamsum, ACT.Exp).then_inc(lam_exp, 1)
        for v in range(8):
            act.wait_ge(v_turned, v + 1)
            act.activation(proj[:, AV + v, :], ps[:, v % 2, :], ACT.Copy).then_inc(v_stored, 1)
        act.wait_ge(biasrow_ready, 1)
        act.dma_start(bias_scratch, biasrow[:, :].rearrange("h (o w) -> h o w", o=1).broadcast_to([12, P, WIDTH])).then_inc(bias_stored, 16)
        n = 0
        for qt in range(1, QT):
            for h in range(8):
                act.wait_ge(idx_logits, n + 1)
                if n >= 2:
                    act.wait_ge(idx_added, n - 1)
                act.activation(relu[:, n % 2, 0:(qt + 1) * P], ps[:, 4 + n % 2, 0:(qt + 1) * P], ACT.Relu,
                               scale=0.125).then_inc(idx_relu, 1)
                n += 1
        act.wait_ge(bias_stored, 16)

        def load_table(hd):
            src = bass.AP(bias_scratch.tensor, hd * P * WIDTH + P - 1, [[WIDTH - 1, P], [1, T]])
            act.dma_start(table[:, hd % 2, :], src).then_inc(table_arrived[hd % 2], 16)

        load_table(0)
        load_table(1)

        def attend(A_, units, exps, store_to, outs, extra=None):
            for s in range(units + 4):
                if s < units:
                    exps(s)
                    if extra:
                        extra(s)
                if 0 <= s - 2 < units:
                    u = s - 2
                    act.wait_ge(A_.turned, u + 1)
                    if u // 4 >= 2:
                        act.wait_ge(A_.head_done, (u // 4 - 1) * A_.per_head)
                    target, blocks = store_to(u)
                    act.activation(target, ps[:, 4 + u % 2, 0:blocks * P].rearrange("p (b q) -> p b q", q=P),
                                   ACT.Copy).then_inc(A_.turned_stored, 1)
                if s >= 4 and (s - 4) % 4 == 3:
                    outs((s - 4) // 4)

        def mixer_exps(u):
            hd, qt = u // 4, u % 4
            b, nk = u % 2, (qt + 1) * P
            act.wait_ge(att1.max_ready, u + 1)
            for m in range(2 if hd < 4 else 1):
                act.activation(probs[:, b, m, 0:nk], probs[:, b, m, 0:nk], ACT.Exp, bias=negmax[:, 2 * b + m:2 * b + m + 1],
                               accum_out=expsum[:, 2 * b + m:2 * b + m + 1]).then_inc(att1.exp_ready, 1)
            if qt == 3 and hd + 2 < 12:
                load_table(hd + 2)

        def mixer_outs(hd):
            act.wait_ge(att1.head_done, hd + 1)
            if hd < 4:
                act.activation(diff_out[:, hd, :], ps[:, 6, :], ACT.Copy).then_inc(att1.head_stored, 1)
            else:
                r, chunk_ = 64 * (hd % 2), 4 + (hd - 4) // 2
                act.activation(o_hi[r:r + 64, chunk_, :], ps[r:r + 64, 6, :], ACT.Copy).then_inc(out_high, 1)

        att1.per_head = 1
        act.wait_ge(idx_selected, 3)
        attend(att1, 48, mixer_exps, lambda u: (probs_t[:, (u // 4) % 2, 0:u % 4 + 1, (u % 4) * P:(u % 4 + 1) * P], u % 4 + 1),
               mixer_outs)
        for h in range(HEADS):
            act.activation(diff_sq[:, h, :], diff_out[:, h, :], ACT.Square).then_inc(diff_squares, 1)
        act.wait_ge(diff_sums, HEADS)
        act.activation(diff_root[:, :, :], ps[:, 0:4, :], ACT.Sqrt, scale=1.0 / P, bias=eps_c).then_inc(diff_rooted, 1)
        for h in range(HEADS):
            act.wait_ge(diff_scaled, h + 1)
            act.activation(o_hi[:, h, :], diff_out[:, h, :], ACT.Copy).then_inc(diff_high, 1)
        act.dma_start(mem[:, :, :], A["mem_t"]).then_inc(mem_arrived, 16)
        act.wait_ge(mem_arrived, 16)
        act.activation(mem_sq[:, :, :], mem[:, :, :], ACT.Square).then_inc(mem_squares, 1)
        act.wait_ge(mem_gained, DC)
        act.activation(mem_hi[:, :, :], mem[:, :, :], ACT.Copy).then_inc(mem_high, 1)
        residual("mixer_out", 1)

        act.wait_ge(mem_sums, 1)
        act.activation(rstd_mem[:, :], ps[:, STAT, 0:M], ACT.Sqrt, scale=1.0 / D, bias=eps_c).then_inc(mem_rooted, 1)
        split_only("memory_kv", 16)
        project("memory_q", 8, 1)
        for g in range(4):
            act.wait_ge(memv_turned, g + 1)
            act.activation(mem_v[:, :, 2 * g * P:2 * (g + 1) * P], ps[:, 4 + g % 2, :].rearrange("p (t c) -> p t c", t=2),
                           ACT.Copy).then_inc(memv_stored, 1)

        def plain_exps(A_, buf, scale, n):
            def exps(u):
                act.wait_ge(A_.max_ready, u + 1)
                if u >= 2:
                    act.wait_ge(A_.turned, u - 1)
                act.activation(buf[:, u % 2, 0, :], ps[:, u % 2, 0:n], ACT.Exp, scale=scale, bias=negmax[:, u % 2:u % 2 + 1],
                               accum_out=expsum[:, u % 2:u % 2 + 1]).then_inc(A_.exp_ready, 1)
            return exps

        def memory_outs(h):
            for c in range(2):
                act.wait_ge(att2.head_done, 2 * h + c + 1)
                act.activation(o2_hi[:, 2 * h + c, :], ps[:, 2 + c, :], ACT.Copy).then_inc(out_high, 1)

        att2.per_head = 2
        attend(att2, 16, plain_exps(att2, mprobs, 1.0 / 16, M),
               lambda u: (mprobs_t[:, (u // 4) % 2, :, (u % 4) * P:(u % 4 + 1) * P], 2), memory_outs)
        residual("memory_out", 2)

        feed_forward(0, "conv", 2, conv=True)
        root(3)
        for d in range(DC):
            chunk(4, d, None, (renormed, 0))
        feed_forward(1, "ffn0", 4)

        for part, (buf, name) in enumerate([(dcos[:, :, :], "dcos"), (dsin[:, :, :], "dsin"), (zpos[:, :], "zpos"),
                                            (fw[0:33, 0, :], "fw1"), (fw[:, 1, :], "fw2"), (fw[:, 2, :], "fw3"),
                                            (hy_wout[:, :], "fw_out"), (nyrow[:, :], "nyrow"), (poolw[:, :, :], "pool_w")]):
            act.dma_start(buf, A[name]).then_inc(hy_arrived, 16)
        act.dma_start(absdecay[:, :], A["decay"].broadcast_to([P, 4 * T])).then_inc(hy_arrived, 16)
        for l in range(3):
            act.wait_ge(hy_dve, l + 1)
            act.activation(hid[:, :], scratch[0:64, 1, :], ACT.Sin).then_inc(hy_act, 1)
        act.wait_ge(hy_arrived, 16 * HY_LOADS)
        act.activation(absdecay[:, :], absdecay[:, :], ACT.Abs).then_inc(hy_act, 1)
        act.wait_ge(hy_act, 4)
        for t in range(QT):
            if t:
                act.wait_ge(hy_dve, 3 + FILT_STEPS * (t - 1) + 4)
            act.activation(decayed[:, :], absdecay[:, :], ACT.Exp, scale=col("neg_time", t)).then_inc(hy_act, 1)
            act.wait_ge(hy_dve, 3 + FILT_STEPS * t + 4)
            if t:
                act.wait_ge(hy_pe, 3 + 5 * t)
            act.activation(filt_sq[:, :], filt[:, :], ACT.Square).then_inc(hy_act, 1)
        act.wait_ge(hy_pe, 3 + 5 * QT)
        act.dma_start(bias_b[:, :, :], A["hy_bias"].rearrange("(o a) b -> o a b", o=1).broadcast_to([P, 2, T])).then_inc(hy_arrived, 16)
        act.activation(inv_norm[:, :, :], ps[:, 4:6, :], ACT.Sqrt).then_inc(hy_act, 1)
        act.wait_ge(hy_dve, SPEC_DVE + 18)
        act.dma_start(pool_count[:, :, :], A["pool_count"].rearrange("(o a) b -> o a b", o=1).broadcast_to([P, 4, T])).then_inc(hy_arrived, 16)
        base, outs = PACK_BASE["pool_hyena"] + AHEAD, OUT_BASE["pool_hyena"]
        for j in range(16):
            split_high(base + j)
            if j == 0:
                root(5)
            if j >= 4:
                n = j - 4
                act.wait_ge(outs_done, outs + j + 1)
                act.activation(parts[n // 4][:, n % 4, :], window[:, n % 2, 1:1 + T], ACT.Identity,
                               scale=col("hyena_w", 12 + n), bias=col("hyena_b", n)).then_inc(conv_mid, 1)
        n = 0
        for target in (gate0_t, z_t):
            for c in range(4):
                act.wait_ge(hy_pe, 3 + 5 * QT + 18 + n + 1)
                act.activation(target[:, :, c * P:(c + 1) * P], ps[:, 4 + n % 2, :].rearrange("p (t c) -> p t c", c=P),
                               ACT.Copy).then_inc(hy_act, 1)
                n += 1
        for k in range(DC):
            kk = (k + 4) % 8
            act.wait_ge(mixed_ready, k + 1)
            act.activation(o4_hi[:, kk, :], o4[:, k % 2, :], ACT.Copy).then_inc(out_high, 1)
        residual("pool_hyena_out", 6)
        feed_forward(2, "ffn1", 6)
        feed_forward(3, "ffn2", 7)

        act.dma_start(rope[64:P, :], A["rope"]).then_inc(lat_arrived, 16)
        project("mla_down", 4, 8)
        act.wait_ge(outs_done, OUT_BASE["mla_down"] + 3)
        act.activation(scratch[:, 0:3, :], cq[:, :, :], ACT.Square).then_inc(lat_squares, 1)
        for k in range(2):
            act.wait_ge(lat_sums, k + 1)
            act.activation(cq_root[:, k, :], ps[:, 4 + k, :], ACT.Sqrt, scale=1.0 / (256, 128)[k],
                           bias=eps_c).then_inc(lat_rooted, 1)
        for k in range(3):
            act.wait_ge(lat_normed, k + 1)
            act.activation(cq_hi[:, k, :], cq[:, k, :], ACT.Copy).then_inc(lat_high, 1)

        def up_stores(pr):
            split_high(PACK_BASE["mla_heads"] + AHEAD + pr)
            if pr >= 2:
                act.wait_ge(att3.scores_ready, 8 * (pr - 1))
                act.wait_ge(att3.head_done, 2 * (pr - 1))
            for job in range(5):
                act.wait_ge(up_ready, 5 * pr + job + 1)
                bank = 2 + (5 * pr + job) % 2
                if job < 4:
                    buf = head_q if job < 2 else head_k
                    act.activation(buf[0:64, (2 * pr + job % 2) % 4, :], ps[0:64, bank, :], ACT.Copy).then_inc(up_stored, 1)
                else:
                    act.activation(pair_v[:, pr % 2, :, :], ps[:, bank, :].rearrange("p (t c) -> p t c", c=P),
                                   ACT.Copy).then_inc(up_stored, 1)

        def latent_extra(u):
            if u % 8 == 4 and u // 8 < 7:
                up_stores(u // 8 + 1)

        def latent_outs(hd):
            r = 64 * (hd % 2)
            act.wait_ge(att3.head_done, hd + 1)
            act.activation(o5_hi[r:r + 64, hd // 2, :], ps[r:r + 64, 6, :], ACT.Copy).then_inc(out_high, 1)

        up_stores(0)
        att3.per_head = 1
        attend(att3, 64, plain_exps(att3, lprobs, 96.0 ** -0.5, T),
               lambda u: (lprobs_t[:, (u // 4) % 2, :, (u % 4) * P:(u % 4 + 1) * P], 4), latent_outs, extra=latent_extra)
        residual("mla_out", 9)
        feed_forward(4, "ffn3", 9)
        root(10)
        for d in range(DC):
            act.wait_ge(renormed, 8 + d + 1)
            act.dma_start(out[:, d, :], x[:, d, :]).then_inc(stored, 16)

    @block.vector
    def _(dve):
        order = Order(dve, dve_order)

        def chunk(s, d, i, ready):
            c = 8 * s + d
            row = bass.ds(value(i, 4, d), 1)
            dve.wait_ge(ready[0], value(i, 4, ready[1] + d + 1))
            dve.tensor_scalar(gained[:, d % 2, :], x[:, row, :].rearrange("p a t -> p (a t)"),
                              cols[:, bass.ds(value(i, 4, COLS_OF_SET[s] + d), 1)], None, ALU.mult).then_inc(gain_applied, 1)
            dve.wait_ge(chunk_high, value(i, 4, c + 1))
            dve.tensor_tensor(lin_lo[:, row, :].rearrange("p a t -> p (a t)"), gained[:, d % 2, :],
                              lin_hi[:, row, :].rearrange("p a t -> p (a t)").bitcast(F32), ALU.subtract).then_inc(chunk_ready, 1)
            dve.wait_ge(squares_ready, value(i, 4, c + 1))
            if i is not None or c >= 1:
                dve.wait_ge(squares_summed, value(i, 4, c))
            dve.tensor_tensor(sumsq[:, :], sumsq[:, :], squares[:, d % 2, :], ALU.add).then_inc(squares_summed, 1)

        def norm(s):
            dve.wait_ge(root_ready, s + 1)
            order(dve.reciprocal(rstd[:, :], rstd[:, :]))
            order(dve.memset(sumsq[:, :], 0.0))

        def residual(phase, s, packs_each=1, factor=1.0):
            base, outs = PACK_BASE[phase], OUT_BASE[phase]
            with dve.Fori(0, 2) as i:
                for j in range(4):
                    row = bass.ds(value(i, 4, j), 1)
                    dve.wait_ge(packs_used, value(i, 4 * packs_each, base + packs_each * (j + 1)))
                    xc = x[:, row, :].rearrange("p a t -> p (a t)")
                    dve.scalar_tensor_tensor(out=xc, in0=ps[:, j, :], scalar=factor, in1=xc, op0=ALU.mult,
                                             op1=ALU.add).then_inc(outs_done, 1)
                    chunk(s, j, i, (outs_done, outs))

        def feed_forward(n, name, s, conv=False, factor=0.5):
            base, outs = PACK_BASE[name + "_up"], OUT_BASE[name + "_up"]
            norm(s)

            def up_step(i, g):
                f = value(i, 2, g)
                for side in range(2):
                    dve.wait_ge(packs_used, value(i, 4, base + 2 * g + side + 1))
                    target = padded[:, side, 2:2 + T] if conv else (gate, up)[side][:, g, :]
                    dve.tensor_tensor(target, ps[:, 2 * g + side, :], rstd[:, :], ALU.mult).then_inc(outs_done, 1)
                done = value(i, 4, outs + 2 * g + 2)
                if conv:
                    dve.wait_ge(outs_done, done)
                    for side in range(2):
                        acc = conved[:, 2 * g + side, :]
                        tile = value(i, 2, g + side * FC)
                        dve.wait_ge(conv_begun, value(i, 4, 2 * g + side + 1))
                        order(dve.scalar_tensor_tensor(
                            out=acc, in0=padded[:, side, 1:1 + T], scalar=cols[:, bass.ds(tile + (COLS["conv_w"] + 2 * FC), 1)],
                            in1=acc, op0=ALU.mult, op1=ALU.add))
                        ins = dve.scalar_tensor_tensor(
                            out=acc, in0=padded[:, side, 0:T], scalar=cols[:, bass.ds(tile + COLS["conv_w"], 1)],
                            in1=acc, op0=ALU.mult, op1=ALU.add)
                        if side == 0:
                            ins.then_inc(conv_gate, 1)
                        else:
                            order(ins)
                    g_buf, u_buf, h_buf = conved[:, 2 * g, :], conved[:, 2 * g + 1, :], conved[:, 2 * g + 1, :]
                else:
                    dve.wait_ge(outs_done, done)
                    g_buf, u_buf, h_buf = gate[:, g, :], up[:, g, :], hidden[:, g, :]
                dve.wait_ge(gate_ready, value(i, 2, n * FC + g + 1))
                dve.tensor_tensor(h_buf, g_buf, u_buf, ALU.mult).then_inc(hidden_ready, 1)
                dve.wait_ge(hidden_high, value(i, 2, n * FC + g + 1))
                low = act_lo[:, bass.ds(f, 1), :].rearrange("p a t -> p (a t)")
                high = act_hi[:, bass.ds(f, 1), :].rearrange("p a t -> p (a t)").bitcast(F32)
                dve.tensor_tensor(low, h_buf, high, ALU.subtract).then_inc(hidden_low, 1)

            if conv:
                order(dve.memset(padded[:, :, 0:2], 0.0))
            with dve.Fori(0, FC // 2) as i:
                order.loop(i, 6 if conv else 0)
                up_step(i, 0)
                up_step(i, 1)
            order.end(FC // 2)
            residual(name + "_down", s + 1, packs_each=3, factor=factor)

        order(dve.memset(ones[:, :], 1.0))
        order(dve.memset(eps_c, EPS))
        order(dve.memset(sumsq[:, :], 0.0))
        dve.wait_ge(consts_arrived, 32)
        for d in range(DC):
            chunk(0, d, None, (x_arrived[d // 4], 15 - d))
        dve.wait_ge(mixer_consts, 16 * 5)
        for n in range(2):
            dve.tensor_tensor_reduce(out=lamprod[:, n, :], in0=lamrows[:, 2 * n, :], in1=lamrows[:, 2 * n + 1, :], scale=1.0,
                                     scalar=0.0, op0=ALU.mult, op1=ALU.add, accum_out=lamsum[:, n:n + 1]).then_inc(lam_dot, 1)
        norm(0)
        with dve.Fori(0, 7) as i:
            for j in range(4):
                dve.wait_ge(packs_used, value(i, 4, j + 1))
                dve.tensor_tensor(proj[:, bass.ds(value(i, 4, j), 1), :].rearrange("p a t -> p (a t)"), ps[:, j, :],
                                  rstd[:, :], ALU.mult).then_inc(outs_done, 1)
        for j in range(28, 30):
            dve.wait_ge(packs_used, j + 1)
            dve.tensor_tensor(proj[:, j, :], ps[:, j % 4, :], rstd[:, :], ALU.mult).then_inc(outs_done, 1 if j == 28 else 3)

        dve.wait_ge(lam_exp, 1)
        order(dve.tensor_tensor(lam_c, lamexp[:, 0:1], lamexp[:, 1:2], ALU.subtract))
        order(dve.tensor_scalar(neglam_c, lam_c, -1.0, -LAM_INIT, ALU.mult, ALU.add))
        order(dve.tensor_scalar(small[:, 3:4], col("subln"), 1.0 - LAM_INIT, None, ALU.mult))
        dve.wait_ge(bias_ready, 1)
        order(dve.scalar_tensor_tensor(out=biasrow[:, 0:512], in0=ps[0:12, 2, :], scalar=8.0, in1=maskrow[:, 0:512],
                                       op0=ALU.mult, op1=ALU.add))
        dve.scalar_tensor_tensor(out=biasrow[:, 512:WIDTH], in0=ps[0:12, 3, 0:WIDTH - 512], scalar=8.0,
                                 in1=maskrow[:, 512:WIDTH], op0=ALU.mult, op1=ALU.add).then_inc(biasrow_ready, 1)
        dve.wait_ge(iw_turned, 1)
        order(dve.tensor_scalar(idx_w, ps[:, 6, 0:32], 8 ** -0.5, None, ALU.mult))
        n = 0
        for qt in range(1, QT):
            nk = (qt + 1) * P
            for h in range(8):
                dve.wait_ge(idx_relu, n + 1)
                w = idx_w[:, qt * 8 + h:qt * 8 + h + 1]
                if h == 0:
                    ins = dve.tensor_scalar(score[:, 0:nk], relu[:, n % 2, 0:nk], w, None, ALU.mult)
                else:
                    dve.wait_ge(idx_added, n)
                    ins = dve.scalar_tensor_tensor(out=score[:, 0:nk], in0=relu[:, n % 2, 0:nk], scalar=w, in1=score[:, 0:nk],
                                                   op0=ALU.mult, op1=ALU.add)
                ins.then_inc(idx_added, 1)
                n += 1
            dve.wait_ge(idx_added, n)
            order(dve.tensor_tensor(score[:, qt * P:nk], score[:, qt * P:nk], diagmask[:, :], ALU.add))
            source = score
            for r in range(16):
                order(dve.max(top8, source[:, 0:nk]))
                order(dve.match_replace(out=work[:, 0:nk], in_to_replace=top8, in_values=source[:, 0:nk], imm_value=TAKEN))
                source = work
            at = (0, 0, 2 * P, 5 * P)[qt]
            dve.tensor_scalar(topmask[:, at:at + nk], work[:, 0:nk], 2.0 * NEG, 8.0 * NEG, ALU.is_ge,
                              ALU.mult).then_inc(idx_selected, 1)

        def attend(A_, units, scoring, norming, lows, extra=None):
            for s in range(units + 5):
                if s < units:
                    scoring(s)
                    if extra:
                        extra(s)
                if 0 <= s - 1 < units:
                    norming(s - 1)
                if s >= 5 and (s - 5) % 4 == 3:
                    lows((s - 5) // 4)

        def mixer_scoring(u):
            hd, qt = u // 4, u % 4
            b, nk = u % 2, (qt + 1) * P
            maps = 2 if hd < 4 else 1
            dve.wait_ge(table_arrived[hd % 2], 16 * (hd // 2 + 1))
            bias = table[:, hd % 2, T - nk:T]
            if hd >= 8 and qt:
                at = (0, 0, 2 * P, 5 * P)[qt]
                order(dve.tensor_tensor(scratch[:, 0, 0:nk], bias, topmask[:, at:at + nk], ALU.add))
                bias = scratch[:, 0, 0:nk]
            dve.wait_ge(att1.scores_ready, u + 1)
            if u >= 2:
                dve.wait_ge(att1.turned, u - 1)
            for m in range(maps):
                ins = dve.tensor_tensor_reduce(out=probs[:, b, m, 0:nk], in0=ps[:, 2 * b + m, 0:nk], in1=bias, scale=0.125,
                                               scalar=-3e38, op0=ALU.add, op1=ALU.max, accum_out=rowmax[:, 2 * b + m:2 * b + m + 1])
                if m == maps - 1:
                    ins.then_inc(att1.scores_read, 1)
                    dve.wait_ge(att1.scores_read, u + 1)
                else:
                    order(ins)
            dve.tensor_scalar(negmax[:, 2 * b:2 * b + maps], rowmax[:, 2 * b:2 * b + maps], -1.0, None,
                              ALU.mult).then_inc(att1.max_ready, 1)

        def mixer_norming(u):
            hd, qt = u // 4, u % 4
            b, nk = u % 2, (qt + 1) * P
            maps = 2 if hd < 4 else 1
            dve.wait_ge(att1.exp_ready, 2 * u + 2 if hd < 4 else 16 + u + 1)
            order(dve.reciprocal(invsum[:, 2 * b:2 * b + maps], expsum[:, 2 * b:2 * b + maps]))
            p0, p1 = probs[:, b, 0, 0:nk], probs[:, b, 1, 0:nk]
            first = dve.tensor_scalar(p0, p0, invsum[:, 2 * b:2 * b + 1], None, ALU.mult)
            if maps == 1:
                first.then_inc(att1.probs_ready, 1)
                return
            order(first)
            order(dve.tensor_tensor(invsum[:, 2 * b + 1:2 * b + 2], invsum[:, 2 * b + 1:2 * b + 2], neglam_c, ALU.mult))
            dve.scalar_tensor_tensor(out=p0, in0=p1, scalar=invsum[:, 2 * b + 1:2 * b + 2], in1=p0, op0=ALU.mult,
                                     op1=ALU.add).then_inc(att1.probs_ready, 1)

        def mixer_lows(hd):
            if hd < 4:
                return
            r, chunk_ = 64 * (hd % 2), 4 + (hd - 4) // 2
            dve.wait_ge(out_high, hd - 3)
            dve.tensor_tensor(o_lo[r:r + 64, chunk_, :], ps[r:r + 64, 6, :], o_hi[r:r + 64, chunk_, :].bitcast(F32),
                              ALU.subtract).then_inc(att1.head_stored, 1)

        attend(att1, 48, mixer_scoring, mixer_norming, mixer_lows)
        dve.wait_ge(diff_rooted, 1)
        order(dve.reciprocal(diff_root[:, :, :], diff_root[:, :, :]))
        for h in range(HEADS):
            dve.scalar_tensor_tensor(out=diff_out[:, h, :], in0=diff_out[:, h, :], scalar=small[:, 3:4], in1=diff_root[:, h, :],
                                     op0=ALU.mult, op1=ALU.mult).then_inc(diff_scaled, 1)
        for h in range(HEADS):
            dve.wait_ge(diff_high, h + 1)
            dve.tensor_tensor(o_lo[:, h, :], diff_out[:, h, :], o_hi[:, h, :].bitcast(F32), ALU.subtract).then_inc(diff_done, 1)
        dve.wait_ge(mem_squares, 1)
        for k in range(DC):
            dve.tensor_scalar(mem[:, k, :], mem[:, k, :], col("norm_memkv", k), None, ALU.mult).then_inc(mem_gained, 1)
        dve.wait_ge(mem_high, 1)
        dve.tensor_tensor(mem_lo[:, :, :], mem[:, :, :], mem_hi[:, :, :].bitcast(F32), ALU.subtract).then_inc(mem_ready, 1)
        residual("mixer_out", 1)

        dve.wait_ge(mem_rooted, 1)
        order(dve.reciprocal(rstd_mem[:, :], rstd_mem[:, :]))
        base = PACK_BASE["memory_kv"]
        for target, first in ((mem_k, 0), (memv_f, 8)):
            with dve.Fori(0, 2) as i:
                for j in range(4):
                    dve.wait_ge(packs_used, value(i, 4, base + first + j + 1))
                    dve.tensor_tensor(target[:, bass.ds(value(i, 4, j), 1), :].rearrange("p a t -> p (a t)"), ps[:, j, 0:M],
                                      rstd_mem[:, :], ALU.mult).then_inc(outs_done, 1)
        norm(1)
        base = PACK_BASE["memory_q"]
        with dve.Fori(0, 2) as i:
            for j in range(4):
                dve.wait_ge(packs_used, value(i, 4, base + j + 1))
                dve.tensor_tensor(mem_q[:, bass.ds(value(i, 4, j), 1), :].rearrange("p a t -> p (a t)"), ps[:, j, :],
                                  rstd[:, :], ALU.mult).then_inc(outs_done, 1)

        def plain_scoring(A_, scale, n):
            def scoring(u):
                dve.wait_ge(A_.scores_ready, u + 1)
                order(dve.tensor_reduce(rowmax[:, u % 2:u % 2 + 1], ps[:, u % 2, 0:n], AX_X, ALU.max))
                dve.tensor_scalar(negmax[:, u % 2:u % 2 + 1], rowmax[:, u % 2:u % 2 + 1], -scale, None,
                                  ALU.mult).then_inc(A_.max_ready, 1)
            return scoring

        def plain_norming(A_, buf):
            def norming(u):
                dve.wait_ge(A_.exp_ready, u + 1)
                order(dve.reciprocal(invsum[:, u % 2:u % 2 + 1], expsum[:, u % 2:u % 2 + 1]))
                p = buf[:, u % 2, 0, :]
                dve.tensor_scalar(p, p, invsum[:, u % 2:u % 2 + 1], None, ALU.mult).then_inc(A_.probs_ready, 1)
            return norming

        def memory_lows(h):
            for c in range(2):
                k = 2 * h + c
                dve.wait_ge(out_high, 8 + k + 1)
                dve.tensor_tensor(o2_lo[:, k, :], ps[:, 2 + c, :], o2_hi[:, k, :].bitcast(F32), ALU.subtract).then_inc(out_ready, 1)

        attend(att2, 16, plain_scoring(att2, 1.0 / 16, M), plain_norming(att2, mprobs), memory_lows)
        residual("memory_out", 2)

        feed_forward(0, "conv", 2, conv=True, factor=1.0)

        def renorm(s, gain, count):
            norm(s)
            for d in range(DC):
                dve.scalar_tensor_tensor(out=x[:, d, :], in0=x[:, d, :], scalar=col(gain, d), in1=rstd[:, :], op0=ALU.mult,
                                         op1=ALU.mult).then_inc(renormed, 1)
                if s == 3:
                    chunk(4, d, None, (renormed, 0))

        renorm(3, "norm_final", 0)
        feed_forward(1, "ffn0", 4)

        for l in range(3):
            a, r = scratch[0:64, 0, :], scratch[0:64, 1, :]
            dve.wait_ge(hy_pe, l + 1)
            order(dve.tensor_scalar(a, ps[0:64, 4 + l % 2, :], col("filter_b", l, 64), col("filter_freq", l, 64), ALU.add, ALU.mult))
            order(dve.tensor_scalar(r, a, 1.0 / TWO_PI, ROUND, ALU.mult, ALU.add))
            order(dve.tensor_scalar(r, r, -ROUND, None, ALU.add))
            order(dve.scalar_tensor_tensor(out=a, in0=r, scalar=-TWO_PI_PARTS[0], in1=a, op0=ALU.mult, op1=ALU.add))
            order(dve.scalar_tensor_tensor(out=a, in0=r, scalar=-TWO_PI_PARTS[1], in1=a, op0=ALU.mult, op1=ALU.add))
            order(dve.scalar_tensor_tensor(out=a, in0=r, scalar=-TWO_PI_PARTS[2], in1=a, op0=ALU.mult, op1=ALU.add))
            dve.tensor_scalar(r, a, SIN_MAX, -SIN_MAX, ALU.min, ALU.max).then_inc(hy_dve, 1)
        for t in range(QT):
            dve.wait_ge(hy_act, 4 + 2 * t + 1)
            if t:
                dve.wait_ge(hy_act, 4 + 2 * t)
                dve.wait_ge(hy_dve, 3 + FILT_STEPS * t)
            for c in range(4):
                cut = slice(c * T, (c + 1) * T)
                dve.wait_ge(hy_pe, 3 + 5 * t + c + 1)
                ins = dve.tensor_tensor(filt[:, cut], ps[:, c, :], decayed[:, cut], ALU.mult)
                if t == 0 and c % 2:
                    order(ins)
                    ins = dve.memset(filt[0:1, cut], 0.0)
                ins.then_inc(hy_dve, 1)
            dve.wait_ge(hy_dve, 3 + FILT_STEPS * t + 4)
            both = filt[:, :].rearrange("p (o d c) -> p o d c", o=2, d=2)
            order(dve.tensor_tensor(fsum[:, t, :, :], both[:, :, 0, :], both[:, :, 1, :], ALU.add))
            dve.tensor_tensor(fdiff[:, t, :, :], both[:, :, 0, :], both[:, :, 1, :], ALU.subtract).then_inc(hy_dve, 1)
        dve.wait_ge(hy_act, 13)
        dve.reciprocal(inv_norm[:, :, :], inv_norm[:, :, :]).then_inc(hy_dve, 1)
        dve.wait_ge(hy_dve, SPEC_DVE)
        dve.wait_ge(hy_arrived, 16 * (HY_LOADS + 1))
        n, first = 0, 3 + 5 * QT
        for ft in range(QT):
            weight = col("dft_weight") if ft == 0 else 2.0 / (2 * T)
            for part, spec in enumerate((spec_r, spec_s)):
                for o in range(2):
                    dve.wait_ge(hy_pe, first + n + 1)
                    target = spec[:, ft, o, :]
                    if part == 0:
                        order(dve.tensor_tensor(target, ps[:, n % 4, :], inv_norm[:, o, :], ALU.mult))
                        order(dve.tensor_tensor(target, target, bias_b[:, o, :], ALU.add))
                        dve.tensor_scalar(target, target, weight, None, ALU.mult).then_inc(hy_dve, 1)
                    else:
                        dve.scalar_tensor_tensor(out=target, in0=ps[:, n % 4, :], scalar=weight, in1=inv_norm[:, o, :],
                                                 op0=ALU.mult, op1=ALU.mult).then_inc(hy_dve, 1)
                    n += 1
        for o in range(2):
            dve.wait_ge(hy_pe, first + n + 1)
            order(dve.tensor_tensor(spec_n[0:1, o, :], ps[0:1, n % 4, :], inv_norm[0:1, o, :], ALU.mult))
            order(dve.tensor_tensor(spec_n[0:1, o, :], spec_n[0:1, o, :], bias_b[0:1, o, :], ALU.add))
            dve.tensor_scalar(spec_n[0:1, o, :], spec_n[0:1, o, :], 1.0 / (2 * T), None, ALU.mult).then_inc(hy_dve, 1)
            n += 1
        norm(5)
        order(dve.memset(window[:, :, :], 0.0))
        order(dve.memset(pool_in[:, :], 0.0))
        dve.wait_ge(hy_arrived, 16 * (HY_LOADS + 2))
        base = PACK_BASE["pool_hyena"]
        for g in range(4):
            dve.wait_ge(packs_used, base + g + 1)
            dve.tensor_tensor(pool_in[:, 16:16 + T], ps[:, g, :], rstd[:, :], ALU.mult).then_inc(outs_done, 1)
            dve.wait_ge(outs_done, OUT_BASE["pool_hyena"] + g + 1)
            src, width = pool_in, 16 + T + 16
            for step in range(g + 1):
                width -= 1 << step
                dst = (pool_a, pool_b)[step % 2]
                order(dve.tensor_tensor(dst[:, 0:width], src[:, 0:width], src[:, (1 << step):(1 << step) + width], ALU.add))
                src = dst
            half = 1 << g
            order(dve.tensor_tensor(pooled[:, g, :], src[:, 16 - half:16 - half + T], pool_count[:, g, :], ALU.mult))
            order(dve.tensor_tensor(pooled[:, g, :], pooled[:, g, :], pool_in[:, 16:16 + T], ALU.subtract))
        for n in range(12):
            j = 4 + n
            dve.wait_ge(packs_used, base + j + 1)
            dve.tensor_tensor(window[:, n % 2, 1:1 + T], ps[:, j % 4, :], rstd[:, :], ALU.mult).then_inc(outs_done, 1)
            dve.wait_ge(outs_done, OUT_BASE["pool_hyena"] + j + 1)
            dve.wait_ge(conv_mid, n + 1)
            acc = parts[n // 4][:, n % 4, :]
            order(dve.scalar_tensor_tensor(out=acc, in0=window[:, n % 2, 0:T], scalar=col("hyena_w", n), in1=acc,
                                           op0=ALU.mult, op1=ALU.add))
            order(dve.scalar_tensor_tensor(out=acc, in0=window[:, n % 2, 2:2 + T], scalar=col("hyena_w", 24 + n), in1=acc,
                                           op0=ALU.mult, op1=ALU.add))
        dve.sem_inc(hy_dve, 1)
        first = 3 + 5 * QT + 18 + 8
        dve.wait_ge(hy_act, 13 + 8)
        for o in range(2):
            for ft in range(QT):
                dve.wait_ge(hy_pe, first + 9 * o + ft + 1)
                zr, zs = ps[:, 2 * (ft % 2), :], ps[:, 2 * (ft % 2) + 1, :]
                t = scratch
                order(dve.tensor_tensor(t[:, 0, :], zr, spec_r[:, ft, o, :], ALU.mult))
                order(dve.tensor_tensor(t[:, 1, :], zs, spec_s[:, ft, o, :], ALU.mult))
                order(dve.tensor_tensor(t[:, 2, :], zr, spec_s[:, ft, o, :], ALU.mult))
                order(dve.tensor_tensor(t[:, 3, :], zs, spec_r[:, ft, o, :], ALU.mult))
                order(dve.tensor_tensor(y_r[:, ft, :], t[:, 0, :], t[:, 1, :], ALU.subtract))
                dve.tensor_tensor(y_s[:, ft, :], t[:, 2, :], t[:, 3, :], ALU.add).then_inc(hy_dve, 1)
                dve.wait_ge(hy_dve, CONV_DVE + CONV_STEPS * o + ft + 1)
            dve.wait_ge(hy_pe, first + 9 * o + 5)
            dve.tensor_tensor(y_n[0:1, :], ps[0:1, 6, :], spec_n[0:1, o, :], ALU.mult).then_inc(hy_dve, 1)
            for t in range(QT):
                dve.wait_ge(hy_pe, first + 9 * o + 5 + t + 1)
                if o == 0:
                    dve.tensor_tensor(z_t[:, t, :], ps[:, 4 + t % 2, :], gate0_t[:, t, :], ALU.mult).then_inc(hy_dve, 1)
                else:
                    k = t
                    if k >= 2:
                        dve.wait_ge(out_ready, 8 + k - 1)
                    dve.tensor_tensor(o4[:, k % 2, :], ps[:, 4 + t % 2, :], gate1_f[:, t, :], ALU.mult).then_inc(hy_dve, 1)
                    dve.wait_ge(hy_dve, CONV_DVE + CONV_STEPS * o + 5 + t + 1)
                    dve.sem_inc(mixed_ready, 1)
                    dve.wait_ge(out_high, 16 + k + 1)
                    dve.tensor_tensor(o4_lo[:, 4 + k, :], o4[:, k % 2, :], o4_hi[:, 4 + k, :].bitcast(F32), ALU.subtract).then_inc(out_ready, 1)
        for g in range(4):
            k = 4 + g
            dve.wait_ge(out_ready, 8 + k - 1)
            dve.wait_ge(hy_pe, first + 18 + g + 1)
            dve.tensor_scalar(o4[:, k % 2, :], ps[:, g, :], col("pool_scale", g), None, ALU.mult).then_inc(mixed_ready, 1)
            dve.wait_ge(out_high, 16 + k + 1)
            dve.tensor_tensor(o4_lo[:, g, :], o4[:, k % 2, :], o4_hi[:, g, :].bitcast(F32), ALU.subtract).then_inc(out_ready, 1)
        residual("pool_hyena_out", 6)
        feed_forward(2, "ffn1", 6)
        feed_forward(3, "ffn2", 7)

        norm(8)
        base = PACK_BASE["mla_down"]
        for j in range(3):
            dve.wait_ge(packs_used, base + j + 1)
            dve.tensor_tensor(cq[:, j, :], ps[:, j, :], rstd[:, :], ALU.mult).then_inc(outs_done, 1)
        dve.wait_ge(packs_used, base + 4)
        dve.tensor_tensor(roped[64:P, :], ps[64:P, 3, :], rstd[64:P, :], ALU.mult).then_inc(outs_done, 1)
        dve.wait_ge(outs_done, OUT_BASE["mla_down"] + 4)
        dve.wait_ge(lat_arrived, 16)
        order(dve.tensor_tensor(scratch[64:96, 3, :], roped[96:128, :], rope[96:128, :], ALU.mult))
        order(dve.tensor_tensor(roped[64:96, :], roped[64:96, :], rope[64:96, :], ALU.mult))
        for b in range(4):
            ins = dve.tensor_tensor(head_k[64:96, b, :], roped[64:96, :], scratch[64:96, 3, :], ALU.add)
            if b < 3:
                order(ins)
            else:
                ins.then_inc(rope_ready, 1)
        for k in range(2):
            dve.wait_ge(lat_rooted, k + 1)
            order(dve.reciprocal(cq_root[:, k, :], cq_root[:, k, :]))
        for k, gain in enumerate([col("q_norm", 0), col("q_norm", 1), col("kv_norm")]):
            dve.scalar_tensor_tensor(out=cq[:, k, :], in0=cq[:, k, :], scalar=gain, in1=cq_root[:, k // 2, :], op0=ALU.mult,
                                     op1=ALU.mult).then_inc(lat_normed, 1)
        for k in range(3):
            dve.wait_ge(lat_high, k + 1)
            dve.tensor_tensor(cq_lo[:, k, :], cq[:, k, :], cq_hi[:, k, :].bitcast(F32), ALU.subtract).then_inc(lat_ready, 1)

        def rotations(pr):
            if pr >= 2:
                dve.wait_ge(att3.scores_ready, 8 * (pr - 1))
            for job in range(2):
                dve.wait_ge(up_ready, 5 * pr + job + 1)
                if 2 * pr + job:
                    dve.wait_ge(up_roped, 2 * pr + job)
                bank = 2 + (5 * pr + job) % 2
                q = head_q[64:96, (2 * pr + job) % 4, :]
                order(dve.tensor_tensor(roped[64:96, :], ps[96:128, bank, :], rope[96:128, :], ALU.mult))
                order(dve.tensor_tensor(q, ps[64:96, bank, :], rope[64:96, :], ALU.mult))
                dve.tensor_tensor(q, q, roped[64:96, :], ALU.add).then_inc(up_roped, 1)

        def latent_extra(u):
            if u % 8 == 4 and u // 8 < 7:
                rotations(u // 8 + 1)

        def latent_lows(hd):
            r = 64 * (hd % 2)
            dve.wait_ge(out_high, 24 + hd + 1)
            dve.tensor_tensor(o5_lo[r:r + 64, hd // 2, :], ps[r:r + 64, 6, :], o5_hi[r:r + 64, hd // 2, :].bitcast(F32),
                              ALU.subtract).then_inc(att3.head_stored, 1)

        dve.wait_ge(rope_ready, 1)
        rotations(0)
        attend(att3, 64, plain_scoring(att3, 96.0 ** -0.5, T), plain_norming(att3, lprobs), latent_lows, extra=latent_extra)
        residual("mla_out", 9)
        feed_forward(4, "ffn3", 9)
        renorm(10, "final_norm_g", 8)

    ctx.close()


def tiles(w):
    k, n = w.shape
    return w.reshape(k // P, P, n // P, P).transpose(2, 1, 0, 3).reshape(n // P, P, k)


def down_tiles(w):
    t = tiles(w)
    pad = np.zeros((t.shape[0], P, 3 * D - t.shape[2]), w.dtype)
    return np.concatenate([t, pad], 2).reshape(-1, P, 3, D).transpose(0, 2, 1, 3).reshape(-1, P, D)


def up_tiles(gate_w, up_w):
    return np.stack([tiles(gate_w), tiles(up_w)], 1).reshape(-1, P, D)


def columns(v, rows=P):
    v = v.reshape(-1, rows).T
    return np.concatenate([v, np.zeros((P - rows, v.shape[1]), v.dtype)]) if rows < P else v


def shape_constants():
    f4 = np.float32
    c = {"ident": np.eye(P, dtype=f4)}
    dist = (T - 1 - np.arange(WIDTH)).astype(np.int64)
    near = np.maximum(dist, 0)
    large = 16 + (np.log(np.maximum(near, 1).astype(f4) / f4(16)) / f4(math.log(2048 / 16)) * f4(16)).astype(np.int32)
    bucket = np.where(near < 16, near, np.minimum(large, 31))
    c["onehot"] = (np.arange(32)[:, None] == bucket[None, :]).astype(f4)
    mask = np.zeros((12, WIDTH), f4)
    mask[:, dist < 0] = 8 * NEG
    count = (near <= 128).astype(int) + (near % 4 == 0) + (near % 16 == 0)
    logs = np.where(count > 0, 8 * np.log(np.maximum(count, 1)), 8 * NEG)
    mask[4:8] = np.where(dist < 0, 8 * NEG, logs).astype(f4)
    c["maskrow"] = mask
    c["diagmask"] = np.where(np.arange(P)[None, :] > np.arange(P)[:, None], NEG, 0.0).astype(f4)
    a = np.arange(T)
    angle = 2 * np.pi * ((a[:, None] * a[None, :]) % (2 * T)) / (2 * T)
    for name, table in (("dcos", np.cos(angle)), ("dsin", np.sin(angle))):
        c[name] = np.ascontiguousarray(table.astype(f4).reshape(QT, P, T).transpose(1, 0, 2))
    sign = np.where(a % 2 == 0, 1.0, -1.0).astype(f4)
    c["nyrow"] = sign[None, :]
    t = np.linspace(0.0, 1.0, T, dtype=f4)
    phase = (f4(2.0 * math.pi) * np.arange(T, dtype=f4) / f4(T))[:, None] * np.linspace(1e-4, 15, 16, dtype=f4)[None, :]
    c["zpos"] = np.ascontiguousarray(np.concatenate([t[:, None], np.cos(phase), -np.sin(phase)], 1).T.astype(f4))
    inv = f4(10000.0) ** (-np.arange(0, 32, 2, dtype=f4) / f4(32))
    ang = (np.arange(T, dtype=f4)[:, None] * inv[None, :]).T
    c["rope"] = np.concatenate([np.cos(ang), np.cos(ang), -np.sin(ang), np.sin(ang)]).astype(f4)
    hi = [np.minimum(a - w // 2 + w, T) - np.maximum(a - w // 2, 0) for w in (2, 4, 8, 16)]
    c["pool_count"] = (1.0 / np.stack(hi)).astype(f4)
    weight = np.full((P, 1), 2.0 / (2 * T), f4)
    weight[0] = 1.0 / (2 * T)
    c["_cols"] = {"neg_time": columns(-t), "dft_weight": weight, "nyquist": columns(sign)}
    return c


def kernel(**inputs):
    import concourse.bacc as bacc
    from concourse.bass_utils import run_bass_kernel_spmd

    w = {k: np.asarray(v) for k, v in inputs.items()}
    c = shape_constants()
    const_cols = c.pop("_cols")
    f4 = np.float32

    w_in = w["w_in"][0]
    none = np.zeros((D, P), f4)
    iq_end = 1536 + 768 + 768 + 512
    ik, iw = w_in[:, iq_end:iq_end + 64], w_in[:, iq_end + 64:]
    mixer = np.concatenate([
        w_in[:, 0:1024], w_in[:, 1536:2048], w_in[:, 2304:2816], w_in[:, 3072:iq_end], ik, ik, iw, none[:, 0:120],
        w_in[:, 1024:1536], w_in[:, 2048:2304], w_in[:, 2816:3072], none, none], 1)
    packs = [tiles(mixer), tiles(w["w_out"][0]), tiles(w["w_mkv"][0]), tiles(w["w_mq"][0]), tiles(w["w_mo"][0]),
             up_tiles(w["w_up"][0][:, :FF], w["w_up"][0][:, FF:]), down_tiles(w["w_down"][0])]

    def ffn(layer, which):
        at = (layer, which)
        return [up_tiles(w["ffn_w_gate_2"][at], w["ffn_w_up_2"][at]), down_tiles(w["ffn_w_down_2"][at])]

    packs += ffn(0, 0) + [tiles(w["mix_w_in_2"][0]), tiles(w["mix_w_out_2"][0])] + ffn(0, 1) + ffn(1, 0)
    dkv = w["mla_w_dkv_2"][0]
    rot = dkv[:, 128:160]
    packs.append(tiles(np.concatenate([w["mla_w_dq_2"][0], dkv[:, 0:128], none[:, 0:64], rot, rot[:, 16:], rot[:, :16]], 1)))
    uq = w["mla_w_uq_2"][0].reshape(2, P, MLA_HEADS, 96)
    uq = np.concatenate([uq, uq[..., 80:96], uq[..., 64:80]], 3)
    ukv = w["mla_w_ukv_2"][0].reshape(P, MLA_HEADS, P)
    uk = np.concatenate([ukv[..., 0:64], np.zeros((P, MLA_HEADS, 64), f4)], 2)
    pairs = np.concatenate([
        uq.transpose(2, 1, 0, 3).reshape(8, 2, P, 2 * P).transpose(0, 2, 1, 3).reshape(8, P, 4 * P),
        uk.reshape(P, 8, 2 * P).transpose(1, 0, 2),
        ukv[..., 64:P].reshape(P, 8, P).transpose(1, 0, 2), np.zeros((8, P, P), f4)], 2)
    packs += [pairs, tiles(w["mla_w_o_2"][0])] + ffn(1, 1) + [np.zeros((AHEAD, P, D), f4)]
    packs = np.ascontiguousarray(np.concatenate(packs))
    assert packs.shape[0] == PACKS + AHEAD, packs.shape

    vectors = {
        "norm_mix": columns(w["norm_mix"]), "norm_mem": columns(w["norm_mem"]), "norm_memkv": columns(w["norm_memkv"]),
        "norm_ffn": columns(w["norm_ffn"]), "norm_final": columns(w["norm_final"]), "norm_g": columns(w["norm_g_2"]),
        "final_norm_g": columns(w["final_norm_g_2"]), "subln": columns(w["subln"]), "q_norm": columns(w["mla_q_norm_g_2"]),
        "kv_norm": columns(w["mla_kv_norm_g_2"]), "pool_scale": columns(w["pool_scale_2"]), "conv_w": columns(w["conv_w"]),
        "conv_b": columns(w["conv_b"]), "hyena_w": columns(w["hyena_conv_w_2"]), "hyena_b": columns(w["hyena_conv_b_2"]),
        "filter_b": columns(np.concatenate([w[f"hyena_ffn_b{n}_2"] for n in (1, 2, 3)]), 64),
        "filter_freq": columns(w["hyena_sin_freq_2"], 64), **const_cols,
    }
    arrays = {
        "packs": packs,
        "cols": np.ascontiguousarray(np.concatenate([vectors[n] for n in COLS], 1)),
        "x_t": np.ascontiguousarray(w["x"][0].T.reshape(DC, P, T).transpose(1, 0, 2)),
        "mem_t": np.ascontiguousarray(w["mem"][0].T.reshape(DC, P, M).transpose(1, 0, 2)),
        "rel_bias": w["rel_bias"],
        "lam": np.concatenate([w[n] for n in ("lam_q1", "lam_k1", "lam_q2", "lam_k2")]),
        "fw1": w["hyena_ffn_w1_2"][0], "fw2": w["hyena_ffn_w2_2"][0], "fw3": w["hyena_ffn_w3_2"][0],
        "fw_out": w["hyena_ffn_w_out_2"][0],
        "pool_w": np.ascontiguousarray(w["pool_w_2"][0].transpose(1, 0, 2)),
        "decay": w["hyena_decay_2"].reshape(1, -1),
        "hy_bias": w["hyena_bias_2"][0],
        **c,
    }
    nc = bacc.Bacc("TRN2", target_bir_lowering=False, num_devices=1)
    feeds, A = {}, {}
    for name, a in arrays.items():
        feeds[f"in_{name}"] = np.ascontiguousarray(a)
        A[name] = nc.dram_tensor(f"in_{name}", a.shape, mybir.dt.from_np(a.dtype), kind="ExternalInput").ap()
    out = nc.dram_tensor("out_t", (P, DC, T), F32, kind="ExternalOutput").ap()
    build_program(nc, A, out)
    r = run_bass_kernel_spmd(nc, [feeds], core_ids=[0])
    got = r.results[0]["out_t"]
    return np.ascontiguousarray(got.transpose(1, 0, 2).reshape(D, T).T)[None]
```

```python
import math
from contextlib import ExitStack

import numpy as np

import concourse.bass as bass
from concourse import mybir

F32 = mybir.dt.float32
F32R = mybir.dt.float32r
ALU = mybir.AluOpType
ACT = mybir.ActivationFunctionType
AX_X = mybir.AxisListType.X

P = 128
D = 1024
DC = D // P
T = 512
QT = T // P
M = 256
FF = 2816
FC = FF // P
EPS = 1e-6
NEG = -1e30
HEADS = 4
LAM_INIT = 0.8 - 0.6 * math.exp(-0.3 * 0)
TAKEN = -3e38
TWO_PI = 2 * math.pi
TWO_PI_PARTS = (6.28125, 0.0019350051879882812, 3.0199159819567636e-07)
ROUND = 1.5 * 2.0 ** 23
SIN_MAX = 3.1415925
WIDTH = 640
MLA_HEADS = 16

STREAM = [
    ("mixer", 32), ("mixer_out", 8), ("memory_kv", 16), ("memory_q", 8), ("memory_out", 8),
    ("conv_up", 2 * FC), ("conv_down", 3 * DC),
    ("ffn0_up", 2 * FC), ("ffn0_down", 3 * DC), ("pool_hyena", 16), ("pool_hyena_out", 8),
    ("ffn1_up", 2 * FC), ("ffn1_down", 3 * DC), ("ffn2_up", 2 * FC), ("ffn2_down", 3 * DC),
    ("mla_down", 4), ("mla_heads", 8), ("mla_out", 8), ("ffn3_up", 2 * FC), ("ffn3_down", 3 * DC),
]
PACKS, PACK_BASE = 0, {}
for _name, _n in STREAM:
    PACK_BASE[_name] = PACKS
    PACKS += _n
AHEAD = 3
OUTPUTS = [
    ("mixer", 32), ("mixer_out", 8), ("memory_kv", 16), ("memory_q", 8), ("memory_out", 8),
    ("conv_up", 2 * FC), ("conv_down", 8), ("ffn0_up", 2 * FC), ("ffn0_down", 8), ("pool_hyena", 16),
    ("pool_hyena_out", 8), ("ffn1_up", 2 * FC), ("ffn1_down", 8), ("ffn2_up", 2 * FC),
    ("ffn2_down", 8), ("mla_down", 4), ("mla_out", 8), ("ffn3_up", 2 * FC), ("ffn3_down", 8),
]
OUT_BASE, _o = {}, 0
for _name, _n in OUTPUTS:
    OUT_BASE[_name] = _o
    _o += _n

COLS = {}
_c = 0
for _name, _n in [
    ("norm_mix", 8), ("norm_mem", 8), ("norm_memkv", 8), ("norm_ffn", 8), ("norm_final", 8),
    ("norm_g", 48), ("final_norm_g", 8), ("subln", 1), ("q_norm", 2), ("kv_norm", 1), ("pool_scale", 4),
    ("conv_w", 3 * 2 * FC), ("conv_b", 2 * FC), ("hyena_w", 36), ("hyena_b", 12),
    ("filter_b", 3), ("filter_freq", 3), ("neg_time", 4), ("dft_weight", 1), ("nyquist", 4),
]:
    COLS[_name] = _c
    _c += _n
N_COLS = _c
COLS_OF_SET = [COLS["norm_mix"], COLS["norm_mem"], COLS["norm_ffn"], N_COLS] + \
    [COLS["norm_g"] + 8 * _n for _n in range(1, 6)] + [COLS["final_norm_g"]]

AQ, AK, BQ, BK, CQ, CK, IQ, IK, IW, AV, BV, CV = 0, 4, 8, 10, 12, 14, 16, 20, 21, 22, 26, 28
N_MIXER = 30


def value(i, step, const):
    return const if i is None else i * step + const


FILT_STEPS = 5
SPEC_DVE = 3 + FILT_STEPS * QT
PARTS_DVE = SPEC_DVE + 18 + 1
CONV_DVE = PARTS_DVE
CONV_STEPS = 2 * QT + 1
HY_LOADS = 4
FILT_ACT = 4 + 8 * QT + 1


def filter_made(t, c):
    return 3 + c + 1 if t == 0 else 3 + 4 + 5 * (t - 1) + c + 1


def filter_decay(t, c):
    return 4 + c + 1 if t == 0 else 8 + 8 * (t - 1) + 2 * c + 2


def filter_squared(t, c):
    return 8 + 8 * t + (2 * c + 1 if t < QT - 1 else c + 1)


DIFF_SUMS = 32
DIFF_SCALED = DIFF_SUMS + 7
TOP_AT = (0, 0, 2 * P, 5 * P)


class Order:

    def __init__(self, engine, sem):
        self.engine, self.sem, self.n, self.i, self.per = engine, sem, 0, None, 0

    def __call__(self, ins):
        ins.then_inc(self.sem, 1)
        self.n += 1
        self.engine.wait_ge(self.sem, value(self.i, self.per, self.n))

    def loop(self, i, per):
        self.i, self.per, self.begin = i, per, self.n

    def end(self, times):
        assert self.n - self.begin == self.per, (self.n - self.begin, self.per)
        self.n, self.i = self.begin + times * self.per, None


def build_program(nc, A, out):
    ctx = ExitStack()
    def sem(name):
        return ctx.enter_context(nc.semaphore(name))

    def region(start):
        place = {"at": start}

        def put(name, shape, dt=F32):
            n = 4
            for s in shape[1:]:
                n *= s
            n = (n + 31) // 32 * 32
            t = nc.alloc_sbuf_tensor_at(name, shape, dt, offset=place["at"])
            place["at"] += n
            return t
        return put, place

    start = (nc.sbuf_base + 63) // 64 * 64
    put, fixed = region(start)
    x = put("x", [P, DC, T])
    raw = put("raw", [P, 2, 8 * P])
    whi = put("whi", [P, 4, 8 * P], F32R)
    wlo = put("wlo", [P, 4, 8 * P], F32R)
    ident = put("ident", [P, P])
    ones = put("ones", [P, P])
    rstd = put("rstd", [P, T])
    sumsq = put("sumsq", [P, T])
    scratch_at = fixed["at"]
    scratch = put("scratch", [P, 4, T])
    squares = scratch[:, 0:2, :]
    gained = scratch[:, 2:4, :]
    cols = put("cols", [P, N_COLS + DC])
    small = put("small", [P, 96])
    lin_at = fixed["at"]
    lin_hi = put("lin_hi", [P, DC, T], F32R)
    lin_lo = put("lin_lo", [P, DC, T], F32R)
    big_at = fixed["at"]
    end = nc.sbuf_usable_end

    def col(name, n=0, rows=P):
        return cols[0:rows, COLS[name] + n:COLS[name] + n + 1]

    eps2_c = small[:, 66:67]
    eps_c, lam_c, neglam_c = small[:, 0:1], small[:, 1:2], small[:, 2:3]
    lamsum = small[:, 4:6]
    lamexp = small[:, 6:8]
    negmax = small[:, 68:74]
    expsum = small[:, 74:80]
    invsum = small[:, 80:86]
    idx_w = small[:, 24:56]
    top8 = small[:, 56:64]

    put, m1 = region(big_at)
    proj = put("proj", [P, N_MIXER, T])
    o_hi = put("o_hi", [P, DC, T], F32R)
    o_lo = put("o_lo", [P, DC, T], F32R)
    table = put("table", [P, 2, T])
    topmask = put("topmask", [P, 9 * P])
    probs_late = put("probs_late", [P, 2, T])
    assert m1["at"] <= end, (m1["at"], end)
    put, m1l = region(lin_at)
    probs_early = put("probs_early", [P, 4, T])
    probs = [probs_early[:, b, :] for b in range(4)] + [probs_late[:, b, :] for b in range(2)]
    probs_t = put("probs_t", [P, 2, QT, T])
    diff_out = put("diff_out", [P, HEADS, T])
    assert m1l["at"] <= big_at
    relu = nc.alloc_sbuf_tensor_at("relu", [P, 2, T], F32, offset=lin_at + 8192)
    diff_sq = nc.alloc_sbuf_tensor_at("diff_sq", [P, HEADS, T], F32, offset=big_at + N_MIXER * T * 4)
    diff_root = nc.alloc_sbuf_tensor_at("diff_root", [P, HEADS, T], F32, offset=big_at + (N_MIXER + DC) * T * 4)
    put, m1d = region(big_at + 61440)
    onehot = put("onehot", [32, WIDTH])
    relb = put("relb", [32, 12])
    biasrow = put("biasrow", [12, WIDTH])
    maskrow = put("maskrow", [12, WIDTH])
    lamrows = put("lamrows", [P, 4, 64])
    lamprod = put("lamprod", [P, 2, 64])
    diagmask = put("diagmask", [P, P])

    put, m2 = region(big_at)
    mem = put("mem", [P, DC, M])
    mem_hi = put("mem_hi", [P, DC, M], F32R)
    mem_lo = put("mem_lo", [P, DC, M], F32R)
    mem_sq = nc.alloc_sbuf_tensor_at("mem_sq", [P, DC, M], F32, offset=m2["at"])
    memv_f = put("memv_f", [P, DC, M])
    mem_k = put("mem_k", [P, DC, M])
    mem_v = put("mem_v", [P, 2, D])
    mem_q = put("mem_q", [P, DC, T])
    rstd_mem = put("rstd_mem", [P, M])
    o2_hi = put("o2_hi", [P, DC, T], F32R)
    o2_lo = put("o2_lo", [P, DC, T], F32R)
    assert m2["at"] <= end, (m2["at"], end)
    put, m2l = region(lin_at)
    mprobs = put("mprobs", [P, 4, M])
    mprobs_t = put("mprobs_t", [P, 2, 2, T])

    put, m3 = region(big_at)
    act_hi = put("act_hi", [P, FC, T], F32R)
    act_lo = put("act_lo", [P, FC, T], F32R)
    m3f = m3["at"]
    gate = put("gate", [P, 2, T])
    up = put("up", [P, 2, T])
    hidden = put("hidden", [P, 2, T])
    assert m3["at"] <= end, (m3["at"], end)
    put, m3c = region(m3f)
    padded = put("padded", [P, 2, 2 + T])
    conved_at = m3c["at"]
    conved = put("conved", [P, 4, T])
    gained_sq = nc.alloc_sbuf_tensor_at("gained_sq", [P, T], F32, offset=conved_at)
    gained_squares = nc.alloc_sbuf_tensor_at("gained_squares", [P, 2, T], F32, offset=conved_at + 4 * T)
    tail_at = (end - 4 * (T + T + 3 * 64)) // 32 * 32
    put, mt = region(tail_at)
    hid = put("hid", [64, T])
    fw = put("fw", [64, 3, 64])
    zpos_at = mt["at"]
    zpos = put("zpos", [33, T])
    assert max(m3["at"], m3c["at"]) <= tail_at, (m3["at"], m3c["at"], tail_at)

    put, m4 = region(big_at)
    dcos = put("dcos", [P, QT, T])
    dsin = put("dsin", [P, QT, T])
    fsum_at = m4["at"]
    fsum = put("fsum", [P, QT, 2, T])
    fdiff = put("fdiff", [P, QT, 2, T])
    spec_at = m4["at"]
    spec_r = put("spec_r", [P, QT, 2, T])
    spec_s = put("spec_s", [P, QT, 2, T])
    spec_n = put("spec_n", [1, 2, T])
    inv_at = m4["at"]
    inv_norm = put("inv_norm", [P, 2, T])
    bias_b = put("bias_b", [P, 2, T])
    nyrow = put("nyrow", [1, T])
    y_n = nc.alloc_sbuf_tensor_at("y_n", [1, T], F32, offset=zpos_at)
    poolw = put("poolw", [P, 4, P])
    window_at = m4["at"]
    window = put("window", [P, 2, T + 2])
    o4 = nc.alloc_sbuf_tensor_at("o4", [P, 2, T], F32, offset=window_at)
    pool_count = nc.alloc_sbuf_tensor_at("pool_count", [P, 4, T], F32, offset=inv_at)
    put, m4p = region(scratch_at)
    pool_in = put("pool_in", [P, 16 + T + 16])
    pool_a = put("pool_a", [P, 16 + T + 16])
    pool_b = put("pool_b", [P, 16 + T + 16])
    assert m4p["at"] <= scratch_at + 8192
    assert m4["at"] <= tail_at, (m4["at"], tail_at)
    put, m4s = region(spec_at)
    absdecay = put("absdecay", [P, 4 * T])
    decayed = put("decayed", [P, 4 * T])
    filt = put("filt", [P, 4 * T])
    filt_sq = put("filt_sq", [P, 4 * T])
    assert m4s["at"] <= spec_at + 32768
    hy_wout = nc.alloc_sbuf_tensor_at("hy_wout", [64, 4 * T], F32, offset=inv_at)
    put, m4f = region(fsum_at)
    gate0_f = put("gate0_f", [P, 4, T])
    gate1_f = put("gate1_f", [P, 4, T])
    z_f = put("z_f", [P, 4, T])
    pooled = put("pooled", [P, 4, T])
    parts = (gate0_f, gate1_f, z_f)
    put, m4l = region(lin_at)
    gate0_t = put("gate0_t", [P, QT, T])
    z_t = put("z_t", [P, QT, T])
    y_r = put("y_r", [P, QT, T])
    y_s = put("y_s", [P, QT, T])
    assert m4l["at"] <= big_at
    put, m4o = region(spec_at)
    o4_hi = put("o4_hi", [P, DC, T], F32R)
    o4_lo = put("o4_lo", [P, DC, T], F32R)

    put, m5 = region(big_at)
    cq = put("cq", [P, 3, T])
    cq_hi = put("cq_hi", [P, 3, T], F32R)
    cq_lo = put("cq_lo", [P, 3, T], F32R)
    cq_root = put("cq_root", [P, 2, T])
    rope = put("rope", [P, T])
    roped = put("roped", [P, T])
    head_q = put("head_q", [P, 4, T])
    head_k = put("head_k", [P, 4, T])
    pair_v = put("pair_v", [P, 2, QT, P])
    o5_hi = put("o5_hi", [P, DC, T], F32R)
    o5_lo = put("o5_lo", [P, DC, T], F32R)
    assert m5["at"] <= end, (m5["at"], end)
    put, m5l = region(lin_at)
    lprobs = put("lprobs", [P, 4, T])
    lprobs_t = put("lprobs_t", [P, 2, QT, T])

    ps = ctx.enter_context(nc.psum_tensor("ps", [P, 8, T], F32))
    STAT = 7

    bias_scratch = nc.dram_tensor("bias_scratch", (12, P, WIDTH), F32, kind="Internal").ap()

    raw_arrived = [sem("raw_even_arrived"), sem("raw_odd_arrived")]
    high_split = sem("high_split")
    low_split = sem("low_split")
    packs_used = sem("packs_used")
    outs_done = sem("outs_done")
    x_arrived = [sem(f"x_quarter{q}_arrived") for q in range(4)]
    consts_arrived = sem("consts_arrived")
    gain_applied = sem("gain_applied")
    chunk_high = sem("chunk_high")
    chunk_ready = sem("chunk_ready")
    squares_ready = sem("squares_ready")
    squares_summed = sem("squares_summed")
    stats_ready = sem("stats_ready")
    root_ready = sem("root_ready")
    renormed = sem("renormed")
    out_high = sem("out_high")
    out_ready = sem("out_ready")
    dve_order = sem("dve_order")
    inv_ready = sem("inv_ready")
    act_order = sem("act_order")
    stored = sem("stored")

    gate_ready = sem("gate_ready")
    hidden_ready = sem("hidden_ready")
    hidden_high = sem("hidden_high")
    hidden_low = sem("hidden_low")
    conv_begun = sem("conv_begun")
    conv_gate = sem("conv_gate")
    bias_ready = sem("bias_ready")
    biasrow_ready = sem("biasrow_ready")
    bias_stored = sem("bias_stored")
    table_arrived = [sem("table_even_arrived"), sem("table_odd_arrived")]
    v_turned = sem("v_turned")
    v_stored = sem("v_stored")
    iw_turned = sem("iw_turned")
    idx_logits = sem("idx_logits")
    idx_relu = sem("idx_relu")
    idx_added = sem("idx_added")
    idx_selected = sem("idx_selected")
    lam_dot = sem("lam_dot")
    lam_exp = sem("lam_exp")
    mixer_consts = sem("mixer_consts")
    diff_squares = sem("diff_squares")
    diff_sums = sem("diff_sums")
    diff_sums_read = sem("diff_sums_read")
    diff_rooted = sem("diff_rooted")
    diff_scaled = sem("diff_scaled")
    diff_high = sem("diff_high")
    diff_done = sem("diff_done")
    mem_arrived = sem("mem_arrived")
    mem_squares = sem("mem_squares")
    mem_sums = sem("mem_sums")
    mem_rooted = sem("mem_rooted")
    mem_gained = sem("mem_gained")
    mem_high = sem("mem_high")
    mem_ready = sem("mem_ready")
    memv_turned = sem("memv_turned")
    memv_stored = sem("memv_stored")
    gained_squared = sem("gained_squared")
    both_sums = sem("both_sums")
    final_sums = sem("final_sums")
    final_rooted = sem("final_rooted")
    mlp_arrived = sem("mlp_arrived")
    wout_arrived = sem("wout_arrived")
    hy_rows_arrived = sem("hy_rows_arrived")
    hy_arrived = sem("hy_arrived")
    hy_pe = sem("hy_pe")
    hy_dve = sem("hy_dve")
    hy_act = sem("hy_act")
    conv_mid = sem("conv_mid")
    mixed_ready = sem("mixed_ready")
    lat_arrived = sem("lat_arrived")
    lat_squares = sem("lat_squares")
    lat_sums = sem("lat_sums")
    lat_rooted = sem("lat_rooted")
    lat_normed = sem("lat_normed")
    lat_high = sem("lat_high")
    lat_ready = sem("lat_ready")
    rope_ready = sem("rope_ready")
    up_ready = sem("up_ready")
    up_stored = sem("up_stored")
    up_roped = sem("up_roped")

    class Attend:

        def __init__(self, name, units, per_head, maps, banks, slots, lag):
            s = lambda what: sem(f"{name}_{what}")
            self.scores_ready = s("scores_ready")
            self.max_ready = s("max_ready")
            self.exp_ready = s("exp_ready")
            self.probs_ready = s("probs_ready")
            self.probs_scaled = s("probs_scaled")
            self.turned = s("turned")
            self.turned_stored = s("turned_stored")
            self.head_done = s("head_done")
            self.head_stored = s("head_stored")
            self.units, self.per_head, self.maps, self.lag = units, per_head, maps, lag
            self.banks, self.slots = banks, slots

        def bank_before(self, u):
            return max([0] + [v + 1 for v in range(u) if set(self.banks(v)) & set(self.banks(u))])

        def before(self, u):
            return max([0] + [v + 1 for v in range(u) if set(self.slots(v)) & set(self.slots(u))])

        def turned_at(self, s):
            return [u for u in range(self.units) if u + self.lag(u) == s]

        def heads_at(self, s, later):
            return [u // 4 for u in self.turned_at(s - later) if u % 4 == 3]

        def steps(self, later):
            return range(self.units + self.lag(self.units - 1) + later)

        def exps_before(self, u):
            return sum(self.maps(v) for v in range(u))

    att1 = Attend("mixer", 48, 1, lambda u: 2 if u < 16 else 1,
                  lambda u: [2 * (u % 2), 2 * (u % 2) + 1] if u < 16 else [u % 4],
                  lambda u: [2 * (u % 3), 2 * (u % 3) + 1] if u < 16 else [(u + 4) % 6], lambda u: 3)
    att2 = Attend("memory", 16, 2, lambda u: 1, lambda u: [(0, 1, STAT)[u % 3]], lambda u: [u % 4], lambda u: 3)
    att3 = Attend("latent", 64, 1, lambda u: 1, lambda u: [(0, 1, STAT)[u % 3]], lambda u: [u % 4], lambda u: 3)

    block = ctx.enter_context(nc.Block())

    LIN = (lin_hi, lin_lo)

    @block.sync
    def _(sp):
        def load_x(q):
            sp.dma_start(x[:, 2 * q:2 * q + 2, :], A["x_t"][:, 2 * q:2 * q + 2, :]).then_inc(x_arrived[q], 16)

        def load(n, i):
            m = value(i, 4, n)
            if i is not None or n >= 2:
                sp.wait_ge(low_split, value(i, 4, n - 1))
            sp.dma_start(raw[:, n % 2, :], A["packs"][bass.ds(m, 1), :, :].rearrange("a p f -> p (a f)")
                         if i is not None else A["packs"][n]).then_inc(raw_arrived[n % 2], 16)

        load_x(0)
        load(0, None)
        for q in range(1, 4):
            load_x(q)
        for n in range(1, 4):
            load(n, None)
        with sp.Fori(0, PACKS // 4 - 1) as i:
            for n in range(4, 8):
                load(n, i)
        for n in range(PACKS, PACKS + AHEAD):
            load(n, None)
        sp.wait_ge(stored, 16 * DC)

    @block.gpsimd
    def _(pool):
        def split_low(n, i):
            pool.wait_ge(high_split, value(i, 4, n + 1))
            pool.tensor_tensor(wlo[:, n % 4, :], raw[:, n % 2, :], whi[:, n % 4, :].bitcast(F32),
                               ALU.subtract).then_inc(low_split, 1)

        mixer_packs = PACK_BASE["mixer_out"]
        with pool.Fori(0, mixer_packs // 4) as i:
            for n in range(4):
                split_low(n, i)
        for n in range(mixer_packs, mixer_packs + AHEAD):
            split_low(n, None)

        for u in range(16, att1.units):
            b = att1.slots(u)[0]
            p0 = probs[b][:, 0:(u % 4 + 1) * P]
            pool.wait_ge(inv_ready, u + 1)
            pool.tensor_scalar(p0, p0, invsum[:, b:b + 1], None, ALU.mult).then_inc(att1.probs_scaled, 1)
        with pool.Fori(0, (PACKS - mixer_packs) // 4) as i:
            for n in range(4):
                split_low(mixer_packs + AHEAD + n, i)

    @block.tensor
    def _(pe):
        def wait_bank(phase, i, step, j):
            n = OUT_BASE[phase] + j - 3
            if i is not None or n > 0:
                pe.wait_ge(outs_done, value(i, step, n))

        def pack(phase, i, per_body, j, target, rhs, chunk0=0, chunks=8, total=8, ready=None):
            hi, lo = rhs
            m = PACK_BASE[phase] + j
            pe.wait_ge(low_split, value(i, per_body, m + 1))
            for b in range(chunks):
                k = chunk0 + b
                if ready is not None:
                    pe.wait_ge(ready[0], ready[1] + k + 1)
                wh = whi[:, j % 4, b * P:(b + 1) * P]
                wl = wlo[:, j % 4, b * P:(b + 1) * P]
                pe.matmul(target, wh, hi[:, k, :], start=(k == 0), stop=False)
                pe.matmul(target, wh, lo[:, k, :], start=False, stop=False)
                mm = pe.matmul(target, wl, hi[:, k, :], start=False, stop=(k == total - 1))
            mm.then_inc(packs_used, 1)

        def stats(s):
            pe.wait_ge(squares_summed, 8 * (s + 1))
            if s:
                pe.wait_ge(root_ready, s)
            if s == 3:
                pe.wait_ge(both_sums, 1)
                pe.matmul(ps[:, 6, :], ones[:, :], sumsq[:, :], start=True, stop=True).then_inc(final_sums, 1)
            source = gained_sq if s == 3 else sumsq
            pe.matmul(ps[:, STAT, :], ones[:, :], source[:, :], start=True, stop=True).then_inc(stats_ready, 1)

        def project(phase, outputs, rhs, ready, s=None, n=T):
            for j in range(4):
                wait_bank(phase, None, 4, j)
                pack(phase, None, 4, j, ps[:, j, 0:n], rhs, ready=ready if j == 0 else None)
                if j == 0 and s is not None:
                    stats(s)
            if outputs > 4:
                with pe.Fori(1, outputs // 4) as i:
                    for j in range(4):
                        wait_bank(phase, i, 4, j)
                        pack(phase, i, 4, j, ps[:, j, 0:n], rhs)

        def project_out(phase, rhs, ready, packs_each=1, total=8):
            with pe.Fori(0, 2) as i:
                for j in range(4):
                    wait_bank(phase, i, 4, j)
                    for c in range(packs_each):
                        pack(phase, i, 4 * packs_each, packs_each * j + c, ps[:, j, :], rhs, chunk0=8 * c,
                             chunks=min(8, total - 8 * c), total=total, ready=ready if j == 0 else None)

        def attend(A_, scores, turn_blocks, product, extra=None):
            for s in A_.steps(3):
                if s < A_.units:
                    scores(s)
                for u in A_.turned_at(s):
                    pe.wait_ge(*((A_.probs_scaled, u - 15) if A_ is att1 and u >= 16 else (A_.probs_ready, u + 1)))
                    if u >= 2:
                        pe.wait_ge(A_.turned_stored, u - 1)
                    source, blocks = turn_blocks(u)
                    for b in range(blocks):
                        mm = pe.transpose(ps[:, 4 + u % 2, b * P:(b + 1) * P], source[:, b * P:(b + 1) * P], ident[:, :])
                    mm.then_inc(A_.turned, 1)
                if extra:
                    extra(s)
                for hd in A_.heads_at(s, 2):
                    product(hd)

        pe.wait_ge(consts_arrived, 32)
        pe.wait_ge(mixer_consts, 16 * 5)
        pe.wait_ge(dve_order, 1)
        project("mixer", 28, LIN, (chunk_ready, 0), s=0)
        for j in range(28, 30):
            wait_bank("mixer", None, 4, j)
            pack("mixer", None, 4, j, ps[:, j % 4, :], LIN)
        for j in range(30, 32):
            pe.wait_ge(low_split, j + 1)
            pe.wait_ge(packs_used, j)
            pe.sem_inc(packs_used, 1)
        pe.wait_ge(outs_done, 32)
        pe.matmul(ps[0:12, 2, :], relb[:, :], onehot[:, 0:512], start=True, stop=True)
        pe.matmul(ps[0:12, 3, 0:WIDTH - 512], relb[:, :], onehot[:, 512:WIDTH], start=True, stop=True).then_inc(bias_ready, 1)
        for v in range(8):
            if v >= 2:
                pe.wait_ge(v_stored, v - 1)
            for t in range(QT):
                mm = pe.transpose(ps[:, v % 2, t * P:(t + 1) * P], proj[:, AV + v, t * P:(t + 1) * P], ident[:, :])
            mm.then_inc(v_turned, 1)
        for t in range(QT):
            mm = pe.transpose(ps[:, 6, t * 8:(t + 1) * 8], proj[0:8, IW, t * P:(t + 1) * P], ident[0:8, 0:8])
        mm.then_inc(iw_turned, 1)
        n = 0
        for qt in range(1, QT):
            for h in range(8):
                r = 64 * (h % 2)
                if n >= 2:
                    pe.wait_ge(idx_relu, n - 1)
                pe.matmul(ps[:, 4 + n % 2, 0:(qt + 1) * P], proj[r:r + 64, IQ + h // 2, qt * P:(qt + 1) * P],
                          proj[r:r + 64, IK, 0:(qt + 1) * P], start=True, stop=True).then_inc(idx_logits, 1)
                n += 1

        def mixer_scores(u):
            hd, qt = u // 4, u % 4
            nk = (qt + 1) * P
            if u == 0:
                pe.wait_ge(v_stored, 8)
                pe.wait_ge(biasrow_ready, 1)
                pe.wait_ge(idx_added, 24)
            if att1.bank_before(u):
                pe.wait_ge(att1.max_ready, att1.bank_before(u))
            if hd < 4:
                maps = [(AQ + hd, AK + hd, 0), (AQ + hd, AK + hd, 64)]
            else:
                h = hd % 4
                q0, k0 = (BQ, BK) if hd < 8 else (CQ, CK)
                maps = [(q0 + h // 2, k0 + h // 2, 64 * (h % 2))]
            for m, (q, k, r) in enumerate(maps):
                mm = pe.matmul(ps[:, att1.banks(u)[m], 0:nk], proj[r:r + 64, q, qt * P:(qt + 1) * P],
                               proj[r:r + 64, k, 0:nk], start=True, stop=True)
            mm.then_inc(att1.scores_ready, 1)

        def mixer_product(hd):
            pe.wait_ge(att1.turned_stored, 4 * (hd + 1))
            if hd:
                pe.wait_ge(att1.head_stored, hd)
            for j in range(QT):
                if hd < 4:
                    v, target = proj[:, AV + hd, j * P:(j + 1) * P], ps[:, 6, j * P:T]
                else:
                    h = hd % 4
                    tile = (BV if hd < 8 else CV) + h // 2
                    r = 64 * (h % 2)
                    v, target = proj[:, tile, j * P + r:j * P + r + 64], ps[r:r + 64, 6, j * P:T]
                mm = pe.matmul(target, v, probs_t[:, hd % 2, j, j * P:T], start=(j == 0), stop=(j == QT - 1))
            mm.then_inc(att1.head_done, 1)

        def mixer_extra(s):
            h = s - DIFF_SUMS
            if 0 <= h < HEADS:
                pe.wait_ge(diff_squares, h + 1)
                if h:
                    pe.wait_ge(diff_sums_read, h)
                pe.matmul(ps[:, STAT, :], ones[:, :], diff_sq[:, h, :], start=True, stop=True).then_inc(diff_sums, 1)

        attend(att1, mixer_scores, lambda u: (probs[att1.slots(u)[0]], u % 4 + 1), mixer_product, extra=mixer_extra)
        pe.wait_ge(att1.head_stored, 12)
        pe.wait_ge(diff_done, HEADS)
        project_out("mixer_out", (o_hi, o_lo), None)

        pe.wait_ge(mem_squares, 1)
        pe.wait_ge(root_ready, 1)
        for k in range(DC):
            mm = pe.matmul(ps[:, STAT, 0:M], ones[:, :], mem_sq[:, k, :], start=(k == 0), stop=(k == DC - 1))
        mm.then_inc(mem_sums, 1)
        pe.wait_ge(mem_ready, 1)
        project("memory_kv", 16, (mem_hi, mem_lo), None, n=M)
        pe.wait_ge(mem_rooted, 1)
        project("memory_q", 8, LIN, (chunk_ready, 8), s=1)
        for g in range(4):
            if g >= 2:
                pe.wait_ge(memv_stored, g - 1)
            for c in range(2):
                for t in range(2):
                    mm = pe.transpose(ps[:, 4 + g % 2, t * M + c * P:t * M + (c + 1) * P],
                                      memv_f[:, 2 * g + c, t * P:(t + 1) * P], ident[:, :])
            mm.then_inc(memv_turned, 1)
        pe.wait_ge(outs_done, OUT_BASE["memory_out"])
        pe.wait_ge(memv_stored, 4)

        def memory_scores(u):
            h, qt = u // 4, u % 4
            if att2.bank_before(u):
                pe.wait_ge(att2.exp_ready, att2.bank_before(u))
            for c in range(2):
                mm = pe.matmul(ps[:, att2.banks(u)[0], 0:M], mem_q[:, 2 * h + c, qt * P:(qt + 1) * P], mem_k[:, 2 * h + c, :],
                               start=(c == 0), stop=(c == 1))
            mm.then_inc(att2.scores_ready, 1)

        def memory_product(h):
            pe.wait_ge(att2.turned_stored, 4 * (h + 1))
            for c in range(2):
                if h:
                    pe.wait_ge(out_ready, 2 * h - 1 + c)
                for j in range(2):
                    mm = pe.matmul(ps[:, 2 + c, :], mem_v[:, j, (2 * h + c) * P:(2 * h + c + 1) * P],
                                   mprobs_t[:, h % 2, j, :], start=(j == 0), stop=(j == 1))
                mm.then_inc(att2.head_done, 1)

        attend(att2, memory_scores, lambda u: (mprobs[:, u % 4, :], 2), memory_product)
        project_out("memory_out", (o2_hi, o2_lo), (out_ready, 0))

        def filter_layer(l):
            if l == 0:
                pe.wait_ge(mlp_arrived, 16 * 4)
            else:
                pe.wait_ge(hy_act, l)
            w = fw[0:33, 0, :] if l == 0 else fw[:, l, :]
            rhs = zpos[:, :] if l == 0 else hid[:, :]
            pe.matmul(ps[0:64, 4 + l % 2, :], w, rhs, start=True, stop=True).then_inc(hy_pe, 1)

        def feed_forward(name, s, hidden_base, layer=None):
            project(name + "_up", 2 * FC, LIN, (chunk_ready, 8 * s), s=s)
            if layer is not None:
                filter_layer(layer)
            project_out(name + "_down", (act_hi, act_lo), (hidden_low, hidden_base), packs_each=3, total=FC)

        feed_forward("conv", 2, 0, layer=0)
        filter_layer(1)
        feed_forward("ffn0", 3, FC, layer=2)

        pe.wait_ge(wout_arrived, 32)
        pe.wait_ge(hy_act, 3)

        def filters(t):
            for c in range(4):
                if t:
                    pe.wait_ge(hy_dve, 3 + FILT_STEPS * (t - 1) + c + 1)
                pe.matmul(ps[:, c, :], hid[:, t * P:(t + 1) * P], hy_wout[:, c * T:(c + 1) * T],
                          start=True, stop=True).then_inc(hy_pe, 1)

        filters(0)
        for t in range(QT):
            if t + 1 < QT:
                filters(t + 1)
            for c in range(4):
                pe.wait_ge(hy_act, filter_squared(t, c))
                mm = pe.matmul(ps[:, 4 + c // 2, :], ones[:, :], filt_sq[:, c * T:(c + 1) * T],
                               start=(t == 0 and c % 2 == 0), stop=(t == QT - 1 and c % 2 == 1),
                               skip_group_check=True)
            mm.then_inc(hy_pe, 1)
        pe.wait_ge(hy_arrived, 16 * HY_LOADS)
        n = 0
        pe.wait_ge(hy_dve, 3 + FILT_STEPS * QT)
        for ft in range(QT):
            for part, (tab, src) in enumerate([(dcos, fsum), (dsin, fdiff)]):
                for o in range(2):
                    if n >= 4:
                        pe.wait_ge(hy_dve, SPEC_DVE + n - 3)
                    for t in range(QT):
                        mm = pe.matmul(ps[:, n % 4, :], tab[:, t, ft * P:(ft + 1) * P], src[:, t, o, :],
                                       start=(t == 0), stop=(t == QT - 1))
                    mm.then_inc(hy_pe, 1)
                    n += 1
        for o in range(2):
            pe.wait_ge(hy_dve, SPEC_DVE + n - 3)
            for t in range(QT):
                mm = pe.matmul(ps[0:1, n % 4, :], col("nyquist", t), fsum[:, t, o, :], start=(t == 0), stop=(t == QT - 1))
            mm.then_inc(hy_pe, 1)
            n += 1
        pe.wait_ge(hy_dve, SPEC_DVE + n)
        project("pool_hyena", 16, LIN, (chunk_ready, 32), s=4)
        n = 0
        for src in (gate0_f, z_f):
            for c in range(4):
                if n == 0:
                    pe.wait_ge(hy_dve, PARTS_DVE)
                if n >= 2:
                    pe.wait_ge(hy_act, FILT_ACT + n - 1)
                for t in range(QT):
                    mm = pe.transpose(ps[:, 4 + n % 2, t * P:(t + 1) * P], src[:, c, t * P:(t + 1) * P], ident[:, :])
                mm.then_inc(hy_pe, 1)
                n += 1
        for o in range(2):
            base = CONV_DVE + o * CONV_STEPS
            pe.wait_ge(hy_act, FILT_ACT + 8)
            pe.wait_ge(hy_dve, base)
            for ft in range(QT):
                if ft >= 2:
                    pe.wait_ge(hy_dve, base + ft - 1)
                for part, tab in enumerate((dcos, dsin)):
                    for t in range(QT):
                        mm = pe.matmul(ps[:, 2 * (ft % 2) + part, :], tab[:, t, ft * P:(ft + 1) * P], z_t[:, t, :],
                                       start=(t == 0), stop=(t == QT - 1))
                mm.then_inc(hy_pe, 1)
            for t in range(QT):
                mm = pe.matmul(ps[0:1, 6, :], col("nyquist", t), z_t[:, t, :], start=(t == 0), stop=(t == QT - 1))
            mm.then_inc(hy_pe, 1)
            pe.wait_ge(hy_dve, base + QT + 1)
            for t in range(QT):
                if t >= 2:
                    pe.wait_ge(hy_dve, base + QT + 1 + t - 1)
                cut = slice(t * P, (t + 1) * P)
                for ft in range(QT):
                    for part, (tab, y) in enumerate(((dcos, y_r), (dsin, y_s))):
                        if o == 0:
                            pe.matmul(ps[:, 4 + t % 2, :], tab[:, ft, cut], y[:, ft, :], start=(ft == 0 and part == 0), stop=False)
                        else:
                            pe.matmul(ps[:, 4 + t % 2, :], y[:, ft, cut], tab[:, ft, :], start=(ft == 0 and part == 0), stop=False)
                if o == 0:
                    mm = pe.matmul(ps[:, 4 + t % 2, :], nyrow[0:1, cut], y_n[0:1, :], start=False, stop=True)
                else:
                    mm = pe.matmul(ps[:, 4 + t % 2, :], y_n[0:1, cut], nyrow[0:1, :], start=False, stop=True)
                mm.then_inc(hy_pe, 1)
        for g in range(4):
            pe.matmul(ps[:, g, :], poolw[:, g, :], pooled[:, g, :], start=True, stop=True).then_inc(hy_pe, 1)
        pe.wait_ge(out_ready, 16)
        project_out("pool_hyena_out", (o4_hi, o4_lo), None)
        feed_forward("ffn1", 5, 2 * FC)
        feed_forward("ffn2", 6, 3 * FC)

        project("mla_down", 4, LIN, (chunk_ready, 56), s=7)
        pe.wait_ge(lat_squares, 1)
        for k in range(2):
            mm = pe.matmul(ps[:, 4, :], ones[:, :], scratch[:, k, :], start=(k == 0), stop=(k == 1))
        mm.then_inc(lat_sums, 1)
        pe.matmul(ps[:, 5, :], ones[:, :], scratch[:, 2, :], start=True, stop=True).then_inc(lat_sums, 1)
        pe.wait_ge(lat_ready, 3)
        pe.wait_ge(rope_ready, 1)
        pe.wait_ge(outs_done, OUT_BASE["mla_out"])

        def up_project(pr, job):
            slot, n = pr % 4, 4 * pr + job
            if job == 0:
                pe.wait_ge(low_split, PACK_BASE["mla_heads"] + pr + 1)
            if n >= 2:
                pe.wait_ge(up_stored, n - 1)
            if job >= 2:
                pe.wait_ge(up_roped, 2 * pr + job - 1)
            if job < 3:
                blocks, chunks = [([0, 1], [0, 1]), ([2, 3], [0, 1]), ([4], [2])][job]
                for b, k in zip(blocks, chunks):
                    wh, wl = whi[:, slot, b * P:(b + 1) * P], wlo[:, slot, b * P:(b + 1) * P]
                    first, last = b == blocks[0], b == blocks[-1]
                    pe.matmul(ps[:, 2 + n % 2, :], wh, cq_hi[:, k, :], start=first, stop=False)
                    pe.matmul(ps[:, 2 + n % 2, :], wh, cq_lo[:, k, :], start=False, stop=False)
                    mm = pe.matmul(ps[:, 2 + n % 2, :], wl, cq_hi[:, k, :], start=False, stop=last)
                mm.then_inc(up_ready, 1)
                return
            wh, wl = whi[:, slot, 5 * P:6 * P], wlo[:, slot, 5 * P:6 * P]
            for t in range(QT):
                cut = slice(t * P, (t + 1) * P)
                target = ps[:, 2 + n % 2, cut]
                pe.matmul(target, cq_hi[:, 2, cut], wh, start=True, stop=False)
                pe.matmul(target, cq_lo[:, 2, cut], wh, start=False, stop=False)
                mm = pe.matmul(target, cq_hi[:, 2, cut], wl, start=False, stop=True)
            mm.then_inc(up_ready, 1)

        def pack_over(pr):
            pe.wait_ge(up_ready, 4 * pr + 4)
            pe.sem_inc(packs_used, 1)

        def latent_scores(u):
            hd, qt = u // 4, u % 4
            if u % 8 == 0:
                pe.wait_ge(up_stored, 4 * (u // 8) + 4)
                pe.wait_ge(up_roped, 2 * (u // 8) + 2)
            if att3.bank_before(u):
                pe.wait_ge(att3.exp_ready, att3.bank_before(u))
            pe.matmul(ps[:, att3.banks(u)[0], :], head_q[0:96, hd % 4, qt * P:(qt + 1) * P], head_k[0:96, hd % 4, :],
                      start=True, stop=True).then_inc(att3.scores_ready, 1)

        def latent_extra(s):
            if 1 <= s % 8 <= 4 and s // 8 < 7:
                up_project(s // 8 + 1, s % 8 - 1)
            if s % 8 == 5 and s // 8 < 7:
                pack_over(s // 8 + 1)

        def latent_product(hd):
            pe.wait_ge(att3.turned_stored, 4 * (hd + 1))
            if hd:
                pe.wait_ge(att3.head_stored, hd)
            r = 64 * (hd % 2)
            for j in range(QT):
                mm = pe.matmul(ps[r:r + 64, 6, :], pair_v[:, (hd // 2) % 2, j, r:r + 64],
                               lprobs_t[:, hd % 2, j, :], start=(j == 0), stop=(j == QT - 1))
            mm.then_inc(att3.head_done, 1)

        for job in range(4):
            up_project(0, job)
        pack_over(0)
        attend(att3, latent_scores, lambda u: (lprobs[:, u % 4, :], 4), latent_product,
               extra=latent_extra)
        pe.wait_ge(att3.head_stored, MLA_HEADS)
        project_out("mla_out", (o5_hi, o5_lo), None)
        feed_forward("ffn3", 8, 4 * FC)
        stats(9)

    @block.scalar
    def _(act):
        order = Order(act, act_order)

        def split_high(n, i=None, per=4):
            act.wait_ge(raw_arrived[n % 2], value(i, 8 * per, 16 * (n // 2 + 1)))
            if i is not None or n >= 4:
                act.wait_ge(packs_used, value(i, per, n - 3))
            act.activation(whi[:, n % 4, :], raw[:, n % 2, :], ACT.Copy).then_inc(high_split, 1)

        def split_only(phase, packs):
            base = PACK_BASE[phase] + AHEAD
            with act.Fori(0, packs // 4) as i:
                for j in range(4):
                    split_high(base + j, i)

        def chunk(s, d, i, ready):
            c = 8 * s + d
            row = bass.ds(value(i, 4, d), 1)
            act.wait_ge(ready[0], value(i, 4, ready[1] + d + 1))
            if i is not None or c >= 2:
                act.wait_ge(squares_summed, value(i, 4, c - 1))
            act.activation(squares[:, d % 2, :], x[:, row, :].rearrange("p a t -> p (a t)"), ACT.Square).then_inc(squares_ready, 1)
            if s == 3:
                act.activation(gained_squares[:, d % 2, :], x[:, row, :].rearrange("p a t -> p (a t)"), ACT.Square,
                               scale=cols[:, bass.ds(value(i, 4, COLS["norm_final"] + d), 1)]).then_inc(gained_squared, 1)
            act.wait_ge(gain_applied, value(i, 4, c + 1))
            act.activation(lin_hi[:, row, :].rearrange("p a t -> p (a t)"), gained[:, d % 2, :], ACT.Copy).then_inc(chunk_high, 1)

        def root(s):
            act.wait_ge(stats_ready, s + 1)
            act.activation(rstd[:, :], ps[:, STAT, :], ACT.Sqrt, scale=1.0 / D,
                           bias=eps2_c if s == 3 else eps_c).then_inc(root_ready, 1)
            if s == 3:
                act.wait_ge(final_sums, 1)
                act.activation(scratch[:, 0, :], ps[:, 6, :], ACT.Sqrt, scale=1.0 / D, bias=eps_c).then_inc(final_rooted, 1)

        def project(phase, packs, s):
            base = PACK_BASE[phase] + AHEAD
            split_high(base)
            root(s)
            for j in range(1, 4):
                split_high(base + j)
            if packs > 4:
                with act.Fori(1, packs // 4) as i:
                    for j in range(4):
                        split_high(base + j, i)

        def residual(phase, s, packs_each=1):
            base = PACK_BASE[phase] + AHEAD
            with act.Fori(0, 2) as i:
                for j in range(4):
                    for c in range(packs_each):
                        split_high(base + packs_each * j + c, i, 4 * packs_each)
                    chunk(s, j, i, (outs_done, OUT_BASE[phase]))

        def filter_layer(l):
            act.wait_ge(hy_dve, l + 1)
            act.activation(hid[:, :], hid[:, :], ACT.Sin).then_inc(hy_act, 1)

        def feed_forward(n, name, s, conv=False, layer=None):
            base, outs = PACK_BASE[name + "_up"] + AHEAD, OUT_BASE[name + "_up"]

            def up_step(i, g, first=False):
                split_high(base + 2 * g, i)
                if first:
                    root(s)
                split_high(base + 2 * g + 1, i)
                f = value(i, 2, g)
                if conv:
                    for side in range(2):
                        act.wait_ge(outs_done, value(i, 4, outs + 2 * g + 1 + side))
                        if i is not None or g >= 2:
                            act.wait_ge(hidden_low, value(i, 2, n * FC + g - 1))
                        tile = value(i, 2, g + side * FC)
                        act.activation(conved[:, 2 * g + side, :], padded[:, side, 2:2 + T], ACT.Identity,
                                       scale=cols[:, bass.ds(tile + (COLS["conv_w"] + 2 * 2 * FC), 1)],
                                       bias=cols[:, bass.ds(tile + COLS["conv_b"], 1)]).then_inc(conv_begun, 1)
                    act.wait_ge(conv_gate, value(i, 2, g + 1))
                    g_buf, h_buf = conved[:, 2 * g, :], conved[:, 2 * g + 1, :]
                else:
                    act.wait_ge(outs_done, value(i, 4, outs + 2 * g + 1))
                    g_buf, h_buf = gate[:, g, :], hidden[:, g, :]
                act.activation(g_buf, g_buf, ACT.Silu).then_inc(gate_ready, 1)
                act.wait_ge(hidden_ready, value(i, 2, n * FC + g + 1))
                act.activation(act_hi[:, bass.ds(f, 1), :].rearrange("p a t -> p (a t)"), h_buf, ACT.Copy).then_inc(hidden_high, 1)

            up_step(None, 0, first=True)
            up_step(None, 1)
            with act.Fori(1, FC // 2) as i:
                up_step(i, 0)
                up_step(i, 1)
            if layer is not None:
                filter_layer(layer)
            residual(name + "_down", s + 1, packs_each=3)

        act.dma_start(cols[:, 0:N_COLS], A["cols"]).then_inc(consts_arrived, 16)
        act.dma_start(ident[:, :], A["ident"]).then_inc(consts_arrived, 16)
        act.dma_start(onehot[:, :], A["onehot"]).then_inc(mixer_consts, 16)
        act.dma_start(relb[:, :], A["rel_bias"]).then_inc(mixer_consts, 16)
        act.dma_start(maskrow[:, :], A["maskrow"]).then_inc(mixer_consts, 16)
        act.dma_start(diagmask[:, :], A["diagmask"]).then_inc(mixer_consts, 16)
        act.dma_start(lamrows[:, :, :], A["lam"].rearrange("(o a) b -> o a b", o=1).broadcast_to([P, 4, 64])).then_inc(mixer_consts, 16)
        for d in range(DC):
            chunk(0, d, None, (x_arrived[d // 2], 15 - d))
            if d in (1, 5, 7):
                split_high((d - 1) // 2 - d // 5)
        project("mixer", 32, 0)

        act.wait_ge(lam_dot, 2)
        act.activation(lamexp, lamsum, ACT.Exp).then_inc(lam_exp, 1)
        for v in range(8):
            act.wait_ge(v_turned, v + 1)
            act.activation(proj[:, AV + v, :], ps[:, v % 2, :], ACT.Copy).then_inc(v_stored, 1)
        act.wait_ge(biasrow_ready, 1)
        act.dma_start(bias_scratch, biasrow[:, :].rearrange("h (o w) -> h o w", o=1).broadcast_to([12, P, WIDTH])).then_inc(bias_stored, 16)
        n = 0
        for qt in range(1, QT):
            for h in range(8):
                act.wait_ge(idx_logits, n + 1)
                if n >= 2:
                    act.wait_ge(idx_added, n - 1)
                act.activation(relu[:, n % 2, 0:(qt + 1) * P], ps[:, 4 + n % 2, 0:(qt + 1) * P], ACT.Relu,
                               scale=0.125).then_inc(idx_relu, 1)
                n += 1
        act.wait_ge(bias_stored, 16)

        def load_table(hd):
            src = bass.AP(bias_scratch.tensor, hd * P * WIDTH + P - 1, [[WIDTH - 1, P], [1, T]])
            act.dma_start(table[:, hd % 2, :], src).then_inc(table_arrived[hd % 2], 16)

        load_table(0)
        load_table(1)

        def attend(A_, exps, store_to, outs, extra=None):
            for s in A_.steps(4):
                for u in A_.turned_at(s):
                    act.wait_ge(A_.turned, u + 1)
                    if u // 4 >= 2:
                        act.wait_ge(A_.head_done, (u // 4 - 1) * A_.per_head)
                    target, blocks = store_to(u)
                    act.activation(target, ps[:, 4 + u % 2, 0:blocks * P].rearrange("p (b q) -> p b q", q=P),
                                   ACT.Copy).then_inc(A_.turned_stored, 1)
                if s < A_.units:
                    exps(s)
                if extra:
                    extra(s)
                for hd in A_.heads_at(s, 3):
                    outs(hd)

        def mixer_exps(u):
            hd, qt = u // 4, u % 4
            nk = (qt + 1) * P
            act.wait_ge(att1.max_ready, u + 1)
            for b in att1.slots(u):
                act.activation(probs[b][:, 0:nk], probs[b][:, 0:nk], ACT.Exp, scale=-1.0, bias=negmax[:, b:b + 1],
                               accum_out=expsum[:, b:b + 1]).then_inc(att1.exp_ready, 1)
            if qt == 3 and hd + 2 < 12:
                load_table(hd + 2)

        def mixer_outs(hd):
            act.wait_ge(att1.head_done, hd + 1)
            if hd < 4:
                act.activation(diff_out[:, hd, :], ps[:, 6, :], ACT.Copy).then_inc(att1.head_stored, 1)
            else:
                r, chunk_ = 64 * (hd % 2), 4 + (hd - 4) // 2
                act.activation(o_hi[r:r + 64, chunk_, :], ps[r:r + 64, 6, :], ACT.Copy).then_inc(out_high, 1)

        def mixer_extra(s):
            h = s - DIFF_SUMS + 2
            if 0 <= h < HEADS:
                act.wait_ge(att1.head_stored, HEADS)
                act.activation(diff_sq[:, h, :], diff_out[:, h, :], ACT.Square).then_inc(diff_squares, 1)
            if s == DIFF_SCALED - 2:
                act.wait_ge(diff_sums_read, HEADS)
                order(act.activation(diff_root[:, :, :], diff_root[:, :, :], ACT.Ln))
            h = s - DIFF_SCALED + 1
            if 0 <= h < HEADS:
                act.activation(diff_root[:, h, :], diff_root[:, h, :], ACT.Exp, scale=-0.5).then_inc(diff_rooted, 1)
            h = s - DIFF_SCALED - 1
            if 0 <= h < HEADS:
                act.wait_ge(diff_scaled, h + 1)
                act.activation(o_hi[:, h, :], diff_out[:, h, :], ACT.Copy).then_inc(diff_high, 1)

        act.wait_ge(idx_added, 24)
        attend(att1, mixer_exps, lambda u: (probs_t[:, (u // 4) % 2, 0:u % 4 + 1, (u % 4) * P:(u % 4 + 1) * P], u % 4 + 1),
               mixer_outs, extra=mixer_extra)
        act.dma_start(mem[:, :, :], A["mem_t"]).then_inc(mem_arrived, 16)
        act.wait_ge(mem_arrived, 16)
        act.activation(mem_sq[:, :, :], mem[:, :, :], ACT.Square).then_inc(mem_squares, 1)
        act.wait_ge(mem_gained, DC)
        act.activation(mem_hi[:, :, :], mem[:, :, :], ACT.Copy).then_inc(mem_high, 1)
        residual("mixer_out", 1)

        act.wait_ge(mem_sums, 1)
        act.activation(rstd_mem[:, :], ps[:, STAT, 0:M], ACT.Sqrt, scale=1.0 / D, bias=eps_c).then_inc(mem_rooted, 1)
        split_only("memory_kv", 16)
        project("memory_q", 8, 1)
        for g in range(4):
            act.wait_ge(memv_turned, g + 1)
            act.activation(mem_v[:, :, 2 * g * P:2 * (g + 1) * P], ps[:, 4 + g % 2, :].rearrange("p (t c) -> p t c", t=2),
                           ACT.Copy).then_inc(memv_stored, 1)

        def plain_exps(A_, buf, n):
            def exps(u):
                bank, b = A_.banks(u)[0], u % 4
                act.wait_ge(A_.max_ready, u + 1)
                if A_.before(u):
                    act.wait_ge(A_.turned, A_.before(u))
                act.activation(buf[:, b, :], ps[:, bank, 0:n], ACT.Exp, bias=negmax[:, b:b + 1],
                               accum_out=expsum[:, b:b + 1]).then_inc(A_.exp_ready, 1)
            return exps

        def memory_outs(h):
            for c in range(2):
                act.wait_ge(att2.head_done, 2 * h + c + 1)
                act.activation(o2_hi[:, 2 * h + c, :], ps[:, 2 + c, :], ACT.Copy).then_inc(out_high, 1)

        attend(att2, plain_exps(att2, mprobs, M),
               lambda u: (mprobs_t[:, (u // 4) % 2, :, (u % 4) * P:(u % 4 + 1) * P], 2), memory_outs)
        residual("memory_out", 2)

        for buf, name in [(zpos[:, :], "zpos"), (fw[0:33, 0, :], "fw1"), (fw[:, 1, :], "fw2"), (fw[:, 2, :], "fw3")]:
            act.dma_start(buf, A[name]).then_inc(mlp_arrived, 16)
        feed_forward(0, "conv", 2, conv=True, layer=0)
        filter_layer(1)
        feed_forward(1, "ffn0", 3, layer=2)

        act.dma_start(hy_wout[:, :], A["fw_out"]).then_inc(wout_arrived, 16)
        act.dma_start(absdecay[:, :], A["decay"].broadcast_to([P, 4 * T])).then_inc(wout_arrived, 16)
        for buf, name in [(dcos[:, :, :], "dcos"), (dsin[:, :, :], "dsin"), (nyrow[:, :], "nyrow"), (poolw[:, :, :], "pool_w")]:
            act.dma_start(buf, A[name]).then_inc(hy_arrived, 16)
        act.wait_ge(wout_arrived, 32)
        act.activation(absdecay[:, :], absdecay[:, :], ACT.Abs).then_inc(hy_act, 1)
        act.wait_ge(hy_act, 4)

        def decay(t, c):
            cut = slice(c * T, (c + 1) * T)
            act.activation(decayed[:, cut], absdecay[:, cut], ACT.Exp, scale=col("neg_time", t)).then_inc(hy_act, 1)

        for c in range(4):
            decay(0, c)
        for t in range(QT):
            for c in range(4):
                act.wait_ge(hy_dve, 3 + FILT_STEPS * t + c + 1)
                if t:
                    act.wait_ge(hy_pe, 3 + 4 + 5 * t)
                cut = slice(c * T, (c + 1) * T)
                act.activation(filt_sq[:, cut], filt[:, cut], ACT.Square).then_inc(hy_act, 1)
                if t + 1 < QT:
                    decay(t + 1, c)
        act.wait_ge(hy_pe, 3 + 5 * QT)
        act.dma_start(bias_b[:, :, :], A["hy_bias"].rearrange("(o a) b -> o a b", o=1).broadcast_to([P, 2, T])).then_inc(hy_rows_arrived, 16)
        order(act.activation(inv_norm[:, :, :], ps[:, 4:6, :], ACT.Ln))
        act.activation(inv_norm[:, :, :], inv_norm[:, :, :], ACT.Exp, scale=-0.5).then_inc(hy_act, 1)
        act.wait_ge(hy_dve, SPEC_DVE + 18)
        act.dma_start(pool_count[:, :, :], A["pool_count"].rearrange("(o a) b -> o a b", o=1).broadcast_to([P, 4, T])).then_inc(hy_rows_arrived, 16)
        base, outs = PACK_BASE["pool_hyena"] + AHEAD, OUT_BASE["pool_hyena"]
        for j in range(16):
            split_high(base + j)
            if j == 0:
                root(4)
            if j >= 4:
                n = j - 4
                act.wait_ge(outs_done, outs + j + 1)
                act.activation(parts[n // 4][:, n % 4, :], window[:, n % 2, 1:1 + T], ACT.Identity,
                               scale=col("hyena_w", 12 + n), bias=col("hyena_b", n)).then_inc(conv_mid, 1)
        n = 0
        for target in (gate0_t, z_t):
            for c in range(4):
                act.wait_ge(hy_pe, 3 + 5 * QT + 18 + n + 1)
                act.activation(target[:, :, c * P:(c + 1) * P], ps[:, 4 + n % 2, :].rearrange("p (t c) -> p t c", c=P),
                               ACT.Copy).then_inc(hy_act, 1)
                n += 1
        for k in range(DC):
            kk = (k + 4) % 8
            act.wait_ge(mixed_ready, k + 1)
            act.activation(o4_hi[:, kk, :], o4[:, k % 2, :], ACT.Copy).then_inc(out_high, 1)
        residual("pool_hyena_out", 5)
        feed_forward(2, "ffn1", 5)
        feed_forward(3, "ffn2", 6)

        act.dma_start(rope[64:P, :], A["rope"]).then_inc(lat_arrived, 16)
        project("mla_down", 4, 7)
        act.wait_ge(outs_done, OUT_BASE["mla_down"] + 3)
        act.activation(scratch[:, 0:3, :], cq[:, :, :], ACT.Square).then_inc(lat_squares, 1)
        for k in range(2):
            act.wait_ge(lat_sums, k + 1)
            order(act.activation(cq_root[:, k, :], ps[:, 4 + k, :], ACT.Ln, scale=1.0 / (256, 128)[k], bias=eps_c))
        for k in range(2):
            act.activation(cq_root[:, k, :], cq_root[:, k, :], ACT.Exp, scale=-0.5).then_inc(lat_rooted, 1)
        for k in range(3):
            act.wait_ge(lat_normed, k + 1)
            act.activation(cq_hi[:, k, :], cq[:, k, :], ACT.Copy).then_inc(lat_high, 1)

        def up_store(pr, job):
            if job == 0:
                split_high(PACK_BASE["mla_heads"] + AHEAD + pr)
                if pr >= 2:
                    act.wait_ge(att3.scores_ready, 8 * (pr - 1))
            act.wait_ge(up_ready, 4 * pr + job + 1)
            bank = 2 + (4 * pr + job) % 2
            if job < 2:
                act.activation(head_q[0:64, (2 * pr + job) % 4, :], ps[0:64, bank, :], ACT.Copy).then_inc(up_stored, 1)
            elif job == 2:
                act.activation(head_k[0:64, 2 * pr % 4, :], ps[0:64, bank, :], ACT.Copy)
                act.activation(head_k[0:64, (2 * pr + 1) % 4, :], ps[64:P, bank, :], ACT.Copy).then_inc(up_stored, 1)
            else:
                if pr >= 2:
                    act.wait_ge(att3.head_done, 2 * (pr - 1))
                act.activation(pair_v[:, pr % 2, :, :], ps[:, bank, :].rearrange("p (t c) -> p t c", c=P),
                               ACT.Copy).then_inc(up_stored, 1)

        def latent_extra(s):
            if 2 <= s % 8 <= 5 and s // 8 < 7:
                up_store(s // 8 + 1, s % 8 - 2)

        def latent_outs(hd):
            r = 64 * (hd % 2)
            act.wait_ge(att3.head_done, hd + 1)
            act.activation(o5_hi[r:r + 64, hd // 2, :], ps[r:r + 64, 6, :], ACT.Copy).then_inc(out_high, 1)

        for job in range(4):
            up_store(0, job)
        attend(att3, plain_exps(att3, lprobs, T),
               lambda u: (lprobs_t[:, (u // 4) % 2, :, (u % 4) * P:(u % 4 + 1) * P], 4), latent_outs, extra=latent_extra)
        residual("mla_out", 8)
        feed_forward(4, "ffn3", 8)
        root(9)
        for d in range(DC):
            act.wait_ge(renormed, d + 1)
            act.dma_start(out[:, d, :], x[:, d, :]).then_inc(stored, 16)

    @block.vector
    def _(dve):
        order = Order(dve, dve_order)

        def chunk(s, d, i, ready):
            c = 8 * s + d
            row = bass.ds(value(i, 4, d), 1)
            dve.wait_ge(ready[0], value(i, 4, ready[1] + d + 1))
            dve.tensor_scalar(gained[:, d % 2, :], x[:, row, :].rearrange("p a t -> p (a t)"),
                              cols[:, bass.ds(value(i, 4, COLS_OF_SET[s] + d), 1)], None, ALU.mult).then_inc(gain_applied, 1)
            dve.wait_ge(chunk_high, value(i, 4, c + 1))
            dve.tensor_tensor(lin_lo[:, row, :].rearrange("p a t -> p (a t)"), gained[:, d % 2, :],
                              lin_hi[:, row, :].rearrange("p a t -> p (a t)").bitcast(F32), ALU.subtract).then_inc(chunk_ready, 1)
            dve.wait_ge(squares_ready, value(i, 4, c + 1))
            if i is not None or c >= 1:
                dve.wait_ge(squares_summed, value(i, 4, c))
            dve.tensor_tensor(sumsq[:, :], sumsq[:, :], squares[:, d % 2, :], ALU.add).then_inc(squares_summed, 1)
            if s == 3:
                dve.wait_ge(gained_squared, value(i, 4, d + 1))
                order(dve.tensor_tensor(gained_sq[:, :], gained_sq[:, :], gained_squares[:, d % 2, :], ALU.add))

        def norm(s):
            dve.wait_ge(root_ready, s + 1)
            order(dve.reciprocal(rstd[:, :], rstd[:, :]))
            if s == 3:
                dve.wait_ge(final_sums, 1)
            order(dve.memset(sumsq[:, :], 0.0))

        def residual(phase, s, packs_each=1, factor=1.0):
            base, outs = PACK_BASE[phase], OUT_BASE[phase]
            with dve.Fori(0, 2) as i:
                order.loop(i, 4 if s == 3 else 0)
                for j in range(4):
                    row = bass.ds(value(i, 4, j), 1)
                    dve.wait_ge(packs_used, value(i, 4 * packs_each, base + packs_each * (j + 1)))
                    xc = x[:, row, :].rearrange("p a t -> p (a t)")
                    dve.scalar_tensor_tensor(out=xc, in0=ps[:, j, :], scalar=factor, in1=xc, op0=ALU.mult,
                                             op1=ALU.add).then_inc(outs_done, 1)
                    chunk(s, j, i, (outs_done, outs))
            order.end(2)

        def filter_layer(l):
            a, r = ps[0:64, 4 + l % 2, :], hid[:, :]
            dve.wait_ge(hy_pe, l + 1)
            order(dve.tensor_scalar(a, a, col("filter_b", l, 64), col("filter_freq", l, 64), ALU.add, ALU.mult))
            order(dve.tensor_scalar(r, a, 1.0 / TWO_PI, ROUND, ALU.mult, ALU.add))
            order(dve.tensor_scalar(r, r, -ROUND, None, ALU.add))
            for part in TWO_PI_PARTS:
                order(dve.scalar_tensor_tensor(out=a, in0=r, scalar=-part, in1=a, op0=ALU.mult, op1=ALU.add))
            dve.tensor_scalar(r, a, SIN_MAX, -SIN_MAX, ALU.min, ALU.max).then_inc(hy_dve, 1)

        def feed_forward(n, name, s, conv=False, factor=0.5, layer=None):
            base, outs = PACK_BASE[name + "_up"], OUT_BASE[name + "_up"]
            norm(s)
            if s == 3:
                dve.wait_ge(final_rooted, 1)
                order(dve.reciprocal(scratch[:, 0, :], scratch[:, 0, :]))
                for d in range(DC):
                    ins = dve.scalar_tensor_tensor(out=x[:, d, :], in0=x[:, d, :], scalar=col("norm_final", d),
                                                   in1=scratch[:, 0, :], op0=ALU.mult, op1=ALU.mult)
                order(ins)

            def up_step(i, g):
                f = value(i, 2, g)
                for side in range(2):
                    dve.wait_ge(packs_used, value(i, 4, base + 2 * g + side + 1))
                    target = padded[:, side, 2:2 + T] if conv else (gate, up)[side][:, g, :]
                    dve.tensor_tensor(target, ps[:, 2 * g + side, :], rstd[:, :], ALU.mult).then_inc(outs_done, 1)
                done = value(i, 4, outs + 2 * g + 2)
                if conv:
                    dve.wait_ge(outs_done, done)
                    for side in range(2):
                        acc = conved[:, 2 * g + side, :]
                        tile = value(i, 2, g + side * FC)
                        dve.wait_ge(conv_begun, value(i, 4, 2 * g + side + 1))
                        order(dve.scalar_tensor_tensor(
                            out=acc, in0=padded[:, side, 1:1 + T], scalar=cols[:, bass.ds(tile + (COLS["conv_w"] + 2 * FC), 1)],
                            in1=acc, op0=ALU.mult, op1=ALU.add))
                        ins = dve.scalar_tensor_tensor(
                            out=acc, in0=padded[:, side, 0:T], scalar=cols[:, bass.ds(tile + COLS["conv_w"], 1)],
                            in1=acc, op0=ALU.mult, op1=ALU.add)
                        if side == 0:
                            ins.then_inc(conv_gate, 1)
                        else:
                            order(ins)
                    g_buf, u_buf, h_buf = conved[:, 2 * g, :], conved[:, 2 * g + 1, :], conved[:, 2 * g + 1, :]
                else:
                    dve.wait_ge(outs_done, done)
                    g_buf, u_buf, h_buf = gate[:, g, :], up[:, g, :], hidden[:, g, :]
                dve.wait_ge(gate_ready, value(i, 2, n * FC + g + 1))
                dve.tensor_tensor(h_buf, g_buf, u_buf, ALU.mult).then_inc(hidden_ready, 1)
                dve.wait_ge(hidden_high, value(i, 2, n * FC + g + 1))
                low = act_lo[:, bass.ds(f, 1), :].rearrange("p a t -> p (a t)")
                high = act_hi[:, bass.ds(f, 1), :].rearrange("p a t -> p (a t)").bitcast(F32)
                dve.tensor_tensor(low, h_buf, high, ALU.subtract).then_inc(hidden_low, 1)

            if conv:
                order(dve.memset(padded[:, :, 0:2], 0.0))
            with dve.Fori(0, FC // 2) as i:
                order.loop(i, 6 if conv else 0)
                up_step(i, 0)
                up_step(i, 1)
            order.end(FC // 2)
            if layer is not None:
                filter_layer(layer)
            if conv:
                order(dve.memset(gained_sq[:, :], 0.0))
            residual(name + "_down", s + 1, packs_each=3, factor=factor)

        order(dve.memset(ones[:, :], 1.0))
        order(dve.memset(eps_c, EPS))
        order(dve.memset(sumsq[:, :], 0.0))
        order(dve.memset(eps2_c, EPS * EPS))
        dve.wait_ge(consts_arrived, 32)
        order(dve.tensor_tensor(cols[:, N_COLS:N_COLS + DC], cols[:, COLS["norm_final"]:COLS["norm_final"] + DC],
                                cols[:, COLS["norm_g"]:COLS["norm_g"] + DC], ALU.mult))
        for d in range(DC):
            chunk(0, d, None, (x_arrived[d // 2], 15 - d))
        dve.wait_ge(mixer_consts, 16 * 5)
        for n in range(2):
            dve.tensor_tensor_reduce(out=lamprod[:, n, :], in0=lamrows[:, 2 * n, :], in1=lamrows[:, 2 * n + 1, :], scale=1.0,
                                     scalar=0.0, op0=ALU.mult, op1=ALU.add, accum_out=lamsum[:, n:n + 1]).then_inc(lam_dot, 1)
        norm(0)
        with dve.Fori(0, 7) as i:
            for j in range(4):
                dve.wait_ge(packs_used, value(i, 4, j + 1))
                dve.tensor_tensor(proj[:, bass.ds(value(i, 4, j), 1), :].rearrange("p a t -> p (a t)"), ps[:, j, :],
                                  rstd[:, :], ALU.mult).then_inc(outs_done, 1)
        for j in range(28, 30):
            dve.wait_ge(packs_used, j + 1)
            dve.tensor_tensor(proj[:, j, :], ps[:, j % 4, :], rstd[:, :], ALU.mult).then_inc(outs_done, 1 if j == 28 else 3)

        dve.wait_ge(lam_exp, 1)
        order(dve.tensor_tensor(lam_c, lamexp[:, 0:1], lamexp[:, 1:2], ALU.subtract))
        order(dve.tensor_scalar(neglam_c, lam_c, -1.0, -LAM_INIT, ALU.mult, ALU.add))
        order(dve.tensor_scalar(small[:, 3:4], col("subln"), 1.0 - LAM_INIT, None, ALU.mult))
        dve.wait_ge(bias_ready, 1)
        order(dve.scalar_tensor_tensor(out=biasrow[:, 0:512], in0=ps[0:12, 2, :], scalar=8.0, in1=maskrow[:, 0:512],
                                       op0=ALU.mult, op1=ALU.add))
        dve.scalar_tensor_tensor(out=biasrow[:, 512:WIDTH], in0=ps[0:12, 3, 0:WIDTH - 512], scalar=8.0,
                                 in1=maskrow[:, 512:WIDTH], op0=ALU.mult, op1=ALU.add).then_inc(biasrow_ready, 1)
        dve.wait_ge(iw_turned, 1)
        order(dve.tensor_scalar(idx_w, ps[:, 6, 0:32], 8 ** -0.5, None, ALU.mult))
        n = 0
        for qt in range(1, QT):
            nk = (qt + 1) * P
            for h in range(8):
                dve.wait_ge(idx_relu, n + 1)
                w = idx_w[:, qt * 8 + h:qt * 8 + h + 1]
                score = topmask[:, TOP_AT[qt]:TOP_AT[qt] + nk]
                if h == 0:
                    ins = dve.tensor_scalar(score, relu[:, n % 2, 0:nk], w, None, ALU.mult)
                else:
                    dve.wait_ge(idx_added, n)
                    ins = dve.scalar_tensor_tensor(out=score, in0=relu[:, n % 2, 0:nk], scalar=w, in1=score,
                                                   op0=ALU.mult, op1=ALU.add)
                ins.then_inc(idx_added, 1)
                n += 1
            dve.wait_ge(idx_added, n)
            order(dve.tensor_tensor(score[:, qt * P:nk], score[:, qt * P:nk], diagmask[:, :], ALU.add))

        def top_round(qt, r):
            score = topmask[:, TOP_AT[qt]:TOP_AT[qt] + (qt + 1) * P]
            order(dve.max(top8, score))
            order(dve.match_replace(out=score, in_to_replace=top8, in_values=score, imm_value=TAKEN))
            if r == 15:
                ins = dve.tensor_scalar(score, score, 2.0 * NEG, 8.0 * NEG, ALU.is_ge, ALU.mult)
                ins.then_inc(idx_selected, 1)
                dve.wait_ge(idx_selected, qt)


        def attend(A_, scoring, norming, lows, extra=None):
            for s in A_.steps(5):
                if s < A_.units:
                    scoring(s)
                if 0 <= s - 1 < A_.units:
                    norming(s - 1)
                if extra:
                    extra(s)
                for hd in A_.heads_at(s, 4):
                    lows(hd)

        def mixer_scoring(u):
            hd, qt = u // 4, u % 4
            slots, nk = att1.slots(u), (qt + 1) * P
            dve.wait_ge(table_arrived[hd % 2], 16 * (hd // 2 + 1))
            bias = table[:, hd % 2, T - nk:T]
            if hd >= 8 and qt:
                order(dve.tensor_tensor(scratch[:, 0, 0:nk], bias, topmask[:, TOP_AT[qt]:TOP_AT[qt] + nk], ALU.add))
                bias = scratch[:, 0, 0:nk]
            dve.wait_ge(att1.scores_ready, u + 1)
            if att1.before(u):
                dve.wait_ge(att1.turned, att1.before(u))
            for bank, b in zip(att1.banks(u), slots):
                ins = dve.tensor_tensor_reduce(out=probs[b][:, 0:nk], in0=ps[:, bank, 0:nk], in1=bias, scale=-0.125,
                                               scalar=3e38, op0=ALU.add, op1=ALU.min, accum_out=negmax[:, b:b + 1])
                if b == slots[-1]:
                    ins.then_inc(att1.max_ready, 1)
                    if hd >= 8 and qt:
                        dve.wait_ge(att1.max_ready, u + 1)

        def mixer_norming(u):
            slots = att1.slots(u)
            b = slots[0]
            dve.wait_ge(att1.exp_ready, att1.exps_before(u + 1))
            ins = dve.reciprocal(invsum[:, b:slots[-1] + 1], expsum[:, b:slots[-1] + 1])
            if len(slots) == 2:
                order(ins)
                ins = dve.tensor_tensor(invsum[:, b + 1:b + 2], invsum[:, b + 1:b + 2], neglam_c, ALU.mult)
            ins.then_inc(inv_ready, 1)
            if len(slots) == 2:
                dve.wait_ge(inv_ready, u + 1)
                p0, p1 = probs[b][:, 0:(u % 4 + 1) * P], probs[b + 1][:, 0:(u % 4 + 1) * P]
                order(dve.tensor_scalar(p0, p0, invsum[:, b:b + 1], None, ALU.mult))
                dve.scalar_tensor_tensor(out=p0, in0=p1, scalar=invsum[:, b + 1:b + 2], in1=p0, op0=ALU.mult,
                                         op1=ALU.add).then_inc(att1.probs_ready, 1)

        def mixer_lows(hd):
            if hd < 4:
                return
            r, chunk_ = 64 * (hd % 2), 4 + (hd - 4) // 2
            dve.wait_ge(out_high, hd - 3)
            dve.tensor_tensor(o_lo[r:r + 64, chunk_, :], ps[r:r + 64, 6, :], o_hi[r:r + 64, chunk_, :].bitcast(F32),
                              ALU.subtract).then_inc(att1.head_stored, 1)

        def mixer_extra(s):
            if s < 32:
                for n in range(3 * s // 2, 3 * (s + 1) // 2):
                    top_round(1 + n // 16, n % 16)
            h = s - DIFF_SUMS - 1
            if 0 <= h < HEADS:
                dve.wait_ge(diff_sums, h + 1)
                dve.tensor_scalar(diff_root[:, h, :], ps[:, STAT, :], 1.0 / P, EPS, ALU.mult, ALU.add).then_inc(diff_sums_read, 1)
            h = s - DIFF_SCALED
            if 0 <= h < HEADS:
                dve.wait_ge(diff_rooted, h + 1)
                dve.scalar_tensor_tensor(out=diff_out[:, h, :], in0=diff_out[:, h, :], scalar=small[:, 3:4],
                                         in1=diff_root[:, h, :], op0=ALU.mult, op1=ALU.mult).then_inc(diff_scaled, 1)
            h = s - DIFF_SCALED - 5
            if 0 <= h < HEADS:
                dve.wait_ge(diff_scaled, HEADS)
                dve.wait_ge(diff_high, h + 1)
                dve.tensor_tensor(o_lo[:, h, :], diff_out[:, h, :], o_hi[:, h, :].bitcast(F32), ALU.subtract).then_inc(diff_done, 1)

        attend(att1, mixer_scoring, mixer_norming, mixer_lows, extra=mixer_extra)
        dve.wait_ge(mem_squares, 1)
        for k in range(DC):
            dve.tensor_scalar(mem[:, k, :], mem[:, k, :], col("norm_memkv", k), None, ALU.mult).then_inc(mem_gained, 1)
        dve.wait_ge(mem_high, 1)
        dve.tensor_tensor(mem_lo[:, :, :], mem[:, :, :], mem_hi[:, :, :].bitcast(F32), ALU.subtract).then_inc(mem_ready, 1)
        residual("mixer_out", 1)

        dve.wait_ge(mem_rooted, 1)
        order(dve.reciprocal(rstd_mem[:, :], rstd_mem[:, :]))
        base = PACK_BASE["memory_kv"]
        for target, first in ((mem_k, 0), (memv_f, 8)):
            with dve.Fori(0, 2) as i:
                for j in range(4):
                    dve.wait_ge(packs_used, value(i, 4, base + first + j + 1))
                    dve.tensor_tensor(target[:, bass.ds(value(i, 4, j), 1), :].rearrange("p a t -> p (a t)"), ps[:, j, 0:M],
                                      rstd_mem[:, :], ALU.mult).then_inc(outs_done, 1)
        norm(1)
        base = PACK_BASE["memory_q"]
        with dve.Fori(0, 2) as i:
            for j in range(4):
                dve.wait_ge(packs_used, value(i, 4, base + j + 1))
                dve.scalar_tensor_tensor(out=mem_q[:, bass.ds(value(i, 4, j), 1), :].rearrange("p a t -> p (a t)"),
                                         in0=ps[:, j, :], scalar=1.0 / 16, in1=rstd[:, :], op0=ALU.mult,
                                         op1=ALU.mult).then_inc(outs_done, 1)

        def plain_scoring(A_, n):
            def scoring(u):
                bank, b = A_.banks(u)[0], u % 4
                dve.wait_ge(A_.scores_ready, u + 1)
                dve.tensor_reduce(negmax[:, b:b + 1], ps[:, bank, 0:n], AX_X, ALU.max,
                                  negate=True).then_inc(A_.max_ready, 1)
            return scoring

        def plain_norming(A_, buf):
            def norming(u):
                b = u % 4
                dve.wait_ge(A_.exp_ready, u + 1)
                order(dve.reciprocal(invsum[:, b:b + 1], expsum[:, b:b + 1]))
                p = buf[:, b, :]
                dve.tensor_scalar(p, p, invsum[:, b:b + 1], None, ALU.mult).then_inc(A_.probs_ready, 1)
            return norming

        def memory_lows(h):
            for c in range(2):
                k = 2 * h + c
                dve.wait_ge(out_high, 8 + k + 1)
                dve.tensor_tensor(o2_lo[:, k, :], ps[:, 2 + c, :], o2_hi[:, k, :].bitcast(F32), ALU.subtract).then_inc(out_ready, 1)

        attend(att2, plain_scoring(att2, M), plain_norming(att2, mprobs), memory_lows)
        residual("memory_out", 2)

        feed_forward(0, "conv", 2, conv=True, factor=1.0, layer=0)

        dve.scalar_tensor_tensor(out=gained_sq[:, :], in0=sumsq[:, :], scalar=EPS, in1=gained_sq[:, :], op0=ALU.mult,
                                 op1=ALU.add).then_inc(both_sums, 1)
        filter_layer(1)
        feed_forward(1, "ffn0", 3, layer=2)

        for t in range(QT):
            if t:
                dve.wait_ge(hy_dve, 3 + FILT_STEPS * t)
            for c in range(4):
                cut = slice(c * T, (c + 1) * T)
                dve.wait_ge(hy_pe, filter_made(t, c))
                dve.wait_ge(hy_act, filter_decay(t, c))
                if t:
                    dve.wait_ge(hy_act, filter_squared(t - 1, c))
                ins = dve.tensor_tensor(filt[:, cut], ps[:, c, :], decayed[:, cut], ALU.mult)
                if t == 0 and c % 2:
                    order(ins)
                    ins = dve.memset(filt[0:1, cut], 0.0)
                ins.then_inc(hy_dve, 1)
            dve.wait_ge(hy_dve, 3 + FILT_STEPS * t + 4)
            both = filt[:, :].rearrange("p (o d c) -> p o d c", o=2, d=2)
            order(dve.tensor_tensor(fsum[:, t, :, :], both[:, :, 0, :], both[:, :, 1, :], ALU.add))
            dve.tensor_tensor(fdiff[:, t, :, :], both[:, :, 0, :], both[:, :, 1, :], ALU.subtract).then_inc(hy_dve, 1)
        dve.wait_ge(hy_act, FILT_ACT)
        dve.wait_ge(hy_rows_arrived, 16)
        n, first = 0, 3 + 5 * QT
        for ft in range(QT):
            weight = col("dft_weight") if ft == 0 else 2.0 / (2 * T)
            for part, spec in enumerate((spec_r, spec_s)):
                for o in range(2):
                    dve.wait_ge(hy_pe, first + n + 1)
                    target = spec[:, ft, o, :]
                    if part == 0:
                        order(dve.tensor_tensor(target, ps[:, n % 4, :], inv_norm[:, o, :], ALU.mult))
                        order(dve.tensor_tensor(target, target, bias_b[:, o, :], ALU.add))
                        dve.tensor_scalar(target, target, weight, None, ALU.mult).then_inc(hy_dve, 1)
                    else:
                        dve.scalar_tensor_tensor(out=target, in0=ps[:, n % 4, :], scalar=weight, in1=inv_norm[:, o, :],
                                                 op0=ALU.mult, op1=ALU.mult).then_inc(hy_dve, 1)
                    n += 1
        for o in range(2):
            dve.wait_ge(hy_pe, first + n + 1)
            order(dve.tensor_tensor(spec_n[0:1, o, :], ps[0:1, n % 4, :], inv_norm[0:1, o, :], ALU.mult))
            order(dve.tensor_tensor(spec_n[0:1, o, :], spec_n[0:1, o, :], bias_b[0:1, o, :], ALU.add))
            dve.tensor_scalar(spec_n[0:1, o, :], spec_n[0:1, o, :], 1.0 / (2 * T), None, ALU.mult).then_inc(hy_dve, 1)
            n += 1
        norm(4)
        order(dve.memset(window[:, :, :], 0.0))
        order(dve.memset(pool_in[:, :], 0.0))
        dve.wait_ge(hy_rows_arrived, 32)
        base = PACK_BASE["pool_hyena"]
        for g in range(4):
            dve.wait_ge(packs_used, base + g + 1)
            dve.tensor_tensor(pool_in[:, 16:16 + T], ps[:, g, :], rstd[:, :], ALU.mult).then_inc(outs_done, 1)
            dve.wait_ge(outs_done, OUT_BASE["pool_hyena"] + g + 1)
            src, width = pool_in, 16 + T + 16
            for step in range(g + 1):
                width -= 1 << step
                dst = (pool_a, pool_b)[step % 2]
                order(dve.tensor_tensor(dst[:, 0:width], src[:, 0:width], src[:, (1 << step):(1 << step) + width], ALU.add))
                src = dst
            half = 1 << g
            order(dve.tensor_tensor(pooled[:, g, :], src[:, 16 - half:16 - half + T], pool_count[:, g, :], ALU.mult))
            order(dve.tensor_tensor(pooled[:, g, :], pooled[:, g, :], pool_in[:, 16:16 + T], ALU.subtract))
        for n in range(12):
            j = 4 + n
            dve.wait_ge(packs_used, base + j + 1)
            dve.tensor_tensor(window[:, n % 2, 1:1 + T], ps[:, j % 4, :], rstd[:, :], ALU.mult).then_inc(outs_done, 1)
            dve.wait_ge(outs_done, OUT_BASE["pool_hyena"] + j + 1)
            dve.wait_ge(conv_mid, n + 1)
            acc = parts[n // 4][:, n % 4, :]
            order(dve.scalar_tensor_tensor(out=acc, in0=window[:, n % 2, 0:T], scalar=col("hyena_w", n), in1=acc,
                                           op0=ALU.mult, op1=ALU.add))
            order(dve.scalar_tensor_tensor(out=acc, in0=window[:, n % 2, 2:2 + T], scalar=col("hyena_w", 24 + n), in1=acc,
                                           op0=ALU.mult, op1=ALU.add))
        dve.sem_inc(hy_dve, 1)
        first = 3 + 5 * QT + 18 + 8
        dve.wait_ge(hy_act, FILT_ACT + 8)
        for o in range(2):
            for ft in range(QT):
                dve.wait_ge(hy_pe, first + 9 * o + ft + 1)
                zr, zs = ps[:, 2 * (ft % 2), :], ps[:, 2 * (ft % 2) + 1, :]
                t = scratch
                order(dve.tensor_tensor(t[:, 0, :], zr, spec_r[:, ft, o, :], ALU.mult))
                order(dve.tensor_tensor(t[:, 1, :], zs, spec_s[:, ft, o, :], ALU.mult))
                order(dve.tensor_tensor(t[:, 2, :], zr, spec_s[:, ft, o, :], ALU.mult))
                order(dve.tensor_tensor(t[:, 3, :], zs, spec_r[:, ft, o, :], ALU.mult))
                order(dve.tensor_tensor(y_r[:, ft, :], t[:, 0, :], t[:, 1, :], ALU.subtract))
                dve.tensor_tensor(y_s[:, ft, :], t[:, 2, :], t[:, 3, :], ALU.add).then_inc(hy_dve, 1)
                dve.wait_ge(hy_dve, CONV_DVE + CONV_STEPS * o + ft + 1)
            dve.wait_ge(hy_pe, first + 9 * o + 5)
            dve.tensor_tensor(y_n[0:1, :], ps[0:1, 6, :], spec_n[0:1, o, :], ALU.mult).then_inc(hy_dve, 1)
            for t in range(QT):
                dve.wait_ge(hy_pe, first + 9 * o + 5 + t + 1)
                if o == 0:
                    dve.tensor_tensor(z_t[:, t, :], ps[:, 4 + t % 2, :], gate0_t[:, t, :], ALU.mult).then_inc(hy_dve, 1)
                else:
                    k = t
                    if k >= 2:
                        dve.wait_ge(out_ready, 8 + k - 1)
                    dve.tensor_tensor(o4[:, k % 2, :], ps[:, 4 + t % 2, :], gate1_f[:, t, :], ALU.mult).then_inc(hy_dve, 1)
                    dve.wait_ge(hy_dve, CONV_DVE + CONV_STEPS * o + 5 + t + 1)
                    dve.sem_inc(mixed_ready, 1)
                    dve.wait_ge(out_high, 16 + k + 1)
                    dve.tensor_tensor(o4_lo[:, 4 + k, :], o4[:, k % 2, :], o4_hi[:, 4 + k, :].bitcast(F32), ALU.subtract).then_inc(out_ready, 1)
        for g in range(4):
            k = 4 + g
            dve.wait_ge(out_ready, 8 + k - 1)
            dve.wait_ge(hy_pe, first + 18 + g + 1)
            dve.tensor_scalar(o4[:, k % 2, :], ps[:, g, :], col("pool_scale", g), None, ALU.mult).then_inc(mixed_ready, 1)
            dve.wait_ge(out_high, 16 + k + 1)
            dve.tensor_tensor(o4_lo[:, g, :], o4[:, k % 2, :], o4_hi[:, g, :].bitcast(F32), ALU.subtract).then_inc(out_ready, 1)
        residual("pool_hyena_out", 5)
        feed_forward(2, "ffn1", 5)
        feed_forward(3, "ffn2", 6)

        norm(7)
        base = PACK_BASE["mla_down"]
        for j in range(3):
            dve.wait_ge(packs_used, base + j + 1)
            dve.tensor_tensor(cq[:, j, :], ps[:, j, :], rstd[:, :], ALU.mult).then_inc(outs_done, 1)
        dve.wait_ge(packs_used, base + 4)
        dve.tensor_tensor(roped[64:P, :], ps[64:P, 3, :], rstd[64:P, :], ALU.mult).then_inc(outs_done, 1)
        dve.wait_ge(outs_done, OUT_BASE["mla_down"] + 4)
        dve.wait_ge(lat_arrived, 16)
        order(dve.tensor_tensor(scratch[64:96, 3, :], roped[96:128, :], rope[96:128, :], ALU.mult))
        order(dve.tensor_tensor(roped[64:96, :], roped[64:96, :], rope[64:96, :], ALU.mult))
        for b in range(4):
            ins = dve.tensor_tensor(head_k[64:96, b, :], roped[64:96, :], scratch[64:96, 3, :], ALU.add)
            if b < 3:
                order(ins)
            else:
                ins.then_inc(rope_ready, 1)
        order(dve.tensor_scalar(small[:, 64:66], cols[:, COLS["q_norm"]:COLS["q_norm"] + 2], 96.0 ** -0.5, None, ALU.mult))
        for k, gain in enumerate([small[:, 64:65], small[:, 65:66], col("kv_norm")]):
            dve.wait_ge(lat_rooted, k // 2 + 1)
            dve.scalar_tensor_tensor(out=cq[:, k, :], in0=cq[:, k, :], scalar=gain, in1=cq_root[:, k // 2, :], op0=ALU.mult,
                                     op1=ALU.mult).then_inc(lat_normed, 1)
        for k in range(3):
            dve.wait_ge(lat_high, k + 1)
            dve.tensor_tensor(cq_lo[:, k, :], cq[:, k, :], cq_hi[:, k, :].bitcast(F32), ALU.subtract).then_inc(lat_ready, 1)

        def rotation(pr, job):
            if pr >= 2:
                dve.wait_ge(att3.scores_ready, 8 * (pr - 1))
            dve.wait_ge(up_ready, 4 * pr + job + 1)
            if 2 * pr + job:
                dve.wait_ge(up_roped, 2 * pr + job)
            bank = 2 + (4 * pr + job) % 2
            q = head_q[64:96, (2 * pr + job) % 4, :]
            order(dve.tensor_tensor(roped[64:96, :], ps[96:128, bank, :], rope[96:128, :], ALU.mult))
            order(dve.tensor_tensor(q, ps[64:96, bank, :], rope[64:96, :], ALU.mult))
            dve.tensor_tensor(q, q, roped[64:96, :], ALU.add).then_inc(up_roped, 1)

        def latent_extra(s):
            if 2 <= s % 8 <= 3 and s // 8 < 7:
                rotation(s // 8 + 1, s % 8 - 2)

        def latent_lows(hd):
            r = 64 * (hd % 2)
            dve.wait_ge(out_high, 24 + hd + 1)
            dve.tensor_tensor(o5_lo[r:r + 64, hd // 2, :], ps[r:r + 64, 6, :], o5_hi[r:r + 64, hd // 2, :].bitcast(F32),
                              ALU.subtract).then_inc(att3.head_stored, 1)

        dve.wait_ge(rope_ready, 1)
        rotation(0, 0)
        rotation(0, 1)
        attend(att3, plain_scoring(att3, T), plain_norming(att3, lprobs), latent_lows, extra=latent_extra)
        residual("mla_out", 8)
        feed_forward(4, "ffn3", 8)
        norm(9)
        for d in range(DC):
            dve.scalar_tensor_tensor(out=x[:, d, :], in0=x[:, d, :], scalar=col("final_norm_g", d), in1=rstd[:, :],
                                     op0=ALU.mult, op1=ALU.mult).then_inc(renormed, 1)

    ctx.close()


def tiles(w):
    k, n = w.shape
    return w.reshape(k // P, P, n // P, P).transpose(2, 1, 0, 3).reshape(n // P, P, k)


def down_tiles(w):
    t = tiles(w)
    pad = np.zeros((t.shape[0], P, 3 * D - t.shape[2]), w.dtype)
    return np.concatenate([t, pad], 2).reshape(-1, P, 3, D).transpose(0, 2, 1, 3).reshape(-1, P, D)


def up_tiles(gate_w, up_w):
    return np.stack([tiles(gate_w), tiles(up_w)], 1).reshape(-1, P, D)


def columns(v, rows=P):
    v = v.reshape(-1, rows).T
    return np.concatenate([v, np.zeros((P - rows, v.shape[1]), v.dtype)]) if rows < P else v


def shape_constants():
    f4 = np.float32
    c = {"ident": np.eye(P, dtype=f4)}
    dist = (T - 1 - np.arange(WIDTH)).astype(np.int64)
    near = np.maximum(dist, 0)
    large = 16 + (np.log(np.maximum(near, 1).astype(f4) / f4(16)) / f4(math.log(2048 / 16)) * f4(16)).astype(np.int32)
    bucket = np.where(near < 16, near, np.minimum(large, 31))
    c["onehot"] = (np.arange(32)[:, None] == bucket[None, :]).astype(f4)
    mask = np.zeros((12, WIDTH), f4)
    mask[:, dist < 0] = 8 * NEG
    count = (near <= 128).astype(int) + (near % 4 == 0) + (near % 16 == 0)
    logs = np.where(count > 0, 8 * np.log(np.maximum(count, 1)), 8 * NEG)
    mask[4:8] = np.where(dist < 0, 8 * NEG, logs).astype(f4)
    c["maskrow"] = mask
    c["diagmask"] = np.where(np.arange(P)[None, :] > np.arange(P)[:, None], NEG, 0.0).astype(f4)
    a = np.arange(T)
    angle = 2 * np.pi * ((a[:, None] * a[None, :]) % (2 * T)) / (2 * T)
    for name, table in (("dcos", np.cos(angle)), ("dsin", np.sin(angle))):
        c[name] = np.ascontiguousarray(table.astype(f4).reshape(QT, P, T).transpose(1, 0, 2))
    sign = np.where(a % 2 == 0, 1.0, -1.0).astype(f4)
    c["nyrow"] = sign[None, :]
    t = np.linspace(0.0, 1.0, T, dtype=f4)
    phase = (f4(2.0 * math.pi) * np.arange(T, dtype=f4) / f4(T))[:, None] * np.linspace(1e-4, 15, 16, dtype=f4)[None, :]
    c["zpos"] = np.ascontiguousarray(np.concatenate([t[:, None], np.cos(phase), -np.sin(phase)], 1).T.astype(f4))
    inv = f4(10000.0) ** (-np.arange(0, 32, 2, dtype=f4) / f4(32))
    ang = (np.arange(T, dtype=f4)[:, None] * inv[None, :]).T
    c["rope"] = np.concatenate([np.cos(ang), np.cos(ang), -np.sin(ang), np.sin(ang)]).astype(f4)
    hi = [np.minimum(a - w // 2 + w, T) - np.maximum(a - w // 2, 0) for w in (2, 4, 8, 16)]
    c["pool_count"] = (1.0 / np.stack(hi)).astype(f4)
    weight = np.full((P, 1), 2.0 / (2 * T), f4)
    weight[0] = 1.0 / (2 * T)
    c["_cols"] = {"neg_time": columns(-t), "dft_weight": weight, "nyquist": columns(sign)}
    return c


def kernel(**inputs):
    import concourse.bacc as bacc
    from concourse.bass_utils import run_bass_kernel_spmd

    w = {k: np.asarray(v) for k, v in inputs.items()}
    c = shape_constants()
    const_cols = c.pop("_cols")
    f4 = np.float32

    w_in = w["w_in"][0]
    none = np.zeros((D, P), f4)
    iq_end = 1536 + 768 + 768 + 512
    ik, iw = w_in[:, iq_end:iq_end + 64], w_in[:, iq_end + 64:]
    mixer = np.concatenate([
        w_in[:, 0:1024], w_in[:, 1536:2048], w_in[:, 2304:2816], w_in[:, 3072:iq_end], ik, ik, iw, none[:, 0:120],
        w_in[:, 1024:1536], w_in[:, 2048:2304], w_in[:, 2816:3072], none, none], 1)
    packs = [tiles(mixer), tiles(w["w_out"][0]), tiles(w["w_mkv"][0]), tiles(w["w_mq"][0]), tiles(w["w_mo"][0]),
             up_tiles(w["w_up"][0][:, :FF], w["w_up"][0][:, FF:]), down_tiles(w["w_down"][0])]

    def ffn(layer, which):
        at = (layer, which)
        return [up_tiles(w["ffn_w_gate_2"][at], w["ffn_w_up_2"][at]), down_tiles(w["ffn_w_down_2"][at])]

    packs += ffn(0, 0) + [tiles(w["mix_w_in_2"][0]), tiles(w["mix_w_out_2"][0])] + ffn(0, 1) + ffn(1, 0)
    dkv = w["mla_w_dkv_2"][0]
    rot = dkv[:, 128:160]
    packs.append(tiles(np.concatenate([w["mla_w_dq_2"][0], dkv[:, 0:128], none[:, 0:64], rot, rot[:, 16:], rot[:, :16]], 1)))
    uq = w["mla_w_uq_2"][0].reshape(2, P, MLA_HEADS, 96)
    uq = np.concatenate([uq, uq[..., 80:96], uq[..., 64:80]], 3)
    ukv = w["mla_w_ukv_2"][0].reshape(P, MLA_HEADS, P)
    pairs = np.concatenate([
        uq.transpose(2, 1, 0, 3).reshape(8, 2, P, 2 * P).transpose(0, 2, 1, 3).reshape(8, P, 4 * P),
        ukv[..., 0:64].reshape(P, 8, P).transpose(1, 0, 2),
        ukv[..., 64:P].reshape(P, 8, P).transpose(1, 0, 2), np.zeros((8, P, 2 * P), f4)], 2)
    packs += [pairs, tiles(w["mla_w_o_2"][0])] + ffn(1, 1) + [np.zeros((AHEAD, P, D), f4)]
    packs = np.ascontiguousarray(np.concatenate(packs))
    assert packs.shape[0] == PACKS + AHEAD, packs.shape

    vectors = {
        "norm_mix": columns(w["norm_mix"]), "norm_mem": columns(w["norm_mem"]), "norm_memkv": columns(w["norm_memkv"]),
        "norm_ffn": columns(w["norm_ffn"]), "norm_final": columns(w["norm_final"]), "norm_g": columns(w["norm_g_2"]),
        "final_norm_g": columns(w["final_norm_g_2"]), "subln": columns(w["subln"]), "q_norm": columns(w["mla_q_norm_g_2"]),
        "kv_norm": columns(w["mla_kv_norm_g_2"]), "pool_scale": columns(w["pool_scale_2"]), "conv_w": columns(w["conv_w"]),
        "conv_b": columns(w["conv_b"]), "hyena_w": columns(w["hyena_conv_w_2"]), "hyena_b": columns(w["hyena_conv_b_2"]),
        "filter_b": columns(np.concatenate([w[f"hyena_ffn_b{n}_2"] for n in (1, 2, 3)]), 64),
        "filter_freq": columns(w["hyena_sin_freq_2"], 64), **const_cols,
    }
    arrays = {
        "packs": packs,
        "cols": np.ascontiguousarray(np.concatenate([vectors[n] for n in COLS], 1)),
        "x_t": np.ascontiguousarray(w["x"][0].T.reshape(DC, P, T).transpose(1, 0, 2)),
        "mem_t": np.ascontiguousarray(w["mem"][0].T.reshape(DC, P, M).transpose(1, 0, 2)),
        "rel_bias": w["rel_bias"],
        "lam": np.concatenate([w[n] for n in ("lam_q1", "lam_k1", "lam_q2", "lam_k2")]),
        "fw1": w["hyena_ffn_w1_2"][0], "fw2": w["hyena_ffn_w2_2"][0], "fw3": w["hyena_ffn_w3_2"][0],
        "fw_out": w["hyena_ffn_w_out_2"][0],
        "pool_w": np.ascontiguousarray(w["pool_w_2"][0].transpose(1, 0, 2)),
        "decay": w["hyena_decay_2"].reshape(1, -1),
        "hy_bias": w["hyena_bias_2"][0],
        **c,
    }
    nc = bacc.Bacc("TRN2", target_bir_lowering=False, num_devices=1)
    feeds, A = {}, {}
    for name, a in arrays.items():
        feeds[f"in_{name}"] = np.ascontiguousarray(a)
        A[name] = nc.dram_tensor(f"in_{name}", a.shape, mybir.dt.from_np(a.dtype), kind="ExternalInput").ap()
    out = nc.dram_tensor("out_t", (P, DC, T), F32, kind="ExternalOutput").ap()
    build_program(nc, A, out)
    r = run_bass_kernel_spmd(nc, [feeds], core_ids=[0])
    got = r.results[0]["out_t"]
    return np.ascontiguousarray(got.transpose(1, 0, 2).reshape(D, T).T)[None]
```
